# Optimizing a Trainium2 kernel written in Bass

```python
import math
import jax, jax.numpy as jnp
from jax import lax
import numpy as np

D_MODEL = 1024
BATCH = 1
SEQ = 256
DEPTH = 1

CHUNK = 64
N_META = 16
Q_BLOCK = 128
HEAD_DIM = 64
ROPE_DIM = HEAD_DIM // 4
ROPE_THETA = 500000.0
SB_HEADS = 8
DSA_HEADS = 8
KV_LATENT = 128
NOPE_DIM = HEAD_DIM - ROPE_DIM
IDX_HEADS = 8
IDX_DIM = 64
TOPK_MAX = 256
N_GROUPS = 4
EXP_PER_GROUP = 8
N_EXPERTS = N_GROUPS * EXP_PER_GROUP
TOP_E = 2
D_EXPERT = 512
EXPERT_BLOCK = 128
NORM_EPS = 1e-6
SB_W = SB_HEADS * HEAD_DIM
DSA_W = DSA_HEADS * HEAD_DIM
SPLITS = (SB_W, SB_W, SB_W, DSA_W, KV_LATENT, ROPE_DIM, IDX_HEADS * IDX_DIM, IDX_DIM, IDX_HEADS, D_MODEL, D_MODEL)
IN_WIDTH = 3 * SB_W + DSA_W + KV_LATENT + ROPE_DIM + IDX_HEADS * IDX_DIM + IDX_DIM + IDX_HEADS + 2 * D_MODEL


def rmsnorm(x, g):
    xf = x.astype(jnp.float32)
    y = xf * lax.rsqrt(jnp.mean(xf * xf, axis=-1, keepdims=True) + NORM_EPS)
    return (y * g.astype(jnp.float32)).astype(x.dtype)

def partial_rope(x, pos):
    half = ROPE_DIM // 2
    inv = ROPE_THETA ** (-jnp.arange(half, dtype=jnp.float32) / half)
    ang = pos.astype(jnp.float32)[:, None] * inv[None, :]
    cos = jnp.cos(ang)[None, :, None, :]
    sin = jnp.sin(ang)[None, :, None, :]
    x1 = x[..., :half].astype(jnp.float32)
    x2 = x[..., half:ROPE_DIM].astype(jnp.float32)
    rot = jnp.concatenate([x1 * cos - x2 * sin, x2 * cos + x1 * sin], axis=-1).astype(x.dtype)
    return jnp.concatenate([rot, x[..., ROPE_DIM:]], axis=-1)

def chunk_ids(pos):
    return jnp.where(pos < N_META, 0, 1 + (pos - N_META) // CHUNK)

def to_blocks(a, t_pad):
    b, t = a.shape[0], a.shape[1]
    pad = [(0, 0), (0, t_pad - t)] + [(0, 0)] * (a.ndim - 2)
    a = jnp.pad(a, pad).reshape((b, t_pad // Q_BLOCK, Q_BLOCK) + a.shape[2:])
    return jnp.moveaxis(a, 1, 0)

def from_blocks(a, t):
    a = jnp.moveaxis(a, 0, 1)
    return a.reshape((a.shape[0], a.shape[1] * a.shape[2]) + a.shape[3:])[:, :t]

def stick_breaking(q, k, v, pos):
    t = q.shape[1]
    t_pad = -(-t // Q_BLOCK) * Q_BLOCK
    scale = 1.0 / math.sqrt(HEAD_DIM)
    qpos = jnp.arange(t_pad).reshape(t_pad // Q_BLOCK, Q_BLOCK)

    def block(args):
        qb, qp = args
        z = jnp.einsum('bqhd,bkhd->bhqk', qb, k).astype(jnp.float32) * scale
        strict = pos[None, :] < qp[:, None]
        log_keep = jnp.where(strict, jax.nn.log_sigmoid(-z), 0.0)
        later = lax.cumsum(log_keep, axis=3, reverse=True) - log_keep
        a = jnp.where(strict, jnp.exp(jax.nn.log_sigmoid(z) + later), 0.0)
        return jnp.einsum('bhqk,bkhd->bqhd', a.astype(v.dtype), v)

    out = lax.map(block, (to_blocks(q, t_pad), qpos))
    return from_blocks(out, t)

def dsa_attention(q_full, kv_all, q_idx, w_idx, k_idx, pos, topk):
    t = q_full.shape[1]
    t_pad = -(-t // Q_BLOCK) * Q_BLOCK
    scale = 1.0 / math.sqrt(HEAD_DIM)
    cid = chunk_ids(pos)
    qcid = chunk_ids(jnp.arange(t_pad)).reshape(t_pad // Q_BLOCK, Q_BLOCK)

    def block(args):
        qf, qi, wi, qc = args
        s_idx = jax.nn.relu(jnp.einsum('bqhd,bkd->bqhk', qi, k_idx))
        score = jnp.einsum('bqh,bqhk->bqk', wi, s_idx).astype(jnp.float32)
        adm = cid[None, :] <= qc[:, None]
        score = jnp.where(adm[None], score, -jnp.inf)
        _, sel = lax.top_k(score, topk)
        valid = cid[sel] <= qc[None, :, None]
        kv_sel = jax.vmap(lambda kv, i: kv[i])(kv_all, sel)
        logits = jnp.einsum('bqhc,bqkc->bqhk', qf, kv_sel).astype(jnp.float32) * scale
        logits = jnp.where(valid[:, :, None, :], logits, -1e30)
        p = jax.nn.softmax(logits, axis=-1)
        return jnp.einsum('bqhk,bqkc->bqhc', p.astype(kv_sel.dtype), kv_sel[..., ROPE_DIM:])

    out = lax.map(block, (to_blocks(q_full, t_pad), to_blocks(q_idx, t_pad), to_blocks(w_idx, t_pad), qcid))
    return from_blocks(out, t)

def mixer(u, w_in, w_uk, w_uv, w_up_a, w_up_b, w_o, pos, topk):
    b, t, _ = u.shape
    proj = u @ w_in
    qa, ka, va, qb, ckv, krope, qi, ki, wi, ga, gb = jnp.split(proj, list(np.cumsum(SPLITS)[:-1]), axis=-1)
    y_a = stick_breaking(qa.reshape(b, t, SB_HEADS, HEAD_DIM), ka.reshape(b, t, SB_HEADS, HEAD_DIM),
                         va.reshape(b, t, SB_HEADS, HEAD_DIM), pos).reshape(b, t, SB_W)
    qb = partial_rope(qb.reshape(b, t, DSA_HEADS, HEAD_DIM), pos)
    q_lat = jnp.einsum('bthn,hcn->bthc', qb[..., ROPE_DIM:], w_uk)
    q_full = jnp.concatenate([qb[..., :ROPE_DIM], q_lat], axis=-1)
    krope = partial_rope(krope[:, :, None, :], pos)[:, :, 0]
    kv_all = jnp.concatenate([krope, ckv], axis=-1)
    qi = partial_rope(qi.reshape(b, t, IDX_HEADS, IDX_DIM), pos)
    ki = partial_rope(ki[:, :, None, :], pos)[:, :, 0]
    o_lat = dsa_attention(q_full, kv_all, qi, wi, ki, pos, topk)
    y_b = jnp.einsum('bthc,hcd->bthd', o_lat, w_uv).reshape(b, t, DSA_W)
    z = jax.nn.sigmoid(ga) * (y_a @ w_up_a) + jax.nn.sigmoid(gb) * (y_b @ w_up_b)
    return z @ w_o

def hier_moe(u, w_group, b_group, w_router, b_router, w1, w3, w2):
    n, d = u.shape
    g_logits = (u @ w_group).astype(jnp.float32) + b_group.astype(jnp.float32)
    g_prob = jax.nn.softmax(g_logits, axis=-1)
    p_grp, g_sel = lax.top_k(g_prob, 1)
    e_logits = ((u @ w_router).astype(jnp.float32) + b_router.astype(jnp.float32)).reshape(n, N_GROUPS, EXP_PER_GROUP)
    gidx = jnp.broadcast_to(g_sel[:, :, None], (n, 1, EXP_PER_GROUP))
    in_grp = jnp.take_along_axis(e_logits, gidx, axis=1)[:, 0]
    e_prob = jax.nn.softmax(in_grp, axis=-1)
    p_exp, e_sel = lax.top_k(e_prob, TOP_E)
    gate = p_grp * p_exp / jnp.sum(p_exp, axis=-1, keepdims=True)
    expert = g_sel * EXP_PER_GROUP + e_sel
    m = n * TOP_E
    e_flat = expert.reshape(m).astype(jnp.int32)
    tok = jnp.repeat(jnp.arange(n, dtype=jnp.int32), TOP_E)
    w_flat = gate.reshape(m)
    order = jnp.argsort(e_flat)
    e_s = e_flat[order]
    counts = jnp.zeros((N_EXPERTS,), jnp.int32).at[e_flat].add(1)
    padded = (counts + EXPERT_BLOCK - 1) // EXPERT_BLOCK * EXPERT_BLOCK
    p_end = jnp.cumsum(padded)
    p_start = p_end - padded
    start = jnp.cumsum(counts) - counts
    dest = p_start[e_s] + jnp.arange(m, dtype=jnp.int32) - start[e_s]
    n_blk = -(-m // EXPERT_BLOCK) + N_EXPERTS
    p_tot = n_blk * EXPERT_BLOCK
    buf_tok = jnp.full((p_tot,), n, jnp.int32).at[dest].set(tok[order])
    buf_w = jnp.zeros((p_tot,), jnp.float32).at[dest].set(w_flat[order])
    blk_e = jnp.minimum(jnp.searchsorted(p_end, jnp.arange(n_blk, dtype=jnp.int32) * EXPERT_BLOCK, side='right'), N_EXPERTS - 1)
    u_pad = jnp.concatenate([u, jnp.zeros((1, d), u.dtype)], axis=0)
    xb = u_pad[buf_tok].reshape(n_blk, EXPERT_BLOCK, d)

    def expert_block(args):
        xe, e = args
        hid = jax.nn.silu(xe @ w1[e]) * (xe @ w3[e])
        return hid @ w2[e]

    yb = lax.map(expert_block, (xb, blk_e)).reshape(p_tot, d)
    out = jnp.zeros((n + 1, d), u.dtype).at[buf_tok].add(yb * buf_w[:, None].astype(yb.dtype))
    return out[:n]

def first_inputs(seed: int = 0) -> dict:
    key = jax.random.key(seed)
    ks = jax.random.split(key, 20)
    f32 = jnp.float32
    nrm = lambda k, shape, s: jax.random.normal(k, shape, f32) * s
    return {
        "x": nrm(ks[0], (BATCH, SEQ, D_MODEL), 1.0),
        "meta_tokens": nrm(ks[1], (N_META, D_MODEL), 1.0),
        "norm_mix_g": 1.0 + nrm(ks[2], (DEPTH, D_MODEL), 0.02),
        "w_in": nrm(ks[3], (DEPTH, D_MODEL, IN_WIDTH), D_MODEL ** -0.5),
        "w_uk": nrm(ks[4], (DEPTH, DSA_HEADS, KV_LATENT, NOPE_DIM), KV_LATENT ** -0.5),
        "w_uv": nrm(ks[5], (DEPTH, DSA_HEADS, KV_LATENT, HEAD_DIM), KV_LATENT ** -0.5),
        "w_up_a": nrm(ks[6], (DEPTH, SB_W, D_MODEL), SB_W ** -0.5),
        "w_up_b": nrm(ks[7], (DEPTH, DSA_W, D_MODEL), DSA_W ** -0.5),
        "w_o": nrm(ks[8], (DEPTH, D_MODEL, D_MODEL), D_MODEL ** -0.5),
        "norm_ffn_g": 1.0 + nrm(ks[9], (DEPTH, D_MODEL), 0.02),
        "w_group": nrm(ks[10], (DEPTH, D_MODEL, N_GROUPS), D_MODEL ** -0.5),
        "b_group": nrm(ks[11], (DEPTH, N_GROUPS), 0.01),
        "w_router": nrm(ks[12], (DEPTH, D_MODEL, N_EXPERTS), D_MODEL ** -0.5),
        "b_router": nrm(ks[13], (DEPTH, N_EXPERTS), 0.01),
        "w1": nrm(ks[14], (DEPTH, N_EXPERTS, D_MODEL, D_EXPERT), D_MODEL ** -0.5),
        "w3": nrm(ks[15], (DEPTH, N_EXPERTS, D_MODEL, D_EXPERT), D_MODEL ** -0.5),
        "w2": nrm(ks[16], (DEPTH, N_EXPERTS, D_EXPERT, D_MODEL), D_EXPERT ** -0.5),
        "norm_final_g": 1.0 + nrm(ks[17], (D_MODEL,), 0.02),
    }

def first_block(x, meta_tokens, norm_mix_g, w_in, w_uk, w_uv, w_up_a, w_up_b, w_o, norm_ffn_g,
              w_group, b_group, w_router, b_router, w1, w3, w2, norm_final_g):
    b, s, d = x.shape
    topk = min(TOPK_MAX, s // 4)
    meta = jnp.broadcast_to(meta_tokens[None].astype(x.dtype), (b, N_META, d))
    h = jnp.concatenate([meta, x], axis=1)
    t = s + N_META
    pos = jnp.arange(t)
    for l in range(DEPTH):
        h = h + mixer(rmsnorm(h, norm_mix_g[l]), w_in[l], w_uk[l], w_uv[l], w_up_a[l], w_up_b[l], w_o[l], pos, topk)
        u = rmsnorm(h, norm_ffn_g[l]).reshape(b * t, d)
        h = h + hier_moe(u, w_group[l], b_group[l], w_router[l], b_router[l], w1[l], w3[l], w2[l]).reshape(b, t, d)
    return rmsnorm(h, norm_final_g)[:, N_META:]


DEPTH_2 = 2

PAD = Q_BLOCK - N_META
N_A_LAYERS = DEPTH_2 // 2
N_B_LAYERS = DEPTH_2 - N_A_LAYERS
RMS_EPS = 1e-6
GN_EPS = 1e-5
ROPE_THETA_2 = 10000.0
MASK_VALUE = -1e30

RET_HEADS = 4
RET_QK_DIM = D_MODEL // RET_HEADS
RET_V_DIM = 2 * D_MODEL // RET_HEADS
RET_IN = 2 * RET_HEADS * RET_QK_DIM + 2 * RET_HEADS * RET_V_DIM

MLA_HEADS = 8
MLA_NOPE = 128
MLA_ROPE = 64
MLA_V = 128
MLA_Q_RANK = 768
MLA_KV_RANK = 512

FFN_HIDDEN = ((8 * D_MODEL + 3 * 256 - 1) // (3 * 256)) * 256


def rmsnorm_2(x, g):
    xf = x.astype(jnp.float32)
    y = xf * lax.rsqrt(jnp.mean(xf * xf, axis=-1, keepdims=True) + RMS_EPS)
    return (y * g.astype(jnp.float32)).astype(x.dtype)

def rope_tables(pos, dim):
    inv = 1.0 / (ROPE_THETA_2 ** (jnp.arange(0, dim, 2, dtype=jnp.float32) / dim))
    ang = pos.astype(jnp.float32)[:, None] * inv[None, :]
    return jnp.cos(ang), jnp.sin(ang)

def apply_rope(x, cos, sin):
    xf = x.astype(jnp.float32)
    half = x.shape[-1] // 2
    x1, x2 = xf[..., :half], xf[..., half:]
    c = cos[None, :, None, :]
    s = sin[None, :, None, :]
    return jnp.concatenate([x1 * c - x2 * s, x1 * s + x2 * c], axis=-1).astype(x.dtype)

def retention_mixer(hn, w_in, gn_g, w_o, cos, sin, valid):
    B, L, _ = hn.shape
    H, DK, DV, C = RET_HEADS, RET_QK_DIM, RET_V_DIM, CHUNK
    NC = L // C
    dt = hn.dtype
    proj = hn @ w_in
    q = proj[..., :H * DK].reshape(B, L, H, DK)
    k = proj[..., H * DK:2 * H * DK].reshape(B, L, H, DK)
    v = proj[..., 2 * H * DK:2 * H * DK + H * DV].reshape(B, L, H, DV)
    gate = proj[..., 2 * H * DK + H * DV:]
    q = apply_rope(q, cos, sin)
    k = apply_rope(k, cos, sin) * (DK ** -0.5) * valid[None, :, None, None]

    def to_chunks(t):
        return t.reshape(B, NC, C, H, t.shape[-1]).transpose(1, 0, 3, 2, 4)

    log_g = jnp.log1p(-jnp.exp2(-5.0 - jnp.arange(H, dtype=jnp.float32)))
    idx = jnp.arange(C, dtype=jnp.float32)
    intra = jnp.exp(log_g[:, None, None] * jnp.abs(idx[:, None] - idx[None, :])).astype(dt)
    q_dec = jnp.exp(log_g[:, None] * (idx + 1.0)).astype(dt)
    k_dec = jnp.exp(log_g[:, None] * (C - 1.0 - idx)).astype(dt)
    chunk_dec = jnp.exp(log_g * C).astype(dt)

    def step(S, qkv):
        qc, kc, vc = qkv
        sc = jnp.einsum('bhid,bhjd->bhij', qc, kc) * intra
        o = (jnp.einsum('bhij,bhjv->bhiv', sc, vc)
             + jnp.einsum('bhid,bhdv->bhiv', qc * q_dec[:, :, None], S))
        S = S * chunk_dec[:, None, None] + jnp.einsum('bhjd,bhjv->bhdv', kc * k_dec[:, :, None], vc)
        return S, o

    S0 = jnp.zeros((B, H, DK, DV), dt)
    _, o = lax.scan(step, S0, (to_chunks(q), to_chunks(k), to_chunks(v)))
    o = o.transpose(1, 0, 3, 2, 4).reshape(B, L, H, DV)
    of = o.astype(jnp.float32)
    mu = jnp.mean(of, axis=-1, keepdims=True)
    var = jnp.mean(jnp.square(of - mu), axis=-1, keepdims=True)
    on = ((of - mu) * lax.rsqrt(var + GN_EPS)).reshape(B, L, H * DV) * gn_g.astype(jnp.float32)
    return (jax.nn.silu(gate) * on.astype(dt)) @ w_o

def mla_shared_kv(h, norm_kv_g, w_kv_a, kv_a_norm_g, w_kv_b, cos, sin):
    B, L, _ = h.shape
    kv_a = rmsnorm_2(h, norm_kv_g) @ w_kv_a
    c_kv = rmsnorm_2(kv_a[..., :MLA_KV_RANK], kv_a_norm_g)
    k_rope = apply_rope(kv_a[..., MLA_KV_RANK:][:, :, None, :], cos, sin)
    kv = (c_kv @ w_kv_b).reshape(B, L, MLA_HEADS, MLA_NOPE + MLA_V)
    k = jnp.concatenate([kv[..., :MLA_NOPE],
                         jnp.broadcast_to(k_rope, (B, L, MLA_HEADS, MLA_ROPE))], axis=-1)
    return k, kv[..., MLA_NOPE:]

def mla_mixer(hn, w_q_a, q_a_norm_g, w_q_b, w_o, k, v, cos, sin, chunk_id, valid_key):
    B, L, _ = hn.shape
    cq = rmsnorm_2(hn @ w_q_a, q_a_norm_g)
    q = (cq @ w_q_b).reshape(B, L, MLA_HEADS, MLA_NOPE + MLA_ROPE)
    q = jnp.concatenate([q[..., :MLA_NOPE], apply_rope(q[..., MLA_NOPE:], cos, sin)], axis=-1)
    q = q * ((MLA_NOPE + MLA_ROPE) ** -0.5)
    outs = []
    for qb in range(L // Q_BLOCK):
        s, e = qb * Q_BLOCK, (qb + 1) * Q_BLOCK
        sc = jnp.einsum('bqhd,bkhd->bhqk', q[:, s:e], k[:, :e]).astype(jnp.float32)
        mask = (chunk_id[None, :e] <= chunk_id[s:e, None]) & valid_key[None, :e]
        sc = jnp.where(mask[None, None], sc, MASK_VALUE)
        p = jax.nn.softmax(sc, axis=-1).astype(v.dtype)
        outs.append(jnp.einsum('bhqk,bkhd->bqhd', p, v[:, :e]))
    o = jnp.concatenate(outs, axis=1).reshape(B, L, MLA_HEADS * MLA_V)
    return o @ w_o

def swiglu(hn, w1, w3, w2):
    return (jax.nn.silu(hn @ w1) * (hn @ w3)) @ w2

def second_inputs(seed: int = 0) -> dict:
    key = jax.random.key(seed)
    ks = jax.random.split(key, 24)
    f32 = jnp.float32
    res = (2 * DEPTH_2) ** -0.5

    def w(k, shape, fan_in, scale=1.0):
        return jax.random.normal(k, shape, f32) * (fan_in ** -0.5) * scale

    def gain(k, shape):
        return 1.0 + 0.02 * jax.random.normal(k, shape, f32)

    return {
        "x": jax.random.normal(ks[0], (BATCH, SEQ, D_MODEL), f32),
        "meta": jax.random.normal(ks[1], (N_META, D_MODEL), f32),
        "norm_mix_g": gain(ks[2], (DEPTH_2, D_MODEL)),
        "norm_ffn_g": gain(ks[3], (DEPTH_2, D_MODEL)),
        "ret_w_in": w(ks[4], (N_A_LAYERS, D_MODEL, RET_IN), D_MODEL),
        "ret_gn_g": gain(ks[5], (N_A_LAYERS, RET_HEADS * RET_V_DIM)),
        "ret_w_o": w(ks[6], (N_A_LAYERS, RET_HEADS * RET_V_DIM, D_MODEL), RET_HEADS * RET_V_DIM, res),
        "mla_norm_kv_g": gain(ks[7], (D_MODEL,)),
        "mla_w_kv_a": w(ks[8], (D_MODEL, MLA_KV_RANK + MLA_ROPE), D_MODEL),
        "mla_kv_a_norm_g": gain(ks[9], (MLA_KV_RANK,)),
        "mla_w_kv_b": w(ks[10], (MLA_KV_RANK, MLA_HEADS * (MLA_NOPE + MLA_V)), MLA_KV_RANK),
        "mla_w_q_a": w(ks[11], (N_B_LAYERS, D_MODEL, MLA_Q_RANK), D_MODEL),
        "mla_q_a_norm_g": gain(ks[12], (N_B_LAYERS, MLA_Q_RANK)),
        "mla_w_q_b": w(ks[13], (N_B_LAYERS, MLA_Q_RANK, MLA_HEADS * (MLA_NOPE + MLA_ROPE)), MLA_Q_RANK),
        "mla_w_o": w(ks[14], (N_B_LAYERS, MLA_HEADS * MLA_V, D_MODEL), MLA_HEADS * MLA_V, res),
        "ffn_w1": w(ks[15], (DEPTH_2, D_MODEL, FFN_HIDDEN), D_MODEL),
        "ffn_w3": w(ks[16], (DEPTH_2, D_MODEL, FFN_HIDDEN), D_MODEL),
        "ffn_w2": w(ks[17], (DEPTH_2, FFN_HIDDEN, D_MODEL), FFN_HIDDEN, res),
        "final_g": gain(ks[18], (D_MODEL,)),
    }

def second_block(x, meta, norm_mix_g, norm_ffn_g, ret_w_in, ret_gn_g, ret_w_o,
              mla_norm_kv_g, mla_w_kv_a, mla_kv_a_norm_g, mla_w_kv_b,
              mla_w_q_a, mla_q_a_norm_g, mla_w_q_b, mla_w_o,
              ffn_w1, ffn_w3, ffn_w2, final_g):
    B, S, D = x.shape
    L = PAD + N_META + S
    h = jnp.concatenate([jnp.zeros((B, PAD, D), x.dtype),
                         jnp.broadcast_to(meta[None].astype(x.dtype), (B, N_META, D)),
                         x], axis=1)
    slot = jnp.arange(L)
    chunk_id = slot // CHUNK
    valid_key = slot >= PAD
    valid = valid_key.astype(x.dtype)
    pos = slot - PAD
    cos_r, sin_r = rope_tables(pos, RET_QK_DIM)
    cos_m, sin_m = rope_tables(pos, MLA_ROPE)

    k_sh = None
    v_sh = None
    for layer in range(DEPTH_2):
        hn = rmsnorm_2(h, norm_mix_g[layer])
        if layer < N_A_LAYERS:
            h = h + retention_mixer(hn, ret_w_in[layer], ret_gn_g[layer], ret_w_o[layer],
                                    cos_r, sin_r, valid)
        else:
            if layer == N_A_LAYERS:
                k_sh, v_sh = mla_shared_kv(h, mla_norm_kv_g, mla_w_kv_a, mla_kv_a_norm_g,
                                           mla_w_kv_b, cos_m, sin_m)
            j = layer - N_A_LAYERS
            h = h + mla_mixer(hn, mla_w_q_a[j], mla_q_a_norm_g[j], mla_w_q_b[j], mla_w_o[j],
                              k_sh, v_sh, cos_m, sin_m, chunk_id, valid_key)
        h = h + swiglu(rmsnorm_2(h, norm_ffn_g[layer]), ffn_w1[layer], ffn_w3[layer], ffn_w2[layer])
    return rmsnorm_2(h, final_g)[:, PAD + N_META:]


def setup_inputs(seed=0):
    out = dict(first_inputs(seed))
    for name, value in second_inputs(seed + 1).items():
        if name != "x":
            out[name + "_2"] = value
    return out


def reference(
    x, meta_tokens, norm_mix_g, w_in, w_uk, w_uv, w_up_a, w_up_b, w_o, norm_ffn_g, w_group,
    b_group, w_router, b_router, w1, w3, w2, norm_final_g, meta_2, norm_mix_g_2, norm_ffn_g_2,
    ret_w_in_2, ret_gn_g_2, ret_w_o_2, mla_norm_kv_g_2, mla_w_kv_a_2, mla_kv_a_norm_g_2,
    mla_w_kv_b_2, mla_w_q_a_2, mla_q_a_norm_g_2, mla_w_q_b_2, mla_w_o_2, ffn_w1_2, ffn_w3_2,
    ffn_w2_2, final_g_2,
):
    x = first_block(
        x, meta_tokens, norm_mix_g, w_in, w_uk, w_uv, w_up_a, w_up_b, w_o, norm_ffn_g, w_group,
        b_group, w_router, b_router, w1, w3, w2, norm_final_g,
    )
    return second_block(
        x, meta_2, norm_mix_g_2, norm_ffn_g_2, ret_w_in_2, ret_gn_g_2, ret_w_o_2,
        mla_norm_kv_g_2, mla_w_kv_a_2, mla_kv_a_norm_g_2, mla_w_kv_b_2, mla_w_q_a_2,
        mla_q_a_norm_g_2, mla_w_q_b_2, mla_w_o_2, ffn_w1_2, ffn_w3_2, ffn_w2_2, final_g_2,
    )


_drawn_inputs = setup_inputs


def setup_inputs(seed=0):
    import zlib

    import numpy as np

    out = dict(_drawn_inputs(seed))
    spreads = {}
    factors = {'norm_ffn_g': 2.832,
     'b_group': 8.0,
     'b_router': 6.598,
     'norm_mix_g_2': 4.588,
     'norm_ffn_g_2': 4.977,
     'ret_gn_g_2': 8.0,
     'mla_norm_kv_g_2': 8.0,
     'mla_kv_a_norm_g_2': 8.0,
     'mla_q_a_norm_g_2': 8.0,
     'final_g_2': 2.786}
    for name, (base, spread) in spreads.items():
        noise = np.random.default_rng([zlib.crc32(name.encode()), seed]).standard_normal(out[name].shape)
        drawn = base * np.exp(spread * noise) if base else spread * noise
        out[name] = __import__('jax').numpy.asarray(drawn.astype(out[name].dtype))
    for name, factor in factors.items():
        out[name] = (out[name] * factor).astype(out[name].dtype)
    return out
```

```python
from contextlib import ExitStack

import numpy as np

import concourse.bass as bass
from concourse import mybir

F32 = mybir.dt.float32
F32R = mybir.dt.float32r
I32 = mybir.dt.int32
ALU = mybir.AluOpType
ACT = mybir.ActivationFunctionType
AX = mybir.AxisListType

P = 128
D = 1024
META = 16
SEQ = 256
T = META + SEQ
CHUNK = 64
KB = D // P
HEADS = 8
HD = 64
TOPK = min(256, SEQ // 4)
LAT = 128
NG, EPG = 4, 8
NE = NG * EPG
DE = 512
TOP_E = 2
SLOTS = T * TOP_E
WIN = 96
ITEMS = NE + 8
XCOLS = SLOTS + WIN
RH = 4
RV = 512
FB = 22
EPS = 1e-6
GN_EPS = 1e-5
BIG = 1e30
KEY_TILES = [(0, 128), (128, 112), (240, 32)]
KEY_COLS = [(0, 128), (128, 128), (240, 32)]
QRY_TILES = [(0, 128), (128, 128), (256, 16)]
SB_COLS = [(0, 0, 272), (272, 128, 144), (416, 240, 32)]
SBW = 448

SLABS = ([("w_in_qa", 32), ("w_in_ka", 32), ("w_in_va", 32), ("w_in_qb", 32), ("w_in_misc", 32),
          ("w_in_qi", 32), ("w_in_ga", 32), ("w_in_ga", 32), ("w_in_gb", 32), ("w_in_gb", 32),
          ("w_up_a", 32), ("w_up_b", 32), ("w_o", 32), ("w_o", 32)]
         + [("ret_qk", 32)] * 4 + [("ret_v", 32)] * 4 + [("ret_gate", 32)] * 4 + [("ret_o", 32)] * 4
         + [("up0", 32)] * 11 + [("down0", FB)] * 8
         + [("kv_c", 32), ("kr_qa", 32), ("qa_rest", 24), ("kv_k", 32), ("kv_v", 32)]
         + [("q_b", 24)] * 3 + [("mla_o", 32)] * 2
         + [("up1", 32)] * 11 + [("down1", FB)] * 8)
FIRST_SLAB = {}
for _n, (_name, _b) in enumerate(SLABS):
    FIRST_SLAB.setdefault(_name, _n)
N_FIRST = FIRST_SLAB["ret_qk"]

UNITS = [("qa", 4, 1, "act"), ("ka", 4, 1, "act"), ("va", 3, 1, "act"), ("qb", 4, 1, "act"),
         ("misc", 4, 1, "act"), ("qi", 4, 1, "act"), ("ga", 8, 2, "act"), ("gb", 8, 2, "act"),
         ("qlat", 8, 0, "act")]
UNITS += [u for h in range(HEADS) for u in ((f"olat{h}", 1, 0, "act"), (f"yb{h}", 1, 0, "dve"))]
UNITS += [("za", 8, 1, "dve"), ("zb", 8, 1, "dve"), ("wo", 8, 2, "dve"),
          ("utok", 6, 0, "act"), ("router", 1, 0, "dve"), ("rank", 3, 0, "dve"), ("disp", 16, 0, "act"),
          ("yslot", 10, 0, "act"), ("gt", 5, 0, "dve"), ("comb", 8, 0, "dve"),
          ("rqk", 16, 4, "dve"), ("rv", 12, 4, "act"), ("gate", 16, 4, "dve"), ("ro", 16, 0, "act"),
          ("rwo", 8, 4, "dve"), ("up0", 44, 11, "dve"), ("down0", 8, 8, "dve"),
          ("kvc", 4, 1, "act"), ("krq", 4, 1, "act"), ("qar", 3, 1, "act"), ("kn", 8, 1, "act"),
          ("vm", 6, 1, "act"), ("qn", 8, 2, "act"), ("qr", 4, 1, "act")]
UNITS += [(f"om{h}", 1, 0, "dve") for h in range(HEADS)]
UNITS += [("mo", 8, 2, "dve"), ("up1", 44, 11, "dve"), ("down1", 8, 8, "dve")]
UNIT0 = {}
FREED = []
SLAB_UNITS = []
_count = {"act": 0, "dve": 0}
for _name, _n, _s, _e in UNITS:
    UNIT0[_name] = len(FREED)
    for _i in range(_n):
        _count[_e] += 1
        FREED.append((_e, _count[_e]))
    for _j in range(_s):
        SLAB_UNITS.append(UNIT0[_name] + _n * (_j + 1) // _s)
assert len(SLAB_UNITS) == len(SLABS)

GAINS = {}
_at = 0
for _name, _n in [("mix", 8), ("ffn", 8), ("final", 8), ("mix0", 8), ("ffn0", 8), ("kv", 8), ("mix1", 8),
                  ("kva", 4), ("qa", 6), ("ffn1", 8), ("final2", 8), ("gn", 16)]:
    GAINS[_name] = _at
    _at += _n
N_GAINS = _at


def program(nc, a, out):
    base0 = 16512
    top = 229368

    def place(name, shape, offset, dt=F32):
        return nc.alloc_sbuf_tensor_at(name, [P] + shape, dt, offset=offset)

    RAW = [place(f"raw{i}", [4096], base0 + 16384 * i) for i in range(3)]
    WH = [place(f"wh{i}", [4096], base0 + 49152 + 16384 * i, F32R) for i in range(2)]
    WL = [place(f"wl{i}", [4096], base0 + 81920 + 16384 * i, F32R) for i in range(2)]
    XPT = [place(f"expert_w{i}", [4096], base0 + 16384 * i) for i in range(6)]
    at = base0 + 114688
    fixed = {}
    for name, shape in [("H", [KB, T]), ("ident", [P]), ("ones", [P]), ("rot", [P]), ("cosw", [T]), ("sinw", [T]), ("gains", [N_GAINS]), ("rs", [T])]:
        fixed[name] = place(name, shape, at)
        at += -(-4 * int(np.prod(shape)) // 32) * 32
    H, ident, ones, rot, cosw, sinw, gains, rs = fixed.values()
    R0 = at

    def region(name, shape, off, dt=F32):
        assert R0 + off + 4 * int(np.prod(shape)) <= top, (name, R0 + off + 4 * int(np.prod(shape)) - top)
        return place(name, shape, R0 + off, dt)

    B = 4 * T
    UH = region("UH", [KB, T], 0, F32R)
    UL = region("UL", [KB, T], 8 * B, F32R)
    QA = region("QA", [4, T], 17408)
    KA = region("KA", [4, 368], 21760)
    VA = region("VA", [3, 512], 27904)
    QB = region("QB", [4, T], 34048)
    QI = region("QI", [4, T], 38400)
    KI = region("KI", [T], 42752)
    CKV = region("CKV", [T], 43840)
    KR = region("KR", [T], 44928)
    WIT = region("WIT", [T], 46016)
    CKVT = region("CKVT", [3, P], 47104)
    WI = region("WI", [3, 8], 48640)
    GA = region("GA", [KB, T], 48768)
    GB = region("GB", [KB, T], 57472)
    SQ = region("SQ", [KB, T], 48768)
    YAH = region("YAH", [4, T], 66176, F32R)
    YAL = region("YAL", [4, T], 70528, F32R)
    YBH = region("YBH", [4, T], 74880, F32R)
    YBL = region("YBL", [4, T], 79232, F32R)
    ROT_T = region("ROT_T", [2, T], 66176)
    SBM = region("SBM", [SBW], 76928)
    negu = region("negu", [P], 78720)
    negones = region("negones", [P], 79232)
    SB_L = [region(f"SB_L{i}", [SBW], 0 + 7168 * i) for i in range(2)]
    SB_SP = [region(f"SB_SP{i}", [SBW], 1792 + 7168 * i) for i in range(2)]
    SB_SPM = [region(f"SB_SPM{i}", [SBW], 3584 + 7168 * i) for i in range(2)]
    SB_A = [region(f"SB_A{i}", [SBW], 5376 + 7168 * i) for i in range(2)]
    QLAT = region("QLAT", [8, T], 0)
    NEG = place("NEG", [3, T], base0 + 65536)
    SCORE = place("SCORE", [3, T], base0 + 65536 + 3 * B)
    PR = [region(f"PR{i}", [T], 15232 + B * i) for i in range(2)]
    ADM = place("ADM", [3, T], base0 + 65536 + 6 * B)
    BND = place("BND", [3, T], base0 + 65536 + 9 * B)
    RL = [place(f"RL{i}", [T], base0 + 98304 + B * i) for i in range(2)]
    PT = [region(f"PT{i}", [3, T], 26112 + 3 * B * i) for i in range(2)]
    OL = region("OL", [T], 32640)
    WUK = region("WUK", [4, P], 74880)
    WUV = place("WUV", [8, HD], base0 + 98304 + 2 * B)
    SMALL = region("SMALL", [96], 83584)
    MAX8 = region("MAX8", [8], 83968)
    ZH = region("ZH", [KB, T], 0, F32R)
    ZL = region("ZL", [KB, T], 8 * B, F32R)
    ZT = region("ZT", [2, T], 17408)
    UM = region("UM", [KB, T], 0)
    G = region("G", [3, SLOTS], 8704)
    UTOK = region("UTOK", [3, D], 15232)
    PERM = region("PERM", [3, XCOLS], 27520)
    XS = region("XS", [KB, XCOLS], 35200)
    YS = region("YS", [KB, XCOLS], 55680)
    YSLOT = region("YSLOT", [5, D], 15232)
    GT = region("GT", [5, T], 36864)
    ro = 76160
    small = {}
    for name, shape in [("LG", [3, 36]), ("RB", [36]), ("DESC", [36]), ("utri", [P]),
                        ("THR", [5]), ("GM", [3]), ("GE", [3, 4]), ("OG", [3, 4]), ("GTMP", [3, 4]),
                        ("PG", [3]), ("EM", [3, 32]), ("O1", [3, 32]), ("O2", [3, 32]), ("ET", [3, 32]),
                        ("M1", [3]), ("M2", [3]), ("TM", [3]), ("G1", [3]), ("G2", [3]), ("MM", [3, 32]),
                        ("DST1", [3]), ("DST2", [3]), ("CC", [8]), ("CB", [P]), ("N5", [5]),
                        ("TA", [96]), ("TF", [96])]:
        small[name] = region(name, shape, ro)
        ro += -(-4 * int(np.prod(shape)) // 32) * 32
    small["IOTA"] = region("IOTA", [XCOLS], 55680 + 8704)
    small["WRT"] = region("WRT", [KB, 36], 55680 + 8704 + 4 * XCOLS)
    utri = small["utri"]
    TBL = region("TBL", [96], ro, I32)
    ro += 384
    XW = [region(f"XW{i}", [KB, WIN], 15232 + 32 * WIN * i) for i in range(2)]
    SG = [region(f"SG{i}", [4, WIN], 15232 + 64 * WIN + 16 * WIN * i) for i in range(2)]
    HID = [region(f"HID{i}", [4, WIN], 15232 + 96 * WIN + 16 * WIN * i) for i in range(2)]
    UMT = region("UMT", [KB, T], 55680)
    RQ = region("RQ", [8, T], 17408)
    RK = region("RK", [8, T], 26112)
    RVV = [region(f"RV{h}", [3, RV], 34816 + 6144 * h) for h in range(RH)]
    GATE = region("GATE", [16, T], 59392)
    DEC = [region(f"DEC{i}", [3, T], 76800 + 3264 * i) for i in range(2)]
    R1 = region("R1", [2, T], 76800)
    R2 = region("R2", [2, T], 78976)
    GSIG = [region(f"GSIG{i}", [T], 81152 + B * i) for i in range(2)]
    ST = [region(f"ST{i}", [3, T], 3264 * i) for i in range(2)]
    RO = region("RO", [4, T], 6528)
    RSQ = region("RSQ", [4, T], 10880)
    GRS = region("GRS", [T], 15232)
    GMU = region("GMU", [T], 16320)
    RHI = region("RHI", [16, T], 59392, F32R)
    RLO = [region(f"RLO{h}", [4, T], 34816 + 6144 * h, F32R) for h in range(RH)]
    SQ2 = region("SQ2", [KB, T], 65280)
    SQ3 = region("SQ3", [KB, T], 65280 - 5888)
    TH = region("TH", [FB, T], 17408, F32R)
    TL = region("TL", [FB, T], 41344, F32R)
    FS = [region(f"FS{i}", [T], 65280 + B * i) for i in range(2)]
    FT = [region(f"FT{i}", [T], 67456 + B * i) for i in range(2)]
    FU = [region(f"FU{i}", [T], 69632 + B * i) for i in range(2)]
    QN = region("QN", [8, T], 17408)
    KN = region("KN", [8, T], 26112)
    QR = region("QR", [4, T], 34816)
    KR2 = region("KR2", [T], 39168)
    VM = region("VM", [3, D], 40256)
    CKH = region("CKH", [4, T], 52544, F32R)
    CKL = region("CKL", [4, T], 56896, F32R)
    CQH = region("CQH", [6, T], 61248, F32R)
    CQL = region("CQL", [6, T], 67776, F32R)
    CRAW = region("CRAW", [6, T], 74304)
    CKRAW = region("CKRAW", [4, T], 61248)
    SQM = region("SQM", [KB, T], 74304)
    SQQ = region("SQQ", [KB, T], 17408)
    ROT_M = region("ROT_M", [2, T], 80832)
    OMH = region("OMH", [8, T], 0, F32R)
    OML = region("OML", [8, T], 8704, F32R)
    NEG2 = region("NEG2", [3, T], 52544)
    PR2 = [region(f"PR2{i}", [T], 55808 + B * i) for i in range(2)]
    PT2 = [region(f"PT2{i}", [3, T], 57984 + 3 * B * i) for i in range(2)]
    OUT = region("OUT", [KB, T], 17408)

    with ExitStack() as ctx:
        def sem(name):
            return ctx.enter_context(nc.semaphore(name))

        PS = ctx.enter_context(nc.psum_tensor("PS", [P, 8, 512], F32))
        raw_full = [sem(f"raw_full{i}") for i in range(3)]
        hi_done = sem("hi_done")
        lo_done = sem("lo_done")
        unit_done = sem("unit_done")
        freed = {"act": sem("freed_act"), "dve": sem("freed_dve")}
        act_step, dve_step, pool_step = sem("act_step"), sem("dve_step"), sem("pool_step")
        const_in, h_in, sb_in, dsa_in, moe_in, tab2_in, meta2_in, mla_in = (
            sem(x) for x in ("const_in", "h_in", "sb_in", "dsa_in", "moe_in", "tab2_in", "meta2_in", "mla_in"))
        dec_in = [sem("dec_in0"), sem("dec_in1")]
        sq_done, ssq_done, var_done, std_done, nrm_done, nhi_done, nlo_done = (
            sem(x) for x in ("sq_done", "ssq_done", "var_done", "std_done", "nrm_done", "nhi_done", "nlo_done"))
        rot_mm, rot_free, rot_done = sem("rot_mm"), sem("rot_free"), sem("rot_done")
        tt_mm, tt_done = sem("tt_mm"), sem("tt_done")
        sb_z, sb_l, sb_spm, sb_x, sb_e, sb_am, sb_y, sb_yd = (
            sem(x) for x in ("sb_z", "sb_l", "sb_spm", "sb_x", "sb_e", "sb_am", "sb_y", "sb_yd"))
        ix_mm, ix_relu, ix_used, ix_neg = sem("ix_mm"), sem("ix_relu"), sem("ix_used"), sem("ix_neg")
        at_l, at_m, at_b, at_e, at_p, at_t, at_ca = (
            sem(x) for x in ("at_l", "at_m", "at_b", "at_e", "at_p", "at_t", "at_ca"))
        z_done, z_hi, z_lo = sem("z_done"), sem("z_hi"), sem("z_lo")
        rt_exp, rt_gd, rt_m = sem("rt_exp"), sem("rt_gd"), sem("rt_m")
        perm_done, tbl_done, ka_zero = sem("perm_done"), sem("tbl_done"), sem("ka_zero")
        xp_full = [sem(f"xp_full{i}") for i in range(6)]
        xw_done, xh_done, xs_done, xt_done, xhid_done, xy_done, xye_done = (
            sem(x) for x in ("xw_done", "xh_done", "xs_done", "xt_done", "xhid_done", "xy_done", "xye_done"))
        moe_pe, moe_act = sem("moe_pe"), sem("moe_act")
        g_done, gsig_done = sem("g_done"), sem("gsig_done")
        rqk_done = sem("rqk_done")
        st_mm, st_done, ro_sum, gmu_done, oc_done, rsq_done, gv_mm, gvar, gstd, rn_done, rhi_done, rlo_done = (
            sem(x) for x in ("st_mm", "st_done", "ro_sum", "gmu_done", "oc_done", "rsq_done", "gv_mm",
                             "gvar", "gstd", "rn_done", "rhi_done", "rlo_done"))
        f_sig, f_hi, f_lo = (sem(x) for x in ("f_sig", "f_hi", "f_lo"))
        stored = sem("stored")
        block = ctx.enter_context(nc.Block())

        def gbank(g):
            return PS[:, g % 4, :]

        def sbank(s):
            return PS[:, 4 + s, :]

        @block.sync
        def _(sp):
            def load(dst, src, s):
                sp.dma_start(dst, src).then_inc(s, 16)

            def slab(n):
                if n >= 3:
                    sp.wait_ge(lo_done, n - 2)
                name, blocks = SLABS[n]
                load(RAW[n % 3][:, 0:blocks * P], a[name][n - FIRST_SLAB[name]], raw_full[n % 3])

            load(H[:], a["h_first"], h_in)
            load(ones[:], a["c_ones"], const_in)
            load(gains[:], a["gains"], const_in)
            slab(0)
            load(ident[:], a["c_ident"], const_in)
            load(rot[:], a["rot_dsa"], const_in)
            load(cosw[:], a["cos_dsa"], const_in)
            load(sinw[:], a["sin_dsa"], const_in)
            load(WUK[:], a["w_uk"], const_in)
            for n in (1, 2):
                slab(n)
            load(SBM[:], a["sb_mask"], sb_in)
            load(negu[:], a["c_negu"], sb_in)
            load(negones[:], a["c_negones"], sb_in)
            for n in range(3, 13):
                slab(n)
            sp.wait_ge(unit_done, SLAB_UNITS[9])
            load(ADM[:], a["adm"], dsa_in)
            load(BND[:], a["bound"], dsa_in)
            load(WUV[:], a["w_uv"], dsa_in)
            slab(13)
            sp.wait_ge(freed["dve"], FREED[UNIT0["wo"] + 7][1])
            for name in ("RB", "DESC", "utri", "THR", "IOTA", "WRT"):
                load(small[name][:], a["m_" + name], moe_in)
            load(rot[:], a["rot_mla"], tab2_in)
            load(cosw[:], a["cos_ret"], tab2_in)
            load(sinw[:], a["sin_ret"], tab2_in)
            sp.wait_ge(lo_done, N_FIRST)
            sp.wait_ge(unit_done, UNIT0["utok"])
            sp.wait_ge(tbl_done, 1)
            items = sp.value_load(TBL[0:1, 80:81], min_val=1, max_val=ITEMS // 2) * 2
            with sp.Fori(0, items, 2) as i:
                for s in range(2):
                    e = sp.value_load(TBL[0:1, bass.ds(i + (ITEMS + s), 1)], min_val=0, max_val=NE - 1)
                    sp.wait_ge(xh_done, i + (s + 1))
                    load(XPT[3 * s][:], a["w1"][e], xp_full[3 * s])
                    load(XPT[3 * s + 1][:], a["w3"][e], xp_full[3 * s + 1])
                    sp.wait_ge(xy_done, i + (s + 1))
                    load(XPT[3 * s + 2][:], a["w2"][e], xp_full[3 * s + 2])
            sp.wait_ge(moe_pe, 1)
            for n in range(N_FIRST, N_FIRST + 3):
                slab(n)
            sp.wait_ge(nrm_done, 8 * 3)
            load(H[:, :, 0:META], a["meta2"], meta2_in)
            ahead = FIRST_SLAB["ret_o"] + 2
            for n in range(N_FIRST + 3, ahead):
                slab(n)

            def decay(h):
                load(DEC[h % 2][:], a["decay"][h], dec_in[h % 2])

            sp.wait_ge(freed["dve"], FREED[UNIT0["gate"] + 15][1])
            decay(0)
            decay(1)
            for n in range(ahead, ahead + 3):
                slab(n)
            for h in range(2, RH):
                sp.wait_ge(st_done, 3 * (h - 1))
                decay(h)
            for n in range(ahead + 3, FIRST_SLAB["kv_c"]):
                slab(n)
            load(cosw[:], a["cos_mla"], mla_in)
            load(sinw[:], a["sin_mla"], mla_in)
            for n in range(FIRST_SLAB["kv_c"], FIRST_SLAB["mla_o"] + 4):
                slab(n)
            sp.wait_ge(unit_done, UNIT0["om0"])
            load(NEG2[:], a["neg"], mla_in)
            for n in range(FIRST_SLAB["mla_o"] + 4, len(SLABS)):
                slab(n)
            sp.wait_ge(nrm_done, 24 + 8 * 5 + 10 + 8)
            load(out, OUT[:, :, META:], stored)
            sp.wait_ge(stored, 16)

        @block.tensor
        def _(pe):
            def bank_free(g):
                if g >= 4:
                    eng, count = FREED[g - 4]
                    pe.wait_ge(freed[eng], count)

            def product(g, n, at_, nk, xh, xl):
                bank_free(g)
                wh, wl = WH[n % 2], WL[n % 2]
                for k in range(nk):
                    c = (at_ + k) * P
                    for j, (w, x) in enumerate(((wh, xh), (wh, xl), (wl, xh))):
                        mm = pe.matmul(gbank(g)[:, 0:T], w[:, c:c + P], x(k),
                                       start=(k == 0 and j == 0), stop=(k == nk - 1 and j == 2))
                mm.then_inc(unit_done, 1)

            def slab_ready(n):
                pe.wait_ge(lo_done, n + 1)

            def token_major(g, n, nk, width, col, xh, xl, t0):
                bank_free(g)
                for k in range(nk):
                    c = k * width + col
                    for j, (x, w) in enumerate(((xh, WH[n % 2]), (xl, WH[n % 2]), (xh, WL[n % 2]))):
                        mm = pe.matmul(gbank(g)[:, 0:512], x(k, t0), w[:, c:c + 512],
                                       start=(k == 0 and j == 0), stop=(k == nk - 1 and j == 2))
                mm.then_inc(unit_done, 1)

            norms = [0]

            def norm_sum(sq, nb, bank):
                norms[0] += 1
                pe.wait_ge(sq_done, norms[0])
                for k in range(nb):
                    mm = pe.matmul(bank[:, 0:T], ones[:], sq[:, k, :], start=(k == 0), stop=(k == nb - 1))
                mm.then_inc(ssq_done, 1)

            U = (lambda k: UH[:, k, :]), (lambda k: UL[:, k, :])
            UT = (lambda k, t: UH[:, k, t:t + P]), (lambda k, t: UL[:, k, t:t + P])
            TOK3 = (0, 128, 144)

            pe.wait_ge(const_in, 16 * 7)
            norm_sum(SQ, KB, sbank(0))
            pe.wait_ge(nlo_done, 8)
            pe.wait_ge(nhi_done, 8)
            for n, name in ((0, "qa"), (1, "ka")):
                slab_ready(n)
                for u in range(4):
                    product(UNIT0[name] + u, n, 8 * u, KB, *U)
            slab_ready(2)
            for j, t0 in enumerate(TOK3):
                token_major(UNIT0["va"] + j, 2, KB, 512, 0, *UT, t0)
            for n, name in ((3, "qb"), (4, "misc"), (5, "qi")):
                slab_ready(n)
                for u in range(4):
                    product(UNIT0[name] + u, n, 8 * u, KB, *U)
            ROT = [(QB, j) for j in range(4)] + [(KR, None), (KI, None)] + [(QI, j) for j in range(4)]
            RAWS = [UNIT0["qb"] + j for j in range(4)] + [UNIT0["misc"] + 1, UNIT0["misc"] + 2] \
                + [UNIT0["qi"] + j for j in range(4)]

            def rotate(j):
                t, b = ROT[j]
                pe.wait_ge(freed["act"], FREED[RAWS[j]][1])
                if j >= 4:
                    pe.wait_ge(rot_free, j - 3)
                pe.matmul(sbank(j % 4)[:, 0:T], rot[:], t[:, b, :] if b is not None else t[:, :],
                          start=True, stop=True).then_inc(rot_mm, 1)

            for n in range(6, 10):
                slab_ready(n)
                for u in range(4):
                    product(UNIT0["ga"] + 4 * (n - 6) + u, n, 8 * u, KB, *U)
                for j in range(3 * (n - 6), min(3 * (n - 6) + 3, 10)):
                    rotate(j)
            pe.wait_ge(rot_free, 10)
            for j, (c, m) in enumerate(KEY_COLS):
                pe.matmul(sbank(0)[0:m, j * P:(j + 1) * P], CKV[:, c:c + m], ident[:],
                          start=(j == 0), stop=True, skip_group_check=True)
            for j, (c, m) in enumerate(QRY_TILES):
                mm = pe.matmul(sbank(0)[0:m, 384 + 8 * j:392 + 8 * j], WIT[0:8, c:c + m], ident[0:8, 0:8],
                               start=False, stop=True, skip_group_check=True)
            mm.then_inc(tt_mm, 1)
            def sb_scores(h, bank, first, last):
                r = slice(HD * (h % 2), HD * (h % 2) + HD)
                for j, (c, q, w) in enumerate(SB_COLS):
                    k0 = KEY_TILES[j][0]
                    mm = pe.matmul(bank[:, c:c + w], KA[r, h // 2, k0:k0 + P], QA[r, h // 2, q:q + w],
                                   start=(first and j == 0), stop=last, skip_group_check=True)
                return mm

            def sb_start(h):
                if h >= 2:
                    pe.wait_ge(sb_spm, h - 1)
                sb_scores(h, sbank(h % 2), True, True).then_inc(sb_z, 1)

            def sb_values(h):
                pe.wait_ge(sb_am, h + 1)
                if h >= 2:
                    pe.wait_ge(sb_yd, h - 1)
                r = slice(HD * (h % 2), HD * (h % 2) + HD)
                for j, (c, q, w) in enumerate(SB_COLS):
                    m = KEY_TILES[j][1]
                    mm = pe.matmul(PS[r, h % 2, q:q + w], VA[0:m, j, HD * h:HD * h + HD],
                                   SB_A[h % 2][0:m, c:c + w], start=(j == 0), stop=(j == 2),
                                   skip_group_check=True)
                mm.then_inc(sb_y, 1)

            def index_products(t):
                q0, m = QRY_TILES[t]
                for h in range(HEADS):
                    j = t * HEADS + h
                    r = slice(HD * (h % 2), HD * (h % 2) + HD)
                    if j >= 2:
                        pe.wait_ge(ix_relu, j - 1)
                    pe.matmul(PS[0:m, 2 + j % 2, 0:T], QI[r, h // 2, q0:q0 + m], KI[r, :],
                              start=True, stop=True).then_inc(ix_mm, 1)

            pe.wait_ge(tt_done, 5)
            pe.wait_ge(sb_in, 48)
            pe.wait_ge(ka_zero, 1)
            pe.wait_ge(freed["act"], FREED[UNIT0["gb"] + 7][1])
            pe.wait_ge(rot_done, 10)
            sb_start(0)
            sb_start(1)
            for h in range(HEADS):
                x = sbank(2 + h % 2)
                pe.wait_ge(sb_spm, h + 1)
                if h >= 2:
                    pe.wait_ge(sb_e, h - 1)
                sb_scores(h, x, True, False)
                spm = SB_SPM[h % 2]
                for j, (c, q, w) in enumerate(SB_COLS):
                    for jj in range(j + 1, 3):
                        c2, q2, w2 = SB_COLS[jj]
                        pe.matmul(x[:, c + q2 - q:c + q2 - q + w2], negones[:], spm[:, c2:c2 + w2],
                                  start=False, stop=False, skip_group_check=True)
                    mm = pe.matmul(x[:, c:c + w], negu[:], spm[:, c:c + w], start=False, stop=(j == 2),
                                   skip_group_check=True)
                mm.then_inc(sb_x, 1)
                if h + 2 < HEADS:
                    sb_start(h + 2)
                if h:
                    sb_values(h - 1)
                if h % 3 == 0:
                    index_products(h // 3)
            sb_values(HEADS - 1)
            pe.wait_ge(sb_yd, HEADS)
            pe.wait_ge(ix_relu, 24)
            for h in range(HEADS):
                g = UNIT0["qlat"] + h
                bank_free(g)
                r = slice(HD * (h % 2), HD * (h % 2) + HD)
                pe.matmul(gbank(g)[:, 0:T], WUK[r, h // 2, :], QB[r, h // 2, :], start=True, stop=True)\
                    .then_inc(unit_done, 1)

            attn = [0, 0]

            def attention(query, value, pr, pt, name, tail):
                base, cbase = attn
                steps = [(h, t) for h in range(HEADS) for t in range(3)]

                def scores(i):
                    h, t = steps[i]
                    q0, m = QRY_TILES[t]
                    if i >= 2:
                        pe.wait_ge(at_m, base + i - 1)
                    for n, (q, k) in enumerate(query(h)):
                        mm = pe.matmul(sbank(i % 2)[0:m, 0:T], q[:, q0:q0 + m], k, start=(n == 0), stop=(n == 1))
                    mm.then_inc(at_l, 1)

                scores(0)
                def weighted(h):
                    g = UNIT0[f"{name}{h}"]
                    bank_free(g)
                    pe.wait_ge(at_ca, base + 3 * h + 3)
                    for j, (k0, mk) in enumerate(KEY_TILES):
                        mm = pe.matmul(gbank(g)[:, 0:T], value(h, j, mk), pt[h % 2][0:mk, j, :],
                                       start=(j == 0), stop=(j == 2))
                    mm.then_inc(unit_done, 1)

                for i, (h, t) in enumerate(steps):
                    if i + 1 < len(steps):
                        scores(i + 1)
                    if t == 0 and h:
                        weighted(h - 1)
                    if t == 1 and h:
                        tail(h - 1)
                    q0, m = QRY_TILES[t]
                    if i >= 2:
                        pe.wait_ge(at_ca, base + i - 1)
                    pe.wait_ge(at_p, base + i + 1)
                    for j, (c, mk) in enumerate(KEY_COLS):
                        mm = pe.matmul(sbank(2 + i % 2)[0:mk, j * P:j * P + m], pr[i % 2][0:m, c:c + mk],
                                       ident[0:m, 0:m], start=(j == 0), stop=True, skip_group_check=True)
                    mm.then_inc(at_t, 1)
                weighted(HEADS - 1)
                tail(HEADS - 1)
                attn[0] += len(steps)

            pe.wait_ge(freed["act"], FREED[UNIT0["qlat"] + 7][1])

            def dsa_query(h):
                r = slice(HD * (h % 2), HD * (h % 2) + HD)
                return (QB[r, h // 2, :], KR[r, :]), (QLAT[:, h, :], CKV[:, :])

            def dsa_tail(h):
                g = UNIT0[f"yb{h}"]
                bank_free(g)
                pe.wait_ge(freed["act"], FREED[UNIT0[f"olat{h}"]][1])
                r = slice(HD * (h % 2), HD * (h % 2) + HD)
                pe.matmul(gbank(g)[r, 0:T], WUV[:, h, :], OL[:], start=True, stop=True).then_inc(unit_done, 1)

            pe.wait_ge(dsa_in, 48)
            attention(dsa_query, lambda h, j, mk: CKVT[0:mk, j, :], PR, PT, "olat", dsa_tail)

            pe.wait_ge(sb_yd, HEADS)
            slab_ready(10)
            for m in range(8):
                product(UNIT0["za"] + m, 10, 4 * m, 4, lambda k: YAH[:, k, :], lambda k: YAL[:, k, :])
            pe.wait_ge(freed["dve"], FREED[UNIT0["yb7"]][1])
            slab_ready(11)
            for m in range(8):
                product(UNIT0["zb"] + m, 11, 4 * m, 4, lambda k: YBH[:, k, :], lambda k: YBL[:, k, :])
            pe.wait_ge(z_hi, 8)
            pe.wait_ge(z_lo, 8)
            for n in (12, 13):
                slab_ready(n)
                for u in range(4):
                    product(UNIT0["wo"] + 4 * (n - 12) + u, n, 8 * u, KB,
                            lambda k: ZH[:, k, :], lambda k: ZL[:, k, :])

            norm_sum(UMT, KB, sbank(0))
            pe.wait_ge(nrm_done, 16)
            for t, (q0, m) in enumerate(QRY_TILES):
                for half in range(2):
                    g = UNIT0["utok"] + 2 * t + half
                    bank_free(g)
                    for k in range(4):
                        mm = pe.matmul(gbank(g)[0:m, k * P:(k + 1) * P], UM[:, 4 * half + k, q0:q0 + m],
                                       ident[:], start=(k == 0), stop=True, skip_group_check=True)
                    mm.then_inc(unit_done, 1)
            g = UNIT0["router"]
            bank_free(g)
            pe.wait_ge(moe_in, 16 * 6)
            for t, (q0, m) in enumerate(QRY_TILES):
                for k in range(KB):
                    mm = pe.matmul(gbank(g)[0:m, 36 * t:36 * t + 36], UM[:, k, q0:q0 + m],
                                   small["WRT"][:, k, :], start=(k == 0), stop=(k == KB - 1),
                                   skip_group_check=True)
            mm.then_inc(unit_done, 1)
            MM, CC, CB, TA, N5 = (small[x] for x in ("MM", "CC", "CB", "TA", "N5"))
            g = UNIT0["rank"]
            bank_free(g)
            pe.wait_ge(rt_m, 1)
            for t in range(3):
                mm = pe.matmul(gbank(g)[0:NE, 0:1], MM[0:QRY_TILES[t][1], t, :], ones[0:QRY_TILES[t][1], 0:1], start=(t == 0), stop=(t == 2))
            mm.then_inc(unit_done, 1)
            g += 1
            bank_free(g)
            pe.wait_ge(rt_m, 2)
            for t in range(3):
                c = slice(NE * t, NE * t + NE)
                m = QRY_TILES[t][1]
                for tt in range(t):
                    pe.matmul(gbank(g)[:, c], ones[:], MM[:, tt, :], start=(tt == 0), stop=False,
                              skip_group_check=True)
                pe.matmul(gbank(g)[:, c], utri[0:m, :], MM[0:m, t, :], start=(t == 0), stop=False,
                          skip_group_check=True)
                pe.matmul(gbank(g)[:, c], CB[0:NE, :], utri[0:NE, 0:NE], start=False, stop=True,
                          skip_group_check=True)
            pe.matmul(gbank(g)[0:NE, 96:97], utri[0:NE, 0:NE], CC[0:NE, 0:1], start=False, stop=True,
                      skip_group_check=True)
            pe.matmul(gbank(g)[0:NE, 97:98], utri[0:NE, 0:NE], CC[0:NE, 1:2], start=False, stop=False,
                      skip_group_check=True)
            pe.matmul(gbank(g)[0:NE, 97:98], ident[0:NE, 0:NE], CC[0:NE, 1:2], start=False, stop=True,
                      skip_group_check=True).then_inc(unit_done, 1)
            g += 1
            bank_free(g)
            pe.wait_ge(rt_m, 3)
            pe.matmul(gbank(g)[0:1, 0:81], ones[0:NE, 0:1], TA[0:NE, 0:81], start=True, stop=True)\
                .then_inc(unit_done, 1)
            pe.wait_ge(perm_done, 1)
            pe.wait_ge(freed["act"], FREED[UNIT0["utok"] + 5][1])
            for k in range(KB):
                for half in range(2):
                    g = UNIT0["disp"] + 2 * k + half
                    bank_free(g)
                    c0 = half * (XCOLS // 2)
                    for t, (q0, m) in enumerate(QRY_TILES):
                        mm = pe.matmul(gbank(g)[:, 0:XCOLS // 2], UTOK[0:m, t, k * P:(k + 1) * P],
                                       PERM[0:m, t, c0:c0 + XCOLS // 2], start=(t == 0), stop=(t == 2))
                    mm.then_inc(unit_done, 1)
            pe.wait_ge(freed["act"], FREED[UNIT0["disp"] + 15][1])
            pe.wait_ge(tbl_done, 1)
            pe.nop().then_inc(xh_done, 2)
            pe.nop().then_inc(xy_done, 2)

            def hidden(base, s):
                pe.wait_ge(xw_done, base + (s + 1))
                pe.wait_ge(xhid_done, base + (s + 1))
                for b in range(2):
                    pe.wait_ge(xp_full[3 * s + b], base * 8 + 16)
                    hb = PS[:, 2 * b + s, :]
                    for m in range(4):
                        for k in range(KB):
                            mm = pe.matmul(hb[:, WIN * m:WIN * m + WIN],
                                           XPT[3 * s + b][:, (m * KB + k) * P:(m * KB + k + 1) * P],
                                           XW[s][:, k, :], start=(k == 0), stop=(k == KB - 1))
                mm.then_inc(xh_done, 1)

            def outputs(base, s):
                pe.wait_ge(xp_full[3 * s + 2], base * 8 + 16)
                pe.wait_ge(xye_done, base + (s + 1))
                pe.wait_ge(xhid_done, base + (s + 3))
                for m in range(8):
                    for k in range(4):
                        mm = pe.matmul(PS[:, 4 + 2 * s + m // 4, WIN * (m % 4):WIN * (m % 4) + WIN],
                                       XPT[3 * s + 2][:, (m * 4 + k) * P:(m * 4 + k + 1) * P],
                                       HID[s][:, k, :], start=(k == 0), stop=(k == 3))
                mm.then_inc(xy_done, 1)

            hidden(0, 0)
            last = pe.value_load(TBL[0:1, 81:82], min_val=2, max_val=ITEMS - 2)
            with pe.Fori(0, last, 2) as i:
                hidden(i, 1)
                outputs(i, 0)
                hidden(i + 2, 0)
                outputs(i, 1)
            hidden(last, 1)
            outputs(last, 0)
            outputs(last, 1)
            pe.wait_ge(xye_done, last + 4)
            pe.nop().then_inc(moe_pe, 1)
            pe.wait_ge(moe_act, 1)
            for st in range(5):
                m = min(P, SLOTS - P * st)
                for half in range(2):
                    g = UNIT0["yslot"] + 2 * st + half
                    bank_free(g)
                    for k in range(4):
                        mm = pe.matmul(gbank(g)[0:m, k * P:(k + 1) * P],
                                       YS[:, 4 * half + k, P * st:P * st + m], ident[:],
                                       start=(k == 0), stop=True, skip_group_check=True)
                    mm.then_inc(unit_done, 1)
            pe.wait_ge(g_done, 3)
            for st in range(5):
                m = min(P, SLOTS - P * st)
                g = UNIT0["gt"] + st
                bank_free(g)
                for t, (q0, mq) in enumerate(QRY_TILES):
                    mm = pe.matmul(gbank(g)[0:m, q0:q0 + mq], G[0:mq, t, P * st:P * st + m],
                                   ident[0:mq, 0:mq], start=(t == 0), stop=True, skip_group_check=True)
                mm.then_inc(unit_done, 1)
            pe.wait_ge(freed["act"], FREED[UNIT0["yslot"] + 9][1])
            pe.wait_ge(freed["dve"], FREED[UNIT0["gt"] + 4][1])
            for k in range(KB):
                g = UNIT0["comb"] + k
                bank_free(g)
                for st in range(5):
                    m = min(P, SLOTS - P * st)
                    mm = pe.matmul(gbank(g)[:, 0:T], YSLOT[0:m, st, k * P:(k + 1) * P], GT[0:m, st, :],
                                   start=(st == 0), stop=(st == 4))
                mm.then_inc(unit_done, 1)
            norm_sum(UMT, KB, sbank(0))
            norm_sum(SQ3, KB, sbank(0))
            pe.wait_ge(nlo_done, 16)
            pe.wait_ge(nhi_done, 16)
            n = FIRST_SLAB["ret_qk"]
            for h in range(RH):
                slab_ready(n + h)
                for u in range(4):
                    product(UNIT0["rqk"] + 4 * h + u, n + h, 8 * u, KB, *U)
            n = FIRST_SLAB["ret_v"]
            for h in range(RH):
                slab_ready(n + h)
                for j, t0 in enumerate(TOK3):
                    token_major(UNIT0["rv"] + 3 * h + j, n + h, KB, 512, 0, *UT, t0)
            n = FIRST_SLAB["ret_gate"]
            for h in range(4):
                slab_ready(n + h)
                for u in range(4):
                    product(UNIT0["gate"] + 4 * h + u, n + h, 8 * u, KB, *U)
            pe.wait_ge(rqk_done, 8)
            pe.wait_ge(freed["act"], FREED[UNIT0["rv"] + 11][1])

            def ret_scores(h):
                for j, (c, mk) in enumerate(KEY_COLS):
                    i = 3 * h + j
                    if i >= 3:
                        pe.wait_ge(st_done, i - 2)
                    for b in range(2):
                        mm = pe.matmul(sbank(i % 3)[0:mk, 0:T], RK[:, 2 * h + b, c:c + mk], RQ[:, 2 * h + b, :],
                                       start=(b == 0), stop=(b == 1))
                    mm.then_inc(st_mm, 1)

            ret_scores(0)
            for h in range(RH):
                pe.wait_ge(st_done, 3 * (h + 1))
                for v in range(4):
                    g = UNIT0["ro"] + 4 * h + v
                    bank_free(g)
                    for j, (k0, mk) in enumerate(KEY_TILES):
                        mm = pe.matmul(gbank(g)[:, 0:T], RVV[h][0:mk, j, v * P:(v + 1) * P],
                                       ST[h % 2][0:mk, j, :], start=(j == 0), stop=(j == 2))
                    mm.then_inc(unit_done, 1)
                if h + 1 < RH:
                    ret_scores(h + 1)
                pe.wait_ge(freed["act"], FREED[UNIT0["ro"] + 4 * h + 3][1])
                if h:
                    pe.wait_ge(gvar, h)
                for v in range(4):
                    mm = pe.matmul(sbank(3)[:, 0:T], ones[:], RO[:, v, :], start=(v == 0), stop=(v == 3))
                mm.then_inc(ro_sum, 1)
                pe.wait_ge(rsq_done, h + 1)
                pe.wait_ge(gmu_done, h + 1)
                for v in range(4):
                    mm = pe.matmul(sbank(3)[:, 0:T], ones[:], RSQ[:, v, :], start=(v == 0), stop=(v == 3))
                mm.then_inc(gv_mm, 1)
            pe.wait_ge(rhi_done, RH)
            pe.wait_ge(rlo_done, RH)
            n = FIRST_SLAB["ret_o"]
            for s in range(4):
                slab_ready(n + s)
                for u in range(2):
                    product(UNIT0["rwo"] + 2 * s + u, n + s, 16 * u, 16,
                            lambda k: RHI[:, k, :], lambda k: RLO[k // 4][:, k % 4, :])

            def ffn(layer, norms_done):
                norm_sum(SQ2, KB, sbank(0))
                pe.wait_ge(nlo_done, norms_done)
                pe.wait_ge(nhi_done, norms_done)
                n = FIRST_SLAB[f"up{layer}"]
                for s in range(11):
                    slab_ready(n + s)
                    for u in range(4):
                        product(UNIT0[f"up{layer}"] + 4 * s + u, n + s, 8 * u, KB, *U)
                pe.wait_ge(f_hi, FB * (layer + 1))
                pe.wait_ge(f_lo, FB * (layer + 1))
                n = FIRST_SLAB[f"down{layer}"]
                for s in range(8):
                    slab_ready(n + s)
                    product(UNIT0[f"down{layer}"] + s, n + s, 0, FB,
                            lambda k: TH[:, k, :], lambda k: TL[:, k, :])

            ffn(0, 24)
            norm_sum(SQM, KB, sbank(0))
            pe.wait_ge(nlo_done, 8 * 4)
            pe.wait_ge(nhi_done, 8 * 4)
            n = FIRST_SLAB["kv_c"]
            slab_ready(n)
            for u in range(4):
                product(UNIT0["kvc"] + u, n, 8 * u, KB, *U)
            slab_ready(n + 1)
            product(UNIT0["krq"], n + 1, 0, KB, *U)
            pe.wait_ge(nlo_done, 8 * 5)
            pe.wait_ge(nhi_done, 8 * 5)
            for u in range(1, 4):
                product(UNIT0["krq"] + u, n + 1, 8 * u, KB, *U)
            norm_sum(SQQ, 4, sbank(0))
            slab_ready(n + 2)
            for u in range(3):
                product(UNIT0["qar"] + u, n + 2, 8 * u, KB, *U)
            pe.wait_ge(nlo_done, 8 * 5 + 4)
            pe.wait_ge(nhi_done, 8 * 5 + 4)
            CK = (lambda k: CKH[:, k, :]), (lambda k: CKL[:, k, :])
            CKT = (lambda k, t: CKH[:, k, t:t + P]), (lambda k, t: CKL[:, k, t:t + P])
            slab_ready(n + 3)
            for u in range(8):
                product(UNIT0["kn"] + u, n + 3, 4 * u, 4, *CK)
                if u == 3:
                    norm_sum(SQQ, 6, sbank(0))
            slab_ready(n + 4)
            for j, t0 in enumerate(TOK3):
                for half in range(2):
                    token_major(UNIT0["vm"] + 2 * j + half, n + 4, 4, D, 512 * half, *CKT, t0)
            pe.wait_ge(nlo_done, 8 * 5 + 10)
            pe.wait_ge(nhi_done, 8 * 5 + 10)
            n = FIRST_SLAB["q_b"]
            for s in range(3):
                slab_ready(n + s)
                for u in range(4):
                    product(UNIT0["qn"] + 4 * s + u, n + s, 6 * u, 6,
                            lambda k: CQH[:, k, :], lambda k: CQL[:, k, :])
            for j in range(5):
                t, src = (QR[:, j, :], UNIT0["qr"] + j) if j < 4 else (KR2[:, :], UNIT0["krq"])
                pe.wait_ge(freed["act"], FREED[src][1])
                if j >= 4:
                    pe.wait_ge(rot_free, 10 + j - 3)
                pe.matmul(sbank(j % 4)[:, 0:T], rot[:], t, start=True, stop=True).then_inc(rot_mm, 1)
            pe.wait_ge(rot_done, 15)

            def mla_query(h):
                r = slice(HD * (h % 2), HD * (h % 2) + HD)
                return (QN[:, h, :], KN[:, h, :]), (QR[r, h // 2, :], KR2[r, :])

            attention(mla_query, lambda h, j, mk: VM[0:mk, j, h * P:(h + 1) * P], PR2, PT2, "om",
                      lambda h: None)
            pe.wait_ge(freed["dve"], FREED[UNIT0["om7"]][1])
            n = FIRST_SLAB["mla_o"]
            for s in range(2):
                slab_ready(n + s)
                for u in range(4):
                    product(UNIT0["mo"] + 4 * s + u, n + s, 8 * u, KB,
                            lambda k: OMH[:, k, :], lambda k: OML[:, k, :])
            ffn(1, 58)
            norm_sum(SQ2, KB, sbank(0))

        @block.scalar
        def _(act):
            steps = [0]

            def link(ins):
                steps[0] += 1
                ins.then_inc(act_step, 1)
                act.wait_ge(act_step, steps[0])

            def hi(n):
                act.wait_ge(raw_full[n % 3], 16 * (n // 3 + 1))
                if n >= 2:
                    act.wait_ge(unit_done, SLAB_UNITS[n - 2])
                w = SLABS[n][1] * P
                act.activation(WH[n % 2][:, 0:w], RAW[n % 3][:, 0:w], ACT.Copy).then_inc(hi_done, 1)

            def read_out(g, dst, func=ACT.Copy, rows=slice(0, P), cols=slice(0, T), **kw):
                act.wait_ge(unit_done, g + 1)
                act.activation(dst, gbank(g)[rows, cols], func, **kw).then_inc(freed["act"], 1)

            norms, split = [0], [0]

            def squares(dst, src):
                act.activation(dst, src, ACT.Square).then_inc(sq_done, 1)

            def std():
                norms[0] += 1
                act.wait_ge(var_done, norms[0])
                act.activation(rs[:], rs[:], ACT.Sqrt).then_inc(std_done, 1)

            def high(dst, src, nrm):
                act.wait_ge(nrm_done, nrm)
                act.activation(dst, src, ACT.Copy).then_inc(nhi_done, 1)

            act.wait_ge(h_in, 16)
            squares(SQ[:], H[:])
            std()
            hi(0)
            for k in range(KB):
                high(UH[:, k, :], SQ[:, k, :], k + 1)
            hi(1)
            for u in range(4):
                read_out(UNIT0["qa"] + u, QA[:, u, :], scale=HD ** -0.5)
            hi(2)
            for u in range(4):
                read_out(UNIT0["ka"] + u, KA[:, u, 0:T])
            hi(3)
            for j in range(3):
                if j < 2:
                    read_out(UNIT0["va"] + j, VA[:, j, :], cols=slice(0, 512))
                else:
                    read_out(UNIT0["va"] + j, VA[0:32, j, :], rows=slice(96, P), cols=slice(0, 512))
            hi(4)
            for u in range(4):
                read_out(UNIT0["qb"] + u, QB[:, u, :])
            hi(5)
            for u, dst in enumerate((CKV, KR, KI, WIT)):
                read_out(UNIT0["misc"] + u, dst[:])
            hi(6)
            for u in range(4):
                read_out(UNIT0["qi"] + u, QI[:, u, :])
            hi(7)
            for n in range(6, 10):
                for u in range(4):
                    k = 4 * (n - 6) + u
                    read_out(UNIT0["ga"] + k, (GA if k < KB else GB)[:, k % KB, :], ACT.Sigmoid)
                if n < 9:
                    hi(n + 2)
            act.wait_ge(tt_mm, 1)
            for j, (k0, mk) in enumerate(KEY_TILES):
                act.activation(CKVT[0:mk, j, :], sbank(0)[0:mk, j * P:(j + 1) * P], ACT.Copy)\
                    .then_inc(tt_done, 1)
            for rows, c in ((P, slice(0, 2)), (16, slice(2, 3))):
                act.activation(WI[0:rows, c, :], sbank(0)[0:rows, 384 + 8 * c.start:384 + 8 * c.stop]
                               .rearrange("p (t h) -> p t h", h=8), ACT.Copy).then_inc(tt_done, 1)

            def sb_log(h):
                L = SB_L[h % 2]
                act.wait_ge(sb_z, h + 1)
                link(act.activation(L[:], sbank(h % 2)[:, 0:SBW], ACT.Abs))
                link(act.activation(L[:], L[:], ACT.Exp, scale=-1.0))
                act.activation(L[:], L[:], ACT.Ln, bias=1.0).then_inc(sb_l, 1)

            def index_relu(t):
                m = QRY_TILES[t][1]
                for h in range(HEADS):
                    j = t * HEADS + h
                    act.wait_ge(ix_mm, j + 1)
                    if j >= 2:
                        act.wait_ge(ix_used, j - 1)
                    act.activation(RL[j % 2][0:m, :], PS[0:m, 2 + j % 2, 0:T], ACT.Relu).then_inc(ix_relu, 1)

            sb_log(0)
            for h in range(HEADS):
                if h + 1 < HEADS:
                    sb_log(h + 1)
                act.wait_ge(sb_x, h + 1)
                if h >= 2:
                    act.wait_ge(sb_y, h - 1)
                act.activation(SB_A[h % 2][:], sbank(2 + h % 2)[:, 0:SBW], ACT.Exp).then_inc(sb_e, 1)
                if h % 3 == 0:
                    index_relu(h // 3)

            for h in range(HEADS):
                read_out(UNIT0["qlat"] + h, QLAT[:, h, :])

            attn = [0]

            def attention(pr, pt, scale, name, tail):
                base = attn[0]
                steps_ = [(h, t) for h in range(HEADS) for t in range(3)]

                def exps(i):
                    m = QRY_TILES[steps_[i][1]][1]
                    act.wait_ge(at_b, base + i + 1)
                    act.activation(pr[i % 2][0:m, :], pr[i % 2][0:m, :], ACT.Exp, scale=scale,
                                   bias=SMALL[0:m, 2 + i % 2:3 + i % 2],
                                   accum_out=SMALL[0:m, 4 + i % 2:5 + i % 2]).then_inc(at_e, 1)

                exps(0)
                for i, (h, t) in enumerate(steps_):
                    if i + 1 < len(steps_):
                        exps(i + 1)
                    if t == 0 and h:
                        tail(h - 1)
                    q0, m = QRY_TILES[t]
                    act.wait_ge(at_t, base + i + 1)
                    if t == 0 and h >= 2:
                        act.wait_ge(unit_done, UNIT0[f"{name}{h - 2}"] + 1)
                    b = sbank(2 + i % 2)
                    act.activation(pt[h % 2][:, 0:2, q0:q0 + m],
                                   b[:, 0:2 * P].rearrange("p (j q) -> p j q", j=2)[:, :, 0:m], ACT.Copy)
                    act.activation(pt[h % 2][0:32, 2, q0:q0 + m], b[0:32, 2 * P:2 * P + m], ACT.Copy)\
                        .then_inc(at_ca, 1)
                tail(HEADS - 1)
                attn[0] += len(steps_)

            def dsa_tail(h):
                if h:
                    act.wait_ge(unit_done, UNIT0[f"yb{h - 1}"] + 1)
                read_out(UNIT0[f"olat{h}"], OL[:])

            attention(PR, PT, HD ** -0.5, "olat", dsa_tail)
            act.wait_ge(unit_done, UNIT0["yb7"] + 1)
            hi(11)
            hi(12)
            for m in range(8):
                act.wait_ge(z_done, m + 1)
                act.activation(ZH[:, m, :], ZT[:, m % 2, :], ACT.Copy).then_inc(z_hi, 1)
            hi(13)

            act.wait_ge(freed["dve"], FREED[UNIT0["wo"] + 7][1])
            squares(UMT[:], H[:])
            std()
            for t, (q0, m) in enumerate(QRY_TILES):
                for half in range(2):
                    read_out(UNIT0["utok"] + 2 * t + half, UTOK[0:m, t, 512 * half:512 * half + 512],
                             rows=slice(0, m), cols=slice(0, 512))
            for j, tile in enumerate(("GE", "M2")):
                act.wait_ge(rt_exp, j + 1)
                act.activation(small[tile][:], small[tile][:], ACT.Exp).then_inc(rt_gd, 1)
            for k in range(KB):
                for half in range(2):
                    c0 = half * (XCOLS // 2)
                    read_out(UNIT0["disp"] + 2 * k + half, XS[:, k, c0:c0 + XCOLS // 2],
                             cols=slice(0, XCOLS // 2))
            act.wait_ge(tbl_done, 1)
            items = act.value_load(TBL[0:1, 80:81], min_val=1, max_val=ITEMS // 2) * 2
            act.nop().then_inc(xye_done, 2)
            with act.Fori(0, items, 2) as i:
                for s in range(2):
                    at_ = act.value_load(TBL[0:1, bass.ds(i + s, 1)], min_val=0, max_val=SLOTS)
                    act.wait_ge(xh_done, i + (s + 3))
                    act.wait_ge(xhid_done, i + (s + 1))
                    act.activation(SG[s][:], PS[:, s, 0:4 * WIN].rearrange("p (m w) -> p m w", m=4),
                                   ACT.Sigmoid).then_inc(xs_done, 1)
                    act.wait_ge(xy_done, i + (s + 3))
                    act.wait_ge(xye_done, i + (s + 2))
                    act.activation(YS[:, :, bass.ds(at_, WIN)].rearrange("p (b m) w -> p b m w", b=2),
                                   PS[:, 4 + 2 * s:6 + 2 * s, 0:4 * WIN].rearrange("p b (m w) -> p b m w", m=4),
                                   ACT.Copy).then_inc(xye_done, 1)
            act.wait_ge(xye_done, items + 2)
            act.nop().then_inc(moe_act, 1)
            for st in range(5):
                m = min(P, SLOTS - P * st)
                for half in range(2):
                    read_out(UNIT0["yslot"] + 2 * st + half, YSLOT[0:m, st, 512 * half:512 * half + 512],
                             rows=slice(0, m), cols=slice(0, 512))
            act.wait_ge(moe_pe, 1)
            act.wait_ge(freed["dve"], FREED[UNIT0["comb"] + 7][1])
            squares(UMT[:], H[:])
            std()
            hi(N_FIRST)
            act.wait_ge(meta2_in, 16)
            act.wait_ge(nrm_done, 24)
            squares(SQ3[:], H[:])
            std()
            for k in range(KB):
                high(UH[:, k, :], SQ3[:, k, :], 24 + k + 1)
            hi(N_FIRST + 1)
            n = FIRST_SLAB["ret_qk"]
            for h in range(RH):
                hi(n + h + 2)
            for h in range(RH):
                for j in range(3):
                    if j < 2:
                        read_out(UNIT0["rv"] + 3 * h + j, RVV[h][:, j, :], cols=slice(0, 512))
                    else:
                        read_out(UNIT0["rv"] + 3 * h + j, RVV[h][0:32, j, :], rows=slice(96, P),
                                 cols=slice(0, 512))
                hi(n + RH + h + 2)
            for s in range(4):
                for u in range(4):
                    j = 4 * s + u
                    g = UNIT0["gate"] + j
                    act.wait_ge(unit_done, g + 1)
                    if j == 0:
                        act.wait_ge(rqk_done, 8)
                    if j >= 2:
                        act.wait_ge(freed["dve"], FREED[g - 2][1])
                    act.activation(GSIG[j % 2][:], gbank(g)[:, 0:T], ACT.Sigmoid).then_inc(gsig_done, 1)
                hi(n + 2 * RH + s + 2)
            for h in range(RH):
                if h:
                    act.wait_ge(rn_done, h)
                for v in range(4):
                    read_out(UNIT0["ro"] + 4 * h + v, RO[:, v, :])
                act.wait_ge(oc_done, h + 1)
                if h:
                    act.wait_ge(rlo_done, h)
                act.activation(RSQ[:], RO[:], ACT.Square).then_inc(rsq_done, 1)
                act.wait_ge(gvar, h + 1)
                act.activation(GRS[:], GRS[:], ACT.Sqrt).then_inc(gstd, 1)
                act.wait_ge(rn_done, h + 1)
                act.activation(RHI[:, 4 * h:4 * h + 4, :], RSQ[:], ACT.Copy).then_inc(rhi_done, 1)
            n = FIRST_SLAB["ret_o"]
            for s in range(4):
                hi(n + s + 2)

            def ffn(layer, before, h_unit, nrm):
                act.wait_ge(freed["dve"], FREED[h_unit][1])
                squares(SQ2[:], H[:])
                std()
                for k in range(KB):
                    high(UH[:, k, :], SQ2[:, k, :], nrm + k + 1)
                n = FIRST_SLAB[f"up{layer}"]
                f0 = FB * layer

                def high_hidden(p):
                    act.wait_ge(freed["dve"], FREED[UNIT0[f"up{layer}"] + 2 * p + 1][1])
                    act.activation(TH[:, p, :], FU[p % 2][:], ACT.Copy).then_inc(f_hi, 1)

                for p in range(FB):
                    g = UNIT0[f"up{layer}"] + 2 * p
                    act.wait_ge(unit_done, g + 1)
                    if p >= 2:
                        act.wait_ge(freed["dve"], FREED[g - 4][1])
                    act.activation(FS[p % 2][:], gbank(g)[:, 0:T], ACT.Sigmoid).then_inc(f_sig, 1)
                    if p:
                        high_hidden(p - 1)
                    if p % 2:
                        if n + p // 2 + 2 < len(SLABS):
                            hi(n + p // 2 + 2)
                high_hidden(FB - 1)
                n = FIRST_SLAB[f"down{layer}"]
                for s in range(8):
                    if n + s + 2 < len(SLABS):
                        hi(n + s + 2)

            ffn(0, 16, UNIT0["rwo"] + 7, 32)
            act.wait_ge(freed["dve"], FREED[UNIT0["down0"] + 7][1])
            squares(SQM[:], H[:])
            std()
            for k in range(KB):
                high(UH[:, k, :], SQM[:, k, :], 40 + k + 1)
            for u in range(4):
                read_out(UNIT0["kvc"] + u, CKRAW[:, u, :])
            act.wait_ge(freed["act"], FREED[UNIT0["kvc"] + 3][1])
            squares(SQQ[:, 0:4, :], CKRAW[:])
            hi(FIRST_SLAB["kv_c"] + 2)
            read_out(UNIT0["krq"], KR2[:])
            for k in range(KB):
                high(UH[:, k, :], SQM[:, k, :], 48 + k + 1)
            for u in range(3):
                read_out(UNIT0["krq"] + 1 + u, CRAW[:, u, :])
            std()
            for k in range(4):
                high(CKH[:, k, :], SQQ[:, k, :], 56 + k + 1)
            hi(FIRST_SLAB["kv_c"] + 3)
            for u in range(3):
                read_out(UNIT0["qar"] + u, CRAW[:, 3 + u, :])
            hi(FIRST_SLAB["kv_c"] + 4)
            act.wait_ge(freed["act"], FREED[UNIT0["qar"] + 2][1])
            act.wait_ge(nlo_done, 44)
            squares(SQQ[:, 0:6, :], CRAW[:])
            for u in range(4):
                read_out(UNIT0["kn"] + u, KN[:, u, :])
            std()
            for u in range(4, 8):
                read_out(UNIT0["kn"] + u, KN[:, u, :])
            for k in range(6):
                high(CQH[:, k, :], SQQ[:, k, :], 60 + k + 1)
            hi(FIRST_SLAB["kv_c"] + 5)
            for j in range(3):
                for half in range(2):
                    g = UNIT0["vm"] + 2 * j + half
                    c = slice(512 * half, 512 * half + 512)
                    if j < 2:
                        read_out(g, VM[:, j, c], cols=slice(0, 512))
                    else:
                        read_out(g, VM[0:32, j, c], rows=slice(96, P), cols=slice(0, 512))
            hi(FIRST_SLAB["kv_c"] + 6)
            for s in range(3):
                for u in range(4):
                    j = 4 * s + u
                    if j == 0:
                        act.wait_ge(nlo_done, 50)
                    read_out(UNIT0["qn"] + j, QN[:, j, :] if j < 8 else QR[:, j - 8, :])
                hi(FIRST_SLAB["q_b"] + s + 2)
            attention(PR2, PT2, (P + HD) ** -0.5, "om", lambda h: None)
            for s in range(2):
                hi(FIRST_SLAB["mla_o"] + s + 2)
            ffn(1, 50, UNIT0["mo"] + 7, 66)
            act.wait_ge(freed["dve"], FREED[UNIT0["down1"] + 7][1])
            squares(SQ2[:], H[:])
            std()

        @block.vector
        def _(dve):
            steps = [0]

            def link(ins):
                steps[0] += 1
                ins.then_inc(dve_step, 1)
                dve.wait_ge(dve_step, steps[0])

            def lo(n):
                dve.wait_ge(hi_done, n + 1)
                w = SLABS[n][1] * P
                dve.tensor_tensor(WL[n % 2][:, 0:w], RAW[n % 3][:, 0:w], WH[n % 2][:, 0:w].bitcast(F32),
                                  ALU.subtract).then_inc(lo_done, 1)

            def freeing(ins, n=1):
                ins.then_inc(freed["dve"], n)

            norms, nrm = [0], [0]

            def scale_of(n):
                norms[0] += 1
                dve.wait_ge(ssq_done, norms[0])
                dve.tensor_scalar(rs[:], sbank(0)[:, 0:T], 1.0 / n, EPS, ALU.mult, ALU.add).then_inc(var_done, 1)
                dve.wait_ge(std_done, norms[0])
                link(dve.reciprocal(rs[:], rs[:]))

            def normed(dst, src, gain, nb, c0=0):
                for k in range(nb):
                    gcol = GAINS[gain] + k
                    dve.scalar_tensor_tensor(out=dst[:, k, c0:], in0=src[:, k, c0:], scalar=gains[:, gcol:gcol + 1],
                                             in1=rs[:, c0:], op0=ALU.mult, op1=ALU.mult).then_inc(nrm_done, 1)

            def add_to_h(g, m):
                dve.wait_ge(unit_done, g + 1)
                freeing(dve.tensor_tensor(H[:, m, :], gbank(g)[:, 0:T], H[:, m, :], ALU.add))

            def bc(ap, shape):
                return ap.broadcast_to(shape)

            dve.wait_ge(const_in, 16 * 7)
            scale_of(D)
            normed(SQ, H, "mix", KB)
            for n in range(8):
                lo(n)

            def rotated(j, t, scratch):
                dve.wait_ge(rot_mm, j + 1)
                dve.tensor_tensor(scratch[:, j % 2, :], sbank((j if j < 10 else j - 10) % 4)[:, 0:T], sinw[:],
                                  ALU.mult).then_inc(rot_free, 1)
                link(dve.tensor_tensor(t, t, cosw[:], ALU.mult))
                dve.wait_ge(rot_free, j + 1)
                dve.tensor_tensor(t, t, scratch[:, j % 2, :], ALU.add).then_inc(rot_done, 1)

            ROT = [QB[:, j, :] for j in range(4)] + [KR[:], KI[:]] + [QI[:, j, :] for j in range(4)]
            for n in range(6, 10):
                for j in range(3 * (n - 6), min(3 * (n - 6) + 3, 10)):
                    rotated(j, ROT[j], ROT_T)
                if n < 9:
                    lo(n + 2)

            def sb_softplus(h):
                dve.wait_ge(sb_l, h + 1)
                link(dve.scalar_tensor_tensor(out=SB_SP[h % 2][:], in0=sbank(h % 2)[:, 0:SBW], scalar=0.0,
                                              in1=SB_L[h % 2][:], op0=ALU.max, op1=ALU.add))
                dve.tensor_tensor(SB_SPM[h % 2][:], SB_SP[h % 2][:], SBM[:], ALU.mult).then_inc(sb_spm, 1)

            def index_scores(t):
                q0, m = QRY_TILES[t]
                sc = SCORE[0:m, t, :]
                for h in range(HEADS):
                    j = t * HEADS + h
                    dve.wait_ge(ix_relu, j + 1)
                    if h:
                        dve.wait_ge(ix_used, j)
                        dve.scalar_tensor_tensor(out=sc, in0=RL[j % 2][0:m, :], scalar=WI[0:m, t, h:h + 1], in1=sc,
                                                 op0=ALU.mult, op1=ALU.add).then_inc(ix_used, 1)
                    else:
                        dve.tensor_scalar(sc, RL[j % 2][0:m, :], WI[0:m, t, h:h + 1], None, ALU.mult)\
                            .then_inc(ix_used, 1)
                dve.wait_ge(ix_used, HEADS * (t + 1))
                link(dve.tensor_tensor(sc, sc, BND[0:m, t, :], ALU.min))

            def take_best(t, rounds):
                m = QRY_TILES[t][1]
                sc = SCORE[0:m, t, :]
                for _ in range(rounds):
                    link(dve.max(MAX8[0:m, :], sc))
                    link(dve.match_replace(sc, MAX8[0:m, :], sc, -3.4e38))

            def key_mask(t):
                m = QRY_TILES[t][1]
                sc = SCORE[0:m, t, :]
                link(dve.scalar_tensor_tensor(out=sc, in0=sc, scalar=-3.3e38, in1=ADM[0:m, t, :],
                                              op0=ALU.is_le, op1=ALU.mult))
                dve.tensor_scalar(NEG[0:m, t, :], sc, -1.0, BIG, ALU.add, ALU.mult).then_inc(ix_neg, 1)

            def index_part(i):
                t = i // 3
                if i % 3 == 0:
                    index_scores(t)
                else:
                    take_best(t, TOPK // 16)
                if i % 3 == 2:
                    key_mask(t)

            def sb_out(h):
                dve.wait_ge(sb_y, h + 1)
                r = slice(HD * (h % 2), HD * (h % 2) + HD)
                link(dve.tensor_copy(YAH[r, h // 2, :], PS[r, h % 2, 0:T]))
                dve.tensor_tensor(YAL[r, h // 2, :], PS[r, h % 2, 0:T], YAH[r, h // 2, :].bitcast(F32),
                                  ALU.subtract).then_inc(sb_yd, 1)

            dve.wait_ge(sb_in, 48)
            dve.wait_ge(dsa_in, 48)
            sb_softplus(0)
            for h in range(HEADS):
                if h + 1 < HEADS:
                    sb_softplus(h + 1)
                dve.wait_ge(sb_e, h + 1)
                dve.scalar_tensor_tensor(out=SB_A[h % 2][:], in0=SB_A[h % 2][:], scalar=3e38, in1=SBM[:],
                                         op0=ALU.min, op1=ALU.mult).then_inc(sb_am, 1)
                if h:
                    sb_out(h - 1)
                index_part(h)
            sb_out(HEADS - 1)
            index_part(8)
            dve.wait_ge(ix_neg, 3)

            attn = [0]

            def attention(neg, pr, scale, tail):
                base = attn[0]
                steps_ = [(h, t) for h in range(HEADS) for t in range(3)]

                def maxima(i):
                    t = steps_[i][1]
                    m = QRY_TILES[t][1]
                    dve.wait_ge(at_l, base + i + 1)
                    if i >= 2:
                        dve.wait_ge(at_t, base + i - 1)
                    mx = SMALL[0:m, i % 2:i % 2 + 1]
                    dve.tensor_tensor_reduce(pr[i % 2][0:m, :], sbank(i % 2)[0:m, 0:T], neg[0:m, t, :], 1.0,
                                             -3.4e38, ALU.add, ALU.max, mx).then_inc(at_m, 1)
                    dve.wait_ge(at_m, base + i + 1)
                    dve.tensor_scalar(SMALL[0:m, 2 + i % 2:3 + i % 2], mx, -scale, None, ALU.mult)\
                        .then_inc(at_b, 1)

                maxima(0)
                for i, (h, t) in enumerate(steps_):
                    m = QRY_TILES[t][1]
                    dve.wait_ge(at_e, base + i + 1)
                    rc = SMALL[0:m, 6 + i % 2:7 + i % 2]
                    link(dve.reciprocal(rc, SMALL[0:m, 4 + i % 2:5 + i % 2]))
                    dve.tensor_scalar(pr[i % 2][0:m, :], pr[i % 2][0:m, :], rc, None, ALU.mult).then_inc(at_p, 1)
                    if i + 1 < len(steps_):
                        maxima(i + 1)
                    if t == 1 and h:
                        tail(h - 1)
                tail(HEADS - 1)
                attn[0] += len(steps_)

            def split_out(g, rows, dh, dl):
                dve.wait_ge(unit_done, g + 1)
                link(dve.tensor_copy(dh, gbank(g)[rows, 0:T]))
                freeing(dve.tensor_tensor(dl, gbank(g)[rows, 0:T], dh.bitcast(F32), ALU.subtract))

            def dsa_tail(h):
                r = slice(HD * (h % 2), HD * (h % 2) + HD)
                split_out(UNIT0[f"yb{h}"], r, YBH[r, h // 2, :], YBL[r, h // 2, :])

            attention(NEG, PR, HD ** -0.5, dsa_tail)
            lo(11)

            for m in range(8):
                g = UNIT0["za"] + m
                dve.wait_ge(unit_done, g + 1)
                freeing(dve.tensor_tensor(GA[:, m, :], gbank(g)[:, 0:T], GA[:, m, :], ALU.mult))
            lo(12)
            for m in range(8):
                g = UNIT0["zb"] + m
                dve.wait_ge(unit_done, g + 1)
                if m >= 2:
                    dve.wait_ge(z_lo, m - 1)
                freeing(dve.tensor_tensor(ZT[:, m % 2, :], gbank(g)[:, 0:T], GB[:, m, :], ALU.mult))
                dve.wait_ge(freed["dve"], FREED[g][1])
                dve.tensor_tensor(ZT[:, m % 2, :], ZT[:, m % 2, :], GA[:, m, :], ALU.add).then_inc(z_done, 1)
            lo(13)
            for m in range(8):
                add_to_h(UNIT0["wo"] + m, m)

            scale_of(D)
            normed(UM, H, "ffn", KB)
            q = small
            n3 = [P, 3]
            LG = q["LG"]
            link(dve.memset(LG[:], 0.0))
            dve.wait_ge(moe_in, 16 * 6)
            g = UNIT0["router"]
            dve.wait_ge(unit_done, g + 1)
            dve.tensor_tensor(LG[:, 0:2, :], gbank(g)[:, 0:72].rearrange("p (t e) -> p t e", t=2),
                              bc(q["RB"][:].unsqueeze(1), [P, 2, 36]), ALU.add)
            freeing(dve.tensor_tensor(LG[0:16, 2, :], gbank(g)[0:16, 72:108], q["RB"][0:16, :], ALU.add))
            dve.wait_ge(freed["dve"], FREED[g][1])
            lg, le = LG[:, :, 0:NG], LG[:, :, NG:NG + NE]

            def first_max(dst, src, n, desc, top_):
                tmp = q["GTMP"] if n == NG else q["ET"]
                link(dve.tensor_reduce(top_[:], src, AX.X, ALU.max))
                link(dve.tensor_tensor(tmp[:], src, bc(top_[:].unsqueeze(2), [P, 3, n]), ALU.is_ge))
                link(dve.tensor_tensor(tmp[:], tmp[:], bc(desc.unsqueeze(1), [P, 3, n]), ALU.mult))
                link(dve.tensor_reduce(q["TM"][:], tmp[:], AX.X, ALU.max))
                link(dve.tensor_tensor(dst[:], bc(desc.unsqueeze(1), [P, 3, n]),
                                       bc(q["TM"][:].unsqueeze(2), [P, 3, n]), ALU.is_equal))

            first_max(q["OG"], lg, NG, q["DESC"][:, 0:NG], q["GM"])
            dve.tensor_tensor(q["GE"][:], lg, bc(q["GM"][:].unsqueeze(2), [P, 3, NG]), ALU.subtract)\
                .then_inc(rt_exp, 1)
            link(dve.tensor_scalar(q["OG"][:], q["OG"][:], -1.0, BIG, ALU.add, ALU.mult))
            for t in range(3):
                ins = dve.tensor_tensor(q["EM"][:, t, :].rearrange("p (g e) -> p g e", g=NG),
                                        le[:, t, :].rearrange("p (g e) -> p g e", g=NG),
                                        bc(q["OG"][:, t, :].unsqueeze(2), [P, NG, EPG]), ALU.add)
            link(ins)
            first_max(q["O1"], q["EM"][:], NE, q["DESC"][:, NG:NG + NE], q["M1"])
            link(dve.scalar_tensor_tensor(out=q["EM"][:], in0=q["O1"][:], scalar=-2 * BIG, in1=q["EM"][:],
                                          op0=ALU.mult, op1=ALU.add))
            first_max(q["O2"], q["EM"][:], NE, q["DESC"][:, NG:NG + NE], q["M2"])
            dve.tensor_tensor(q["MM"][:], q["O1"][:], q["O2"][:], ALU.add).then_inc(rt_m, 1)
            dve.tensor_tensor(q["M2"][:], q["M2"][:], q["M1"][:], ALU.subtract).then_inc(rt_exp, 1)
            dve.wait_ge(rt_gd, 2)
            link(dve.tensor_reduce(q["PG"][:], q["GE"][:], AX.X, ALU.add))
            link(dve.scalar_tensor_tensor(out=q["G1"][:], in0=q["M2"][:], scalar=1.0, in1=q["PG"][:],
                                          op0=ALU.add, op1=ALU.mult))
            link(dve.reciprocal(q["G1"][:], q["G1"][:]))
            dve.tensor_tensor(q["G2"][:], q["G1"][:], q["M2"][:], ALU.mult)
            CC, TA, TF, IO = q["CC"], q["TA"], q["TF"], q["IOTA"]
            g = UNIT0["rank"]
            e = slice(0, NE)
            dve.wait_ge(unit_done, g + 1)
            freeing(dve.tensor_copy(CC[e, 0:1], gbank(g)[e, 0:1]))
            dve.wait_ge(freed["dve"], FREED[g][1])
            link(dve.tensor_scalar(q["N5"][e, :], q["THR"][e, :], CC[e, 0:1], None, ALU.is_lt))
            link(dve.tensor_reduce(CC[e, 1:2], q["N5"][e, :], AX.X, ALU.add))
            dve.tensor_scalar(q["CB"][e, :], ones[e, :], CC[e, 0:1], None, ALU.mult).then_inc(rt_m, 1)
            g += 1
            dve.wait_ge(unit_done, g + 1)
            link(dve.tensor_copy(CC[e, 2:4], gbank(g)[e, 96:98]))
            link(dve.tensor_tensor(CC[e, 4:5], CC[e, 3:4], CC[e, 1:2], ALU.subtract))
            link(dve.scalar_tensor_tensor(out=CC[e, 5:6], in0=CC[e, 4:5], scalar=-float(WIN), in1=CC[e, 2:3],
                                          op0=ALU.mult, op1=ALU.add))
            link(dve.tensor_scalar(CC[e, 5:6], CC[e, 5:6], -float(SLOTS), None, ALU.add))
            link(dve.tensor_scalar(TA[e, ITEMS:2 * ITEMS], IO[e, 0:ITEMS], CC[e, 3:4], None, ALU.is_ge))
            link(dve.scalar_tensor_tensor(out=TF[e, 0:ITEMS], in0=IO[e, 0:ITEMS], scalar=CC[e, 4:5],
                                          in1=TA[e, ITEMS:2 * ITEMS], op0=ALU.is_ge, op1=ALU.subtract))
            link(dve.tensor_scalar(TF[e, ITEMS:2 * ITEMS], IO[e, 0:ITEMS], float(WIN), CC[e, 5:6],
                                   ALU.mult, ALU.add))
            link(dve.tensor_tensor(TA[e, 0:ITEMS], TF[e, ITEMS:2 * ITEMS], TF[e, 0:ITEMS], ALU.mult))
            dve.tensor_copy(TA[e, 80:81], CC[e, 1:2]).then_inc(rt_m, 1)
            dst = gbank(g)[:, 0:3 * NE].rearrange("p (t e) -> p t e", t=3)
            for o, d in (("O1", "DST1"), ("O2", "DST2")):
                link(dve.tensor_tensor(q["ET"][:], dst, q[o][:], ALU.mult))
                link(dve.tensor_reduce(q[d][:], q["ET"][:], AX.X, ALU.add))
            freeing(dve.tensor_copy(q["GTMP"][:, 0, 0:1], gbank(g)[:, 0:1]))
            g += 1
            dve.wait_ge(unit_done, g + 1)
            dve.tensor_scalar(TF[0:1, 0:ITEMS], gbank(g)[0:1, 0:ITEMS], float(SLOTS), None, ALU.add)
            dve.tensor_scalar(TF[0:1, ITEMS:2 * ITEMS], gbank(g)[0:1, ITEMS:2 * ITEMS], float(NE - 1), None,
                              ALU.min)
            link(dve.tensor_copy(CC[0:1, 6:7], gbank(g)[0:1, 80:81]))
            pairs = TA[0:1, 0:ITEMS // 2]
            freeing(dve.tensor_scalar(pairs, IO[0:1, 0:ITEMS:2], CC[0:1, 6:7], None, ALU.is_lt))
            dve.wait_ge(freed["dve"], FREED[g][1])
            link(dve.tensor_reduce(TF[0:1, 80:81], pairs, AX.X, ALU.add))
            link(dve.tensor_scalar(TF[0:1, 81:82], TF[0:1, 80:81], 2.0, -2.0, ALU.mult, ALU.add))
            dve.tensor_copy(TBL[0:1, 0:82], TF[0:1, 0:82]).then_inc(tbl_done, 1)
            for t in range(3):
                link(dve.tensor_scalar(PERM[:, t, :], IO[:], q["DST1"][:, t:t + 1], None, ALU.is_equal))
                ins = dve.scalar_tensor_tensor(out=PERM[:, t, :], in0=IO[:], scalar=q["DST2"][:, t:t + 1],
                                               in1=PERM[:, t, :], op0=ALU.is_equal, op1=ALU.add)
            ins.then_inc(perm_done, 1)
            for t in range(3):
                dve.tensor_scalar(G[:, t, :], IO[:, 0:SLOTS], q["DST1"][:, t:t + 1], q["G1"][:, t:t + 1],
                                  ALU.is_equal, ALU.mult)
            dve.wait_ge(unit_done, UNIT0["disp"] + 16)
            for t in range(3):
                link(dve.tensor_scalar(PERM[:, t, 0:SLOTS], IO[:, 0:SLOTS], q["DST2"][:, t:t + 1],
                                       q["G2"][:, t:t + 1], ALU.is_equal, ALU.mult))
                dve.tensor_tensor(G[:, t, :], G[:, t, :], PERM[:, t, 0:SLOTS], ALU.add).then_inc(g_done, 1)
            items = dve.value_load(TBL[0:1, 80:81], min_val=1, max_val=ITEMS // 2) * 2
            dve.nop().then_inc(xhid_done, 2)
            with dve.Fori(0, items, 2) as i:
                for s in range(2):
                    dve.wait_ge(xs_done, i + (s + 1))
                    dve.wait_ge(xy_done, i + (s + 1))
                    dve.tensor_tensor(SG[s][:], PS[:, s, 0:4 * WIN].rearrange("p (m w) -> p m w", m=4),
                                      SG[s][:], ALU.mult).then_inc(xt_done, 1)
                    dve.wait_ge(xt_done, i + (s + 1))
                    dve.tensor_tensor(HID[s][:], PS[:, 2 + s, 0:4 * WIN].rearrange("p (m w) -> p m w", m=4),
                                      SG[s][:], ALU.mult).then_inc(xhid_done, 1)
            for st in range(5):
                m = min(P, SLOTS - P * st)
                g = UNIT0["gt"] + st
                dve.wait_ge(unit_done, g + 1)
                freeing(dve.tensor_copy(GT[0:m, st, :], gbank(g)[0:m, 0:T]))
            for m in range(8):
                add_to_h(UNIT0["comb"] + m, m)
            scale_of(D)
            lo(N_FIRST)
            normed(H, H, "final", KB, META)
            scale_of(D)
            dve.wait_ge(meta2_in, 16)
            normed(SQ3, H, "mix0", KB)
            lo(N_FIRST + 1)
            n = FIRST_SLAB["ret_qk"]
            for h in range(RH):
                for p in range(2):
                    g = UNIT0["rqk"] + 4 * h + 2 * p
                    b = g % 4
                    dve.wait_ge(unit_done, g + 2)
                    pair = PS[:, b:b + 2, 0:T]
                    dst_ = (RQ, RK)[p]
                    link(dve.tensor_tensor(R1[:], pair, bc(cosw[:].unsqueeze(1), [P, 2, T]), ALU.mult))
                    freeing(dve.tensor_tensor(R2[:], pair, bc(sinw[:].unsqueeze(1), [P, 2, T]), ALU.mult), 2)
                    dve.wait_ge(freed["dve"], FREED[g + 1][1])
                    dve.tensor_tensor(dst_[:, 2 * h, :], R1[:, 0, :], R2[:, 1, :], ALU.subtract)
                    dve.tensor_tensor(dst_[:, 2 * h + 1, :], R2[:, 0, :], R1[:, 1, :], ALU.add)\
                        .then_inc(rqk_done, 1)
                    dve.wait_ge(rqk_done, 2 * h + p + 1)
                lo(n + h + 2)
            for h in range(RH):
                lo(n + RH + h + 2)
            for s in range(4):
                for u in range(4):
                    j = 4 * s + u
                    g = UNIT0["gate"] + j
                    dve.wait_ge(gsig_done, j + 1)
                    freeing(dve.tensor_tensor(GATE[:, j, :], gbank(g)[:, 0:T], GSIG[j % 2][:], ALU.mult))
                lo(n + 2 * RH + s + 2)

            def weigh(h):
                dve.wait_ge(dec_in[h % 2], 16 * (h // 2 + 1))
                if h >= 2:
                    dve.wait_ge(unit_done, UNIT0["ro"] + 4 * (h - 1))
                for j, (k0, mk) in enumerate(KEY_COLS):
                    i = 3 * h + j
                    dve.wait_ge(st_mm, i + 1)
                    dve.tensor_tensor(ST[h % 2][0:mk, j, :], sbank(i % 3)[0:mk, 0:T], DEC[h % 2][0:mk, j, :],
                                      ALU.mult).then_inc(st_done, 1)

            weigh(0)
            for h in range(RH):
                if h + 1 < RH:
                    weigh(h + 1)
                dve.wait_ge(ro_sum, h + 1)
                dve.tensor_scalar(GMU[:], sbank(3)[:, 0:T], 1.0 / RV, None, ALU.mult).then_inc(gmu_done, 1)
                dve.wait_ge(gmu_done, h + 1)
                dve.tensor_tensor(RO[:], RO[:], bc(GMU[:].unsqueeze(1), [P, 4, T]), ALU.subtract)\
                    .then_inc(oc_done, 1)
                dve.wait_ge(gv_mm, h + 1)
                dve.tensor_scalar(GRS[:], sbank(3)[:, 0:T], 1.0 / RV, GN_EPS, ALU.mult, ALU.add).then_inc(gvar, 1)
                dve.wait_ge(gstd, h + 1)
                dve.wait_ge(oc_done, h + 1)
                link(dve.reciprocal(GRS[:], GRS[:]))
                link(dve.tensor_tensor(RO[:], RO[:], bc(GRS[:].unsqueeze(1), [P, 4, T]), ALU.mult))
                for v in range(4):
                    c = GAINS["gn"] + 4 * h + v
                    ins = dve.scalar_tensor_tensor(out=RSQ[:, v, :], in0=RO[:, v, :], scalar=gains[:, c:c + 1],
                                                   in1=GATE[:, 4 * h + v, :], op0=ALU.mult, op1=ALU.mult)
                ins.then_inc(rn_done, 1)
            n = FIRST_SLAB["ret_o"]
            for s in range(4):
                for u in range(2):
                    add_to_h(UNIT0["rwo"] + 2 * s + u, 2 * s + u)
                lo(n + s + 2)

            def ffn(layer, gain):
                scale_of(D)
                normed(SQ2, H, gain, KB)
                n = FIRST_SLAB[f"up{layer}"]
                f0 = FB * layer
                for p in range(FB):
                    g = UNIT0[f"up{layer}"] + 2 * p
                    dve.wait_ge(f_sig, f0 + p + 1)
                    freeing(dve.tensor_tensor(FT[p % 2][:], gbank(g)[:, 0:T], FS[p % 2][:], ALU.mult))
                    dve.wait_ge(freed["dve"], FREED[g][1])
                    dve.wait_ge(unit_done, g + 2)
                    if p >= 2:
                        dve.wait_ge(f_lo, f0 + p - 1)
                    freeing(dve.tensor_tensor(FU[p % 2][:], gbank(g + 1)[:, 0:T], FT[p % 2][:], ALU.mult))
                    if p % 2 and n + p // 2 + 2 < len(SLABS):
                        lo(n + p // 2 + 2)
                n = FIRST_SLAB[f"down{layer}"]
                for s in range(8):
                    add_to_h(UNIT0[f"down{layer}"] + s, s)
                    if n + s + 2 < len(SLABS):
                        lo(n + s + 2)

            ffn(0, "ffn0")
            scale_of(D)
            normed(SQM, H, "kv", KB)
            n = FIRST_SLAB["kv_c"]
            lo(n + 2)
            dve.wait_ge(nlo_done, 32)
            normed(SQM, H, "mix1", KB)
            scale_of(4 * P)
            normed(SQQ, CKRAW, "kva", 4)
            lo(n + 3)
            lo(n + 4)
            scale_of(6 * P)
            normed(SQQ, CRAW, "qa", 6)
            lo(n + 5)
            lo(n + 6)
            for s in range(3):
                lo(n + 7 + s)
            dve.wait_ge(mla_in, 32)
            for j in range(5):
                rotated(10 + j, QR[:, j, :] if j < 4 else KR2[:], ROT_M)
            dve.wait_ge(mla_in, 48)
            attention(NEG2, PR2, (P + HD) ** -0.5,
                      lambda h: split_out(UNIT0[f"om{h}"], slice(0, P), OMH[:, h, :], OML[:, h, :]))
            n = FIRST_SLAB["mla_o"]
            for s in range(2):
                for u in range(4):
                    add_to_h(UNIT0["mo"] + 4 * s + u, 4 * s + u)
                lo(n + s + 2)
            ffn(1, "ffn1")
            scale_of(D)
            normed(OUT, H, "final2", KB)

        @block.gpsimd
        def _(pool):
            low_count = [0]

            def lows(dst, hi_, src, nb):
                for k in range(nb):
                    low_count[0] += 1
                    pool.wait_ge(nhi_done, low_count[0])
                    pool.tensor_tensor(dst[:, k, :], src[:, k, :], hi_[:, k, :].bitcast(F32), ALU.subtract)\
                        .then_inc(nlo_done, 1)

            pool.memset(KA[:, :, T:], 0.0).then_inc(ka_zero, 1)
            lows(UL, UH, SQ, KB)
            for m in range(8):
                pool.wait_ge(z_hi, m + 1)
                pool.tensor_tensor(ZL[:, m, :], ZT[:, m % 2, :], ZH[:, m, :].bitcast(F32), ALU.subtract)\
                    .then_inc(z_lo, 1)
            pool.wait_ge(freed["act"], FREED[UNIT0["disp"] + 15][1])
            pool.wait_ge(tbl_done, 1)
            pool.wait_ge(g_done, 3)
            items = pool.value_load(TBL[0:1, 80:81], min_val=1, max_val=ITEMS // 2) * 2
            with pool.Fori(0, items, 2) as i:
                for s in range(2):
                    at_ = pool.value_load(TBL[0:1, bass.ds(i + s, 1)], min_val=0, max_val=SLOTS)
                    pool.wait_ge(xh_done, i + (s + 1))
                    pool.tensor_copy(XW[s][:], XS[:, :, bass.ds(at_, WIN)]).then_inc(xw_done, 1)
            lows(UL, UH, SQ3, KB)
            for h in range(RH):
                pool.wait_ge(rhi_done, h + 1)
                pool.tensor_tensor(RLO[h][:], RSQ[:], RHI[:, 4 * h:4 * h + 4, :].bitcast(F32), ALU.subtract)\
                    .then_inc(rlo_done, 1)

            def ffn(layer):
                lows(UL, UH, SQ2, KB)
                for p in range(FB):
                    pool.wait_ge(f_hi, FB * layer + p + 1)
                    pool.tensor_tensor(TL[:, p, :], FU[p % 2][:], TH[:, p, :].bitcast(F32), ALU.subtract)\
                        .then_inc(f_lo, 1)

            ffn(0)
            lows(UL, UH, SQM, KB)
            lows(UL, UH, SQM, KB)
            lows(CKL, CKH, SQQ, 4)
            lows(CQL, CQH, SQQ, 6)
            ffn(1)


def constants():
    f4 = np.float32
    pos = np.arange(T)
    chunk = np.where(pos < META, 0, 1 + (pos - META) // CHUNK)
    c = {}
    c["c_ident"] = np.eye(P, dtype=f4)
    c["c_ones"] = np.ones((P, P), f4)
    i, j = np.indices((P, P))
    c["c_negu"] = np.where(i >= j, -1.0, 0.0).astype(f4)
    c["c_negones"] = -np.ones((P, P), f4)
    c["m_utri"] = (i < j).astype(f4)

    def swap(period, half):
        r = np.zeros((P, P), f4)
        for m in range(P):
            w = m % period
            if w < half:
                r[m + half, m] = -1.0
            elif w < 2 * half:
                r[m - half, m] = 1.0
        return r

    def angles(inv, rows):
        ang = pos.astype(f4)[None, :] * inv.astype(f4)[np.maximum(rows, 0)][:, None]
        cos = np.where(rows[:, None] >= 0, np.cos(ang.astype(np.float64)), 1.0).astype(f4)
        sin = np.where(rows[:, None] >= 0, np.sin(ang.astype(np.float64)), 0.0).astype(f4)
        return cos, sin

    r = np.arange(P)
    c["rot_dsa"], c["rot_mla"] = swap(HD, 8), swap(HD, 32)
    inv = f4(500000.0) ** (-np.arange(8, dtype=f4) / f4(8))
    c["cos_dsa"], c["sin_dsa"] = angles(inv, np.where(r % HD < 16, r % 8, -1))
    inv = f4(1.0) / (f4(10000.0) ** (np.arange(0, 256, 2, dtype=f4) / f4(256)))
    c["cos_ret"], c["sin_ret"] = angles(inv, r)
    inv = f4(1.0) / (f4(10000.0) ** (np.arange(0, 64, 2, dtype=f4) / f4(64)))
    c["cos_mla"], c["sin_mla"] = angles(inv, r % 32)
    m = np.zeros((P, SBW), f4)
    for (col, q, w), (k0, mk) in zip(SB_COLS, KEY_TILES):
        m[0:mk, col:col + w] = (k0 + np.arange(mk))[:, None] < (q + np.arange(w))[None, :]
    c["sb_mask"] = m
    adm = np.zeros((P, 3, T), f4)
    for t, (q0, mq) in enumerate(QRY_TILES):
        adm[0:mq, t, :] = chunk[None, :] <= chunk[q0:q0 + mq, None]
    c["adm"] = adm
    c["bound"] = np.where(adm > 0, 3e38, -3e38).astype(f4)
    c["neg"] = np.where(adm > 0, 0.0, -BIG).astype(f4)
    dec = np.zeros((RH, P, 3, T), f4)
    for h in range(RH):
        lg = np.log1p(-(2.0 ** (-5.0 - h)))
        for t, (k0, mk) in enumerate(KEY_TILES):
            k = (k0 + np.arange(mk))[:, None]
            dec[h, 0:mk, t, :] = np.where(chunk[k] <= chunk[None, :], np.exp(lg * np.abs(k - pos[None, :])), 0) / 16.0
    c["decay"] = dec
    c["m_IOTA"] = np.broadcast_to(np.arange(XCOLS, dtype=f4), (P, XCOLS)).copy()
    c["m_THR"] = np.broadcast_to(WIN * np.arange(5, dtype=f4), (P, 5)).copy()
    c["m_DESC"] = np.broadcast_to(np.concatenate([np.arange(NG, 0, -1), np.arange(NE, 0, -1)]).astype(f4),
                                  (P, NG + NE)).copy()
    return c


def units(w):
    k, m = w.shape
    return w.reshape(k // P, P, m // P, P).transpose(1, 2, 0, 3)


def cut(w, n):
    p, u = w.shape[:2]
    return w.reshape(p, n, u // n, -1).transpose(1, 0, 2, 3).reshape(n, p, -1)


def layout(x):
    np_ = {k: np.asarray(v) for k, v in x.items()}
    d = {}
    fm = lambda t: np.ascontiguousarray(t.T.reshape(KB, P, -1).transpose(1, 0, 2))
    d["h_first"] = fm(np.concatenate([np_["meta_tokens"], np_["x"][0]], axis=0))
    d["meta2"] = fm(np_["meta_2"])
    col = lambda g: g.reshape(-1, P).T
    d["gains"] = np.concatenate([col(g) for g in (
        np_["norm_mix_g"][0], np_["norm_ffn_g"][0], np_["norm_final_g"], np_["norm_mix_g_2"][0],
        np_["norm_ffn_g_2"][0], np_["mla_norm_kv_g_2"], np_["norm_mix_g_2"][1], np_["mla_kv_a_norm_g_2"],
        np_["mla_q_a_norm_g_2"][0], np_["norm_ffn_g_2"][1], np_["final_g_2"], np_["ret_gn_g_2"][0])], axis=1)
    w = np_["w_in"][0]
    parts = np.split(w, np.cumsum([512, 512, 512, 512, LAT, 16, 512, HD, HEADS, D, D])[:-1], axis=1)
    qa, ka, va, qb, ckv, kr, qi, ki, wi, ga, gb = parts
    zeros = lambda n: np.zeros((D, n), w.dtype)
    slab_kmajor = lambda v: v.reshape(-1, P, v.shape[1]).transpose(1, 0, 2).reshape(1, P, -1)
    d["w_in_qa"], d["w_in_ka"] = cut(units(qa), 1), cut(units(ka), 1)
    d["w_in_va"] = slab_kmajor(va)
    d["w_in_qb"], d["w_in_qi"] = cut(units(qb), 1), cut(units(qi), 1)
    misc = np.concatenate([ckv, kr, zeros(48), kr, zeros(48), ki, ki, wi, zeros(P - HEADS)], axis=1)
    d["w_in_misc"] = cut(units(misc), 1)
    d["w_in_ga"], d["w_in_gb"] = cut(units(ga), 2), cut(units(gb), 2)
    d["w_up_a"], d["w_up_b"] = cut(units(np_["w_up_a"][0]), 1), cut(units(np_["w_up_b"][0]), 1)
    d["w_o"] = cut(units(np_["w_o"][0]), 2)
    uk = np_["w_uk"][0].transpose(0, 2, 1)
    uk = np.concatenate([np.zeros((HEADS, 16, LAT), uk.dtype), uk], axis=1)
    d["w_uk"] = uk.reshape(4, P, LAT).transpose(1, 0, 2)
    d["w_uv"] = np_["w_uv"][0].transpose(1, 0, 2)
    d["m_RB"] = np.broadcast_to(np.concatenate([np_["b_group"][0], np_["b_router"][0]]), (P, NG + NE))
    d["m_WRT"] = np.concatenate([np_["w_group"][0], np_["w_router"][0]], axis=1)\
        .reshape(KB, P, NG + NE).transpose(1, 0, 2)
    expert = lambda v: v.reshape(NE, v.shape[1] // P, P, v.shape[2] // P, P).transpose(0, 2, 3, 1, 4)\
        .reshape(NE, P, -1)
    d["w1"], d["w3"], d["w2"] = (expert(np_[k][0]) for k in ("w1", "w3", "w2"))
    w = np_["ret_w_in_2"][0]
    q, k = w[:, 0:D].reshape(D, RH, 256), w[:, D:2 * D].reshape(D, RH, 256)
    d["ret_qk"] = cut(units(np.concatenate([q, k], axis=2).reshape(D, 2 * D)), 4)
    d["ret_v"] = np.concatenate([slab_kmajor(w[:, 2 * D + RV * h:2 * D + RV * (h + 1)]) for h in range(RH)])
    d["ret_gate"] = cut(units(w[:, 4 * D:6 * D]), 4)
    d["ret_o"] = cut(units(np_["ret_w_o_2"][0]), 4)
    for layer in range(2):
        w1, w3 = units(np_["ffn_w1_2"][layer]), units(np_["ffn_w3_2"][layer])
        d[f"up{layer}"] = cut(np.stack([w1, w3], axis=2).reshape(P, 2 * FB, KB, P), 11)
        d[f"down{layer}"] = cut(units(np_["ffn_w2_2"][layer]), 8)
    w = np_["mla_w_kv_a_2"]
    d["kv_c"] = cut(units(w[:, 0:512]), 1)
    qa = np_["mla_w_q_a_2"][0]
    d["kr_qa"] = cut(units(np.concatenate([w[:, 512:], w[:, 512:], qa[:, 0:3 * P]], axis=1)), 1)
    d["qa_rest"] = cut(units(qa[:, 3 * P:]), 1)
    w = np_["mla_w_kv_b_2"].reshape(512, HEADS, 2 * P)
    d["kv_k"] = cut(units(w[:, :, 0:P].reshape(512, D)), 1)
    d["kv_v"] = slab_kmajor(w[:, :, P:].reshape(512, D))
    w = np_["mla_w_q_b_2"][0].reshape(768, HEADS, P + HD)
    d["q_b"] = cut(units(np.concatenate([w[:, :, 0:P].reshape(768, D), w[:, :, P:].reshape(768, 512)], axis=1)), 3)
    d["mla_o"] = cut(units(np_["mla_w_o_2"][0]), 2)
    d.update(constants())
    return {k: np.ascontiguousarray(v) for k, v in d.items()}


def kernel(**inputs):
    import concourse.bacc as bacc
    from concourse.bass_utils import run_bass_kernel_spmd

    arrays = layout(inputs)
    nc = bacc.Bacc("TRN2", target_bir_lowering=False, num_devices=1)
    a = {k: nc.dram_tensor("in_" + k, v.shape, mybir.dt.from_np(v.dtype), kind="ExternalInput").ap()
         for k, v in arrays.items()}
    out = nc.dram_tensor("out_0", (P, KB, SEQ), F32, kind="ExternalOutput").ap()
    program(nc, a, out)
    r = run_bass_kernel_spmd(nc, [{"in_" + k: v for k, v in arrays.items()}], core_ids=[0])
    y = r.results[0]["out_0"]
    return y.transpose(2, 1, 0).reshape(1, SEQ, D)
```

```python
from contextlib import ExitStack

import numpy as np

import concourse.bass as bass
from concourse import mybir

F32 = mybir.dt.float32
F32R = mybir.dt.float32r
I32 = mybir.dt.int32
ALU = mybir.AluOpType
ACT = mybir.ActivationFunctionType
AX = mybir.AxisListType

P = 128
D = 1024
META = 16
SEQ = 256
T = META + SEQ
CHUNK = 64
KB = D // P
HEADS = 8
HD = 64
TOPK = min(256, SEQ // 4)
LAT = 128
NG, EPG = 4, 8
NE = NG * EPG
DE = 512
TOP_E = 2
SLOTS = T * TOP_E
WIN = 96
ITEMS = NE + 8
XCOLS = SLOTS + WIN
RH = 4
RV = 512
FB = 22
EPS = 1e-6
GN_EPS = 1e-5
BIG = 1e30
KEY_TILES = [(0, 128), (128, 112), (240, 32)]
KEY_COLS = [(0, 128), (128, 128), (240, 32)]
QRY_TILES = [(0, 128), (128, 128), (256, 16)]
SB_COLS = [(0, 0, 272), (272, 128, 144), (416, 240, 32)]
SBW = 448

SLABS = ([("w_in_qa", 32), ("w_in_ka", 32), ("w_in_va", 32), ("w_in_qb", 32), ("w_in_misc", 32),
          ("w_in_qi", 32), ("w_in_ga", 32), ("w_in_ga", 32), ("w_in_gb", 32), ("w_in_gb", 32),
          ("w_up_a", 32), ("w_up_b", 32), ("w_o", 32), ("w_o", 32)]
         + [("ret_qk", 32)] * 4 + [("ret_v", 32)] * 4 + [("ret_gate", 32)] * 4 + [("ret_o", 32)] * 4
         + [("up0", 32)] * 11 + [("down0", FB)] * 8
         + [("kv_c", 32), ("kr_qa", 32), ("qa_rest", 24), ("kv_k", 32), ("kv_v", 32)]
         + [("q_b", 24)] * 3 + [("mla_o", 32)] * 2
         + [("up1", 32)] * 11 + [("down1", FB)] * 8)
FIRST_SLAB = {}
for _n, (_name, _b) in enumerate(SLABS):
    FIRST_SLAB.setdefault(_name, _n)
N_FIRST = FIRST_SLAB["ret_qk"]

UNITS = [("qa", 4, 1, "act"), ("ka", 4, 1, "act"), ("va", 3, 1, "act"), ("qb", 4, 1, "act"),
         ("misc", 4, 1, "act"), ("qi", 4, 1, "act"), ("ga", 8, 2, "act"), ("gb", 8, 2, "act"),
         ("qlat", 8, 0, "act")]
UNITS += [u for h in range(HEADS) for u in ((f"olat{h}", 1, 0, "act"), (f"yb{h}", 1, 0, "dve"))]
UNITS += [("za", 8, 1, "dve"), ("zb", 8, 1, "dve"), ("wo", 8, 2, "dve"),
          ("router", 1, 0, "dve"), ("utok", 6, 0, "act"), ("rank", 3, 0, "dve"), ("disp", 16, 0, "act"),
          ("yslot", 10, 0, "act"), ("gt", 5, 0, "dve"), ("comb", 8, 0, "dve"),
          ("rqk", 16, 4, "dve"), ("rv", 12, 4, "act"), ("gate", 16, 4, "dve"), ("ro", 16, 0, "act"),
          ("rwo", 8, 4, "dve"), ("up0", 44, 11, "dve"), ("down0", 8, 8, "dve"),
          ("kvc", 4, 1, "act"), ("krq", 4, 1, "act"), ("qar", 3, 1, "act"), ("kn", 8, 1, "act"),
          ("vm", 6, 1, "act"), ("qn", 8, 2, "act"), ("qr", 4, 1, "act")]
UNITS += [(f"om{h}", 1, 0, "dve") for h in range(HEADS)]
UNITS += [("mo", 8, 2, "dve"), ("up1", 44, 11, "dve"), ("down1", 8, 8, "dve")]
UNIT0 = {}
FREED = []
SLAB_UNITS = []
_count = {"act": 0, "dve": 0}
for _name, _n, _s, _e in UNITS:
    UNIT0[_name] = len(FREED)
    for _i in range(_n):
        _count[_e] += 1
        FREED.append((_e, _count[_e]))
    for _j in range(_s):
        SLAB_UNITS.append(UNIT0[_name] + _n * (_j + 1) // _s)
assert len(SLAB_UNITS) == len(SLABS)

ROUNDS = (0, 0, 4, 4, 4, 4, 4, 4)
assert sum(ROUNDS) == 3 * TOPK // 8

GAINS = {}
_at = 0
for _name, _n in [("mix", 8), ("ffn", 8), ("final", 8), ("mix0", 8), ("ffn0", 8), ("kv", 8), ("mix1", 8),
                  ("kva", 4), ("qa", 6), ("ffn1", 8), ("final2", 8), ("gn", 16)]:
    GAINS[_name] = _at
    _at += _n
N_GAINS = _at


def program(nc, a, out):
    base0 = 16512
    top = 229368

    def place(name, shape, offset, dt=F32):
        return nc.alloc_sbuf_tensor_at(name, [P] + shape, dt, offset=offset)

    RAW = [place(f"raw{i}", [4096], base0 + 16384 * i) for i in range(3)]
    WH = [place(f"wh{i}", [4096], base0 + 49152 + 16384 * i, F32R) for i in range(2)]
    WL = [place(f"wl{i}", [4096], base0 + 81920 + 16384 * i, F32R) for i in range(2)]
    XPT = [place(f"expert_w{i}", [4096], base0 + 16384 * i) for i in range(6)]
    at = base0 + 114688
    fixed = {}
    for name, shape in [("H", [KB, T]), ("ident", [P]), ("ones", [P]), ("rot", [P]), ("cosw", [T]), ("sinw", [T]), ("gains", [N_GAINS]), ("rs", [T])]:
        fixed[name] = place(name, shape, at)
        at += -(-4 * int(np.prod(shape)) // 32) * 32
    H, ident, ones, rot, cosw, sinw, gains, rs = fixed.values()
    R0 = at

    def region(name, shape, off, dt=F32):
        assert R0 + off + 4 * int(np.prod(shape)) <= top, (name, R0 + off + 4 * int(np.prod(shape)) - top)
        return place(name, shape, R0 + off, dt)

    B = 4 * T
    UH = region("UH", [KB, T], 0, F32R)
    UL = region("UL", [KB, T], 8 * B, F32R)
    QA = [region("QA_even", [4, T], 17408), region("QA_odd", [4, T], 74880)]
    KA = region("KA", [4, 368], 21760)
    VA = region("VA", [3, 512], 27904)
    QB = region("QB", [4, T], 34048)
    QI = region("QI", [4, T], 38400)
    KI = region("KI", [T], 42752)
    CKV = region("CKV", [T], 43840)
    KR = region("KR", [T], 44928)
    WIT = region("WIT", [T], 46016)
    CKVT = region("CKVT", [3, P], 47104)
    WI = region("WI", [3, 8], 48640)
    GA = region("GA", [KB, T], 48768)
    GB = region("GB", [KB, T], 57472)
    SQ = region("SQ", [KB, T], 48768)
    YAH = region("YAH", [4, T], 66176, F32R)
    YAL = region("YAL", [4, T], 70528, F32R)
    YBH = region("YBH", [4, T], 74880, F32R)
    YBL = region("YBL", [4, T], 79232, F32R)
    ROT_T = region("ROT_T", [2, T], 66176)
    SBM = region("SBM", [SBW], 79232)
    negu = region("negu", [P], 81024)
    negones = region("negones", [P], 81536)
    SB_L = [place(f"SB_L{i}", [SBW], base0 + 32768 + 0 + 7168 * i) for i in range(2)]
    SB_SP = [place(f"SB_SP{i}", [SBW], base0 + 32768 + 1792 + 7168 * i) for i in range(2)]
    SB_SPM = [place(f"SB_SPM{i}", [SBW], base0 + 32768 + 3584 + 7168 * i) for i in range(2)]
    SB_A = [place(f"SB_A{i}", [SBW], base0 + 32768 + 5376 + 7168 * i) for i in range(2)]
    QLAT = region("QLAT", [8, T], 0)
    NEG = place("NEG", [3, T], base0 + 65536)
    SCORE = place("SCORE", [3, T], base0 + 65536 + 3 * B)
    PR = [region(f"PR{i}", [T], 15232 + B * i) for i in range(2)]
    ADM = place("ADM", [3, T], base0 + 65536 + 6 * B)
    BND = place("BND", [3, T], base0 + 65536 + 9 * B)
    RL = [place(f"RL{i}", [T], base0 + 98304 + B * i) for i in range(4)]
    PT = [region(f"PT{i}", [3, T], 26112 + 3 * B * i) for i in range(2)]
    OL = region("OL", [T], 32640)
    WUK = region("WUK", [4, P], 8704)
    WUV = place("WUV", [8, HD], base0 + 98304 + 4 * B)
    SMALL = region("SMALL", [96], 83584)
    MAX8 = region("MAX8", [8], 83968)
    ZH = region("ZH", [KB, T], 0, F32R)
    ZL = region("ZL", [KB, T], 8 * B, F32R)
    ZT = region("ZT", [2, T], 17408)
    UM = region("UM", [KB, T], 0)
    G = region("G", [3, SLOTS], 8704)
    UTH = region("UTH", [3, D], 15232, F32R)
    UTL = region("UTL", [3, D], 55680, F32R)
    UTOK = region("UTOK", [3, D], 35200)
    PERM = region("PERM", [3, XCOLS], 27520, F32R)
    PERMF = region("PERMF", [3, XCOLS], 27520)
    XS = region("XS", [KB, XCOLS], 35200)
    YS = region("YS", [KB, XCOLS], 55680)
    YSLOT = region("YSLOT", [5, D], 15232)
    GT = region("GT", [5, T], 36864)
    ro = 76160
    small = {}
    for name, shape in [("LG", [3, 36]), ("RB", [36]), ("DESC", [36]), ("utri", [P]),
                        ("THR", [5]), ("GM", [3]), ("GE", [3, 4]), ("OG", [3, 4]), ("GTMP", [3, 4]),
                        ("PG", [3]), ("EM", [3, 32]), ("O1", [3, 32]), ("O2", [3, 32]), ("ET", [3, 32]),
                        ("M1", [3]), ("M2", [3]), ("TM", [3]), ("G1", [3]), ("G2", [3]), ("MM", [3, 32]),
                        ("DST1", [3]), ("DST2", [3]), ("CC", [8]), ("CB", [P]), ("N5", [5]),
                        ("TA", [96]), ("TF", [96])]:
        small[name] = region(name, shape, ro)
        ro += -(-4 * int(np.prod(shape)) // 32) * 32
    small["IOTA"] = region("IOTA", [XCOLS], 55680 + 12288)
    small["WRT"] = region("WRT", [KB, 36], 55680 + 12288 + 4 * XCOLS)
    utri = small["utri"]
    TBL = region("TBL", [96], ro, I32)
    ro += 384
    XW = [region(f"XW{i}", [KB, WIN], 15232 + 32 * WIN * i) for i in range(2)]
    SG = [region(f"SG{i}", [4, WIN], 15232 + 64 * WIN + 16 * WIN * i) for i in range(2)]
    HID = [region(f"HID{i}", [4, WIN], 15232 + 96 * WIN + 16 * WIN * i) for i in range(2)]
    UMT = region("UMT", [KB, T], 55680)
    RQ = region("RQ", [8, T], 17408)
    RK = region("RK", [8, T], 26112)
    RVV = [region(f"RV{h}", [3, RV], 34816 + 6144 * h) for h in range(RH)]
    GATE = region("GATE", [16, T], 59392)
    DEC = [region(f"DEC{i}", [3, T], 76800 + 3264 * i) for i in range(2)]
    R1 = region("R1", [2, T], 76800)
    R2 = region("R2", [2, T], 78976)
    GSIG = [region(f"GSIG{i}", [T], 81152 + B * i) for i in range(2)]
    ST = [region(f"ST{i}", [3, T], 3264 * i) for i in range(2)]
    RO = [region("RO_even", [4, T], 6528), region("RO_odd", [4, T], 17408)]
    RSQ = [region("RSQ_even", [4, T], 10880), region("RSQ_odd", [4, T], 26112)]
    GRS = region("GRS", [T], 15232)
    GMU = region("GMU", [T], 16320)
    RHI = region("RHI", [16, T], 59392, F32R)
    RLO = [region(f"RLO{h}", [4, T], 34816 + 6144 * h, F32R) for h in range(RH)]
    SQ2 = region("SQ2", [KB, T], 65280)
    SQR = region("SQR", [KB, T], 17408)
    SQ3 = region("SQ3", [KB, T], 65280 - 5888)
    TH = region("TH", [FB, T], 17408, F32R)
    TL = region("TL", [FB, T], 41344, F32R)
    FS = [region(f"FS{i}", [T], 65280 + B * i) for i in range(2)]
    FT = [region(f"FT{i}", [T], 67456 + B * i) for i in range(2)]
    FU = [region(f"FU{i}", [T], 69632 + B * i) for i in range(2)]
    QN = region("QN", [8, T], 17408)
    KN = region("KN", [8, T], 26112)
    QR = region("QR", [4, T], 34816)
    KR2 = region("KR2", [T], 39168)
    VM = region("VM", [3, D], 40256)
    CKH = region("CKH", [4, T], 52544, F32R)
    CKL = region("CKL", [4, T], 56896, F32R)
    CQH = region("CQH", [6, T], 61248, F32R)
    CQL = region("CQL", [6, T], 67776, F32R)
    CRAW = region("CRAW", [6, T], 74304)
    CKRAW = region("CKRAW", [4, T], 61248)
    SQM = region("SQM", [KB, T], 74304)
    U2H = region("U2H", [KB, T], 17408, F32R)
    U2L = region("U2L", [KB, T], 26112, F32R)
    SQQ = region("SQQ", [KB, T], 40256)
    ROT_M = region("ROT_M", [2, T], 80832)
    OMH = region("OMH", [8, T], 0, F32R)
    OML = region("OML", [8, T], 8704, F32R)
    NEG2 = region("NEG2", [3, T], 52544)
    PR2 = [region(f"PR2{i}", [T], 55808 + B * i) for i in range(2)]
    PT2 = [region(f"PT2{i}", [3, T], 57984 + 3 * B * i) for i in range(2)]
    OUT = region("OUT", [KB, T], 17408)

    with ExitStack() as ctx:
        def sem(name):
            return ctx.enter_context(nc.semaphore(name))

        PS = ctx.enter_context(nc.psum_tensor("PS", [P, 8, 512], F32))
        raw_full = [sem(f"raw_full{i}") for i in range(3)]
        lo_first = sem("lo_first")
        hi_done = sem("hi_done")
        lo_done = sem("lo_done")
        unit_done = sem("unit_done")
        freed = {"act": sem("freed_act"), "dve": sem("freed_dve")}
        act_step, dve_step, pool_step = sem("act_step"), sem("dve_step"), sem("pool_step")
        const_in, norm_in, h_in, h_in2, sb_in, dsa_in, moe_in, tab2_in, meta2_in, mla_in = (
            sem(x) for x in ("const_in", "norm_in", "h_in", "h_in2", "sb_in", "dsa_in", "moe_in", "tab2_in", "meta2_in", "mla_in"))
        dec_in = [sem("dec_in0"), sem("dec_in1")]
        sq_done, ssq_done, var_done, std_done, nrm_done, nhi_done, nlo_done = (
            sem(x) for x in ("sq_done", "ssq_done", "var_done", "std_done", "nrm_done", "nhi_done", "nlo_done"))
        rot_mm, rot_free, rot_done = sem("rot_mm"), sem("rot_free"), sem("rot_done")
        tt_mm, tt_done = sem("tt_mm"), sem("tt_done")
        sb_z, sb_l, sb_spm, sb_x, sb_e, sb_am, sb_y, sb_yh, sb_yd = (
            sem(x) for x in ("sb_z", "sb_l", "sb_spm", "sb_x", "sb_e", "sb_am", "sb_y", "sb_yh", "sb_yd"))
        ix_mm, ix_relu, ix_used, ix_neg = sem("ix_mm"), sem("ix_relu"), sem("ix_used"), sem("ix_neg")
        at_l, at_m, at_b, at_e, at_p, at_t, at_ca = (
            sem(x) for x in ("at_l", "at_m", "at_b", "at_e", "at_p", "at_t", "at_ca"))
        z_done, z_hi, z_lo = sem("z_done"), sem("z_hi"), sem("z_lo")
        rt_exp, rt_gd, rt_m = sem("rt_exp"), sem("rt_gd"), sem("rt_m")
        perm_done, tbl_done, ka_zero, ut_zero, ut_hi, ut_lo = (
            sem(x) for x in ("perm_done", "tbl_done", "ka_zero", "ut_zero", "ut_hi", "ut_lo"))
        xp_full = [sem(f"xp_full{i}") for i in range(6)]
        xw_done, xh_done, xs_done, xt_done, xhid_done, xy_done, xye_done = (
            sem(x) for x in ("xw_done", "xh_done", "xs_done", "xt_done", "xhid_done", "xy_done", "xye_done"))
        moe_pe, moe_act = sem("moe_pe"), sem("moe_act")
        g_done, gsig_done = sem("g_done"), sem("gsig_done")
        rqk_done = sem("rqk_done")
        st_mm, st_done, ro_sum, gmu_done, oc_done, rsq_done, gv_mm, gvar, gstd, rn_done, rhi_done, rlo_done = (
            sem(x) for x in ("st_mm", "st_done", "ro_sum", "gmu_done", "oc_done", "rsq_done", "gv_mm",
                             "gvar", "gstd", "rn_done", "rhi_done", "rlo_done"))
        f_sig, f_hi, f_lo = (sem(x) for x in ("f_sig", "f_hi", "f_lo"))
        stored = sem("stored")
        block = ctx.enter_context(nc.Block())

        def gbank(g):
            return PS[:, g % 4, :]

        def sbank(s):
            return PS[:, 4 + s, :]

        @block.sync
        def _(sp):
            def load(dst, src, s):
                sp.dma_start(dst, src).then_inc(s, 16)

            def slab(n):
                if n >= 3:
                    sp.wait_ge(lo_done, n - 2)
                name, blocks = SLABS[n]
                load(RAW[n % 3][:, 0:blocks * P], a[name][n - FIRST_SLAB[name]], raw_full[n % 3])

            load(H[:, 0:4, :], a["h_first"][:, 0:4, :], h_in)
            load(ones[:], a["c_ones"], norm_in)
            load(H[:, 4:8, :], a["h_first"][:, 4:8, :], h_in2)
            load(gains[:], a["gains"], norm_in)
            slab(0)
            load(ident[:], a["c_ident"], const_in)
            load(rot[:], a["rot_dsa"], const_in)
            load(cosw[:], a["cos_dsa"], const_in)
            load(sinw[:], a["sin_dsa"], const_in)
            for n in (1, 2):
                slab(n)
            load(SBM[:], a["sb_mask"], sb_in)
            load(negu[:], a["c_negu"], sb_in)
            load(negones[:], a["c_negones"], sb_in)
            for n in range(3, 11):
                slab(n)
            sp.wait_ge(unit_done, SLAB_UNITS[9])
            load(ADM[:], a["adm"], dsa_in)
            load(BND[:], a["bound"], dsa_in)
            load(WUV[:], a["w_uv"], dsa_in)
            load(WUK[:], a["w_uk"], dsa_in)
            slab(12)
            sp.wait_ge(sb_yd, HEADS)
            slab(11)
            slab(13)
            sp.wait_ge(freed["dve"], FREED[UNIT0["wo"] + 7][1])
            for name in ("RB", "DESC", "utri", "THR", "IOTA", "WRT"):
                load(small[name][:], a["m_" + name], moe_in)
            load(rot[:], a["rot_mla"], tab2_in)
            load(cosw[:], a["cos_ret"], tab2_in)
            load(sinw[:], a["sin_ret"], tab2_in)
            sp.wait_ge(lo_done, N_FIRST)
            sp.wait_ge(unit_done, UNIT0["utok"])
            sp.wait_ge(tbl_done, 1)
            items = sp.value_load(TBL[0:1, 80:81], min_val=1, max_val=ITEMS // 2) * 2
            with sp.Fori(0, items, 2) as i:
                for s in range(2):
                    e = sp.value_load(TBL[0:1, bass.ds(i + (ITEMS + s), 1)], min_val=0, max_val=NE - 1)
                    sp.wait_ge(xh_done, i + (s + 1))
                    load(XPT[3 * s][:], a["w1"][e], xp_full[3 * s])
                    load(XPT[3 * s + 1][:], a["w3"][e], xp_full[3 * s + 1])
                    sp.wait_ge(xy_done, i + (s + 1))
                    load(XPT[3 * s + 2][:], a["w2"][e], xp_full[3 * s + 2])
            sp.wait_ge(moe_pe, 1)
            for n in range(N_FIRST, N_FIRST + 3):
                slab(n)
            sp.wait_ge(ssq_done, 3)
            load(H[:, :, 0:META], a["meta2"], meta2_in)
            def decay(h):
                load(DEC[h % 2][:], a["decay"][h], dec_in[h % 2])

            for n in range(N_FIRST + 3, FIRST_SLAB["ret_gate"] + 1):
                slab(n)
            sp.wait_ge(rqk_done, 8)
            decay(0)
            ahead = FIRST_SLAB["ret_o"] + 2
            for n in range(FIRST_SLAB["ret_gate"] + 1, ahead):
                slab(n)
            sp.wait_ge(freed["dve"], FREED[UNIT0["gate"] + 15][1])
            decay(1)
            for n in range(ahead, ahead + 3):
                slab(n)
            for h in range(2, RH):
                sp.wait_ge(st_done, 3 * (h - 1))
                decay(h)
            for n in range(ahead + 3, FIRST_SLAB["kv_c"]):
                slab(n)
            load(cosw[:], a["cos_mla"], mla_in)
            load(sinw[:], a["sin_mla"], mla_in)
            for n in range(FIRST_SLAB["kv_c"], FIRST_SLAB["mla_o"] + 4):
                slab(n)
            sp.wait_ge(unit_done, UNIT0["om0"])
            load(NEG2[:], a["neg"], mla_in)
            for n in range(FIRST_SLAB["mla_o"] + 4, len(SLABS)):
                slab(n)
            for half in range(2):
                k = slice(4 * half, 4 * half + 4)
                sp.wait_ge(nrm_done, 24 + 8 * 5 + 10 + 4 * (half + 1))
                load(out[:, k, :], OUT[:, k, META:], stored)
            sp.wait_ge(stored, 32)

        @block.tensor
        def _(pe):
            def bank_free(g):
                if g >= 4:
                    eng, count = FREED[g - 4]
                    pe.wait_ge(freed[eng], count)

            def product(g, n, at_, nk, xh, xl, ready={}):
                bank_free(g)
                wh, wl = WH[n % 2], WL[n % 2]
                for k in range(nk):
                    for sem_, count in ready.get(k, ()):
                        pe.wait_ge(sem_, count)
                    c = (at_ + k) * P
                    for j, (w, x) in enumerate(((wh, xh), (wh, xl), (wl, xh))):
                        mm = pe.matmul(gbank(g)[:, 0:T], w[:, c:c + P], x(k),
                                       start=(k == 0 and j == 0), stop=(k == nk - 1 and j == 2))
                mm.then_inc(unit_done, 1)

            def slab_ready(n):
                pe.wait_ge(lo_done, n + 1)

            def token_major(g, n, nk, width, col, xh, xl, t0):
                bank_free(g)
                for k in range(nk):
                    c = k * width + col
                    for j, (x, w) in enumerate(((xh, WH[n % 2]), (xl, WH[n % 2]), (xh, WL[n % 2]))):
                        mm = pe.matmul(gbank(g)[:, 0:512], x(k, t0), w[:, c:c + 512],
                                       start=(k == 0 and j == 0), stop=(k == nk - 1 and j == 2))
                mm.then_inc(unit_done, 1)

            summed = [0]

            def norm_step(sq, k, nb):
                summed[0] += 1
                pe.wait_ge(sq_done, summed[0])
                mm = pe.matmul(sbank(0)[:, 0:T], ones[:], sq[:, k, :], start=(k == 0), stop=(k == nb - 1))
                if k == nb - 1:
                    mm.then_inc(ssq_done, 1)

            def norm_sum(sq, nb):
                for k in range(nb):
                    norm_step(sq, k, nb)

            def products_as_normed(g, count, n, nk, xh, xl, parts):
                for u in range(count):
                    bank_free(g + u)
                wh, wl = WH[n % 2], WL[n % 2]
                for k in range(nk):
                    pe.wait_ge(nhi_done, parts + k + 1)
                    pe.wait_ge(nlo_done, parts + k + 1)
                    for u in range(count):
                        c = (u * nk + k) * P
                        for j, (w, x) in enumerate(((wh, xh), (wh, xl), (wl, xh))):
                            mm = pe.matmul(gbank(g + u)[:, 0:T], w[:, c:c + P], x(k),
                                           start=(k == 0 and j == 0), stop=(k == nk - 1 and j == 2))
                        if k == nk - 1:
                            mm.then_inc(unit_done, 1)

            U = (lambda k: UH[:, k, :]), (lambda k: UL[:, k, :])
            U2 = (lambda k: U2H[:, k, :]), (lambda k: U2L[:, k, :])
            UT = (lambda k, t: UH[:, k, t:t + P]), (lambda k, t: UL[:, k, t:t + P])
            TOK3 = (0, 128, 144)

            pe.nop().then_inc(xh_done, 2)
            pe.nop().then_inc(xy_done, 2)
            pe.wait_ge(norm_in, 16 * 2)
            norm_sum(SQ, KB)
            for u in range(4):
                if u < 3:
                    pe.wait_ge(lo_first, u + 1)
                else:
                    slab_ready(0)
                product(UNIT0["qa"] + u, 0, 8 * u, KB, *U,
                        {k: ((nhi_done, k + 1), (nlo_done, k + 1)) for k in range(KB)} if u == 0 else {})
            slab_ready(1)
            for u in range(4):
                product(UNIT0["ka"] + u, 1, 8 * u, KB, *U)
            slab_ready(2)
            for j, t0 in enumerate(TOK3):
                token_major(UNIT0["va"] + j, 2, KB, 512, 0, *UT, t0)
            for n, name in ((3, "qb"), (4, "misc"), (5, "qi")):
                slab_ready(n)
                for u in range(4):
                    product(UNIT0[name] + u, n, 8 * u, KB, *U)
            ROT = [(QB, j) for j in range(4)] + [(KR, None), (KI, None)] + [(QI, j) for j in range(4)]
            RAWS = [UNIT0["qb"] + j for j in range(4)] + [UNIT0["misc"] + 1, UNIT0["misc"] + 2] \
                + [UNIT0["qi"] + j for j in range(4)]

            pe.wait_ge(const_in, 16 * 4)

            def rotate(j):
                t, b = ROT[j]
                pe.wait_ge(freed["act"], FREED[RAWS[j]][1])
                if j >= 4:
                    pe.wait_ge(rot_free, j - 3)
                pe.matmul(sbank(j % 4)[:, 0:T], rot[:], t[:, b, :] if b is not None else t[:, :],
                          start=True, stop=True).then_inc(rot_mm, 1)

            for n in range(6, 9):
                slab_ready(n)
                for u in range(4):
                    product(UNIT0["ga"] + 4 * (n - 6) + u, n, 8 * u, KB, *U)
                    if 4 * (n - 6) + u < 10:
                        rotate(4 * (n - 6) + u)
            pe.wait_ge(rot_free, 10)
            for j, (c, m) in enumerate(KEY_COLS):
                pe.matmul(sbank(2)[0:m, j * P:(j + 1) * P], CKV[:, c:c + m], ident[:],
                          start=(j == 0), stop=True, skip_group_check=True)
            for j, (c, m) in enumerate(QRY_TILES):
                mm = pe.matmul(sbank(2)[0:m, 384 + 8 * j:392 + 8 * j], WIT[0:8, c:c + m], ident[0:8, 0:8],
                               start=False, stop=True, skip_group_check=True)
            mm.then_inc(tt_mm, 1)
            def sb_scores(h, bank, first, last):
                for j, (c, q, w) in enumerate(SB_COLS):
                    k0 = KEY_TILES[j][0]
                    mm = pe.matmul(bank[:, c:c + w], KA[:, h // 2, k0:k0 + P], QA[h % 2][:, h // 2, q:q + w],
                                   start=(first and j == 0), stop=last, skip_group_check=True)
                return mm

            def sb_start(h):
                if h >= 2:
                    pe.wait_ge(sb_spm, h - 1)
                sb_scores(h, sbank(h % 2), True, True).then_inc(sb_z, 1)

            def sb_values(h):
                pe.wait_ge(sb_am, h + 1)
                if h >= 2:
                    pe.wait_ge(sb_yd, h - 1)
                r = slice(HD * (h % 2), HD * (h % 2) + HD)
                for j, (c, q, w) in enumerate(SB_COLS):
                    m = KEY_TILES[j][1]
                    mm = pe.matmul(PS[r, h % 2, q:q + w], VA[0:m, j, HD * h:HD * h + HD],
                                   SB_A[h % 2][0:m, c:c + w], start=(j == 0), stop=(j == 2),
                                   skip_group_check=True)
                mm.then_inc(sb_y, 1)

            def index_products(i):
                t = i // 2
                q0, m = QRY_TILES[t]
                for j in range(4 * i, 4 * i + 4):
                    h = j % HEADS
                    r = slice(HD * (h % 2), HD * (h % 2) + HD)
                    if j >= 2:
                        pe.wait_ge(ix_relu, j - 1)
                    pe.matmul(PS[0:m, 2 + j % 2, 0:T], QI[r, h // 2, q0:q0 + m], KI[r, :],
                              start=True, stop=True).then_inc(ix_mm, 1)

            pe.wait_ge(ka_zero, 3)
            sb_start(0)
            sb_start(1)
            slab_ready(9)
            for u in range(4):
                product(UNIT0["gb"] + 4 + u, 9, 8 * u, KB, *U)
            pe.wait_ge(tt_done, 5)
            pe.wait_ge(sb_in, 48)
            pe.wait_ge(freed["act"], FREED[UNIT0["gb"] + 7][1])
            pe.wait_ge(rot_done, 10)
            for h in range(HEADS):
                x = sbank(2 + h % 2)
                pe.wait_ge(sb_spm, h + 1)
                if h >= 2:
                    pe.wait_ge(sb_e, h - 1)
                sb_scores(h, x, True, False)
                spm = SB_SPM[h % 2]
                for j, (c, q, w) in enumerate(SB_COLS):
                    for jj in range(j + 1, 3):
                        c2, q2, w2 = SB_COLS[jj]
                        pe.matmul(x[:, c + q2 - q:c + q2 - q + w2], negones[:], spm[:, c2:c2 + w2],
                                  start=False, stop=False, skip_group_check=True)
                    mm = pe.matmul(x[:, c:c + w], negu[:], spm[:, c:c + w], start=False, stop=(j == 2),
                                   skip_group_check=True)
                mm.then_inc(sb_x, 1)
                if h + 2 < HEADS:
                    sb_start(h + 2)
                if h:
                    sb_values(h - 1)
                if h < 6:
                    index_products(h)
            sb_values(HEADS - 1)
            pe.wait_ge(sb_yd, HEADS)
            pe.wait_ge(ix_relu, 24)
            pe.wait_ge(dsa_in, 64)
            for h in range(HEADS):
                g = UNIT0["qlat"] + h
                bank_free(g)
                r = slice(HD * (h % 2), HD * (h % 2) + HD)
                pe.matmul(gbank(g)[:, 0:T], WUK[r, h // 2, :], QB[r, h // 2, :], start=True, stop=True)\
                    .then_inc(unit_done, 1)

            attn = [0, 0]

            def attention(query, value, pr, pt, name, tail):
                base, cbase = attn
                steps = [(h, t) for h in range(HEADS) for t in range(3)]

                def scores(i):
                    h, t = steps[i]
                    q0, m = QRY_TILES[t]
                    if i >= 2:
                        pe.wait_ge(at_m, base + i - 1)
                    for n, (q, k) in enumerate(query(h)):
                        mm = pe.matmul(sbank(i % 2)[0:m, 0:T], q[:, q0:q0 + m], k, start=(n == 0), stop=(n == 1))
                    mm.then_inc(at_l, 1)

                scores(0)
                def weighted(h):
                    g = UNIT0[f"{name}{h}"]
                    bank_free(g)
                    pe.wait_ge(at_ca, base + 3 * h + 3)
                    for j, (k0, mk) in enumerate(KEY_TILES):
                        mm = pe.matmul(gbank(g)[:, 0:T], value(h, j, mk), pt[h % 2][0:mk, j, :],
                                       start=(j == 0), stop=(j == 2))
                    mm.then_inc(unit_done, 1)

                for i, (h, t) in enumerate(steps):
                    if i + 1 < len(steps):
                        scores(i + 1)
                    if t == 0 and h:
                        weighted(h - 1)
                    if t == 1 and h:
                        tail(h - 1)
                    q0, m = QRY_TILES[t]
                    if i >= 2:
                        pe.wait_ge(at_ca, base + i - 1)
                    pe.wait_ge(at_p, base + i + 1)
                    for j, (c, mk) in enumerate(KEY_COLS):
                        mm = pe.matmul(sbank(2 + i % 2)[0:mk, j * P:j * P + m], pr[i % 2][0:m, c:c + mk],
                                       ident[0:m, 0:m], start=(j == 0), stop=True, skip_group_check=True)
                    mm.then_inc(at_t, 1)
                weighted(HEADS - 1)
                tail(HEADS - 1)
                attn[0] += len(steps)

            pe.wait_ge(freed["act"], FREED[UNIT0["qlat"] + 7][1])

            def dsa_query(h):
                r = slice(HD * (h % 2), HD * (h % 2) + HD)
                return (QB[r, h // 2, :], KR[r, :]), (QLAT[:, h, :], CKV[:, :])

            def dsa_tail(h):
                g = UNIT0[f"yb{h}"]
                bank_free(g)
                pe.wait_ge(freed["act"], FREED[UNIT0[f"olat{h}"]][1])
                r = slice(HD * (h % 2), HD * (h % 2) + HD)
                pe.matmul(gbank(g)[r, 0:T], WUV[:, h, :], OL[:], start=True, stop=True).then_inc(unit_done, 1)

            attention(dsa_query, lambda h, j, mk: CKVT[0:mk, j, :], PR, PT, "olat", dsa_tail)

            pe.wait_ge(sb_yd, HEADS)
            slab_ready(10)
            for m in range(8):
                product(UNIT0["za"] + m, 10, 4 * m, 4, lambda k: YAH[:, k, :], lambda k: YAL[:, k, :])
            pe.wait_ge(freed["dve"], FREED[UNIT0["yb7"]][1])
            slab_ready(11)
            for m in range(8):
                product(UNIT0["zb"] + m, 11, 4 * m, 4, lambda k: YBH[:, k, :], lambda k: YBL[:, k, :])
            pe.wait_ge(z_hi, 8)
            pe.wait_ge(z_lo, 8)
            for n in (12, 13):
                slab_ready(n)
                for u in range(4):
                    m = 4 * (n - 12) + u
                    product(UNIT0["wo"] + m, n, 8 * u, KB, lambda k: ZH[:, k, :], lambda k: ZL[:, k, :])
                    if m:
                        norm_step(UMT, m - 1, KB)

            norm_step(UMT, KB - 1, KB)
            g = UNIT0["router"]
            bank_free(g)
            pe.wait_ge(moe_in, 16 * 6)
            for t, (q0, m) in enumerate(QRY_TILES):
                for k in range(KB):
                    if t == 0:
                        pe.wait_ge(nrm_done, 8 + k + 1)
                    mm = pe.matmul(gbank(g)[0:m, 36 * t:36 * t + 36], UM[:, k, q0:q0 + m],
                                   small["WRT"][:, k, :], start=(k == 0), stop=(k == KB - 1),
                                   skip_group_check=True)
            mm.then_inc(unit_done, 1)
            for t, (q0, m) in enumerate(QRY_TILES):
                for half in range(2):
                    g = UNIT0["utok"] + 2 * t + half
                    bank_free(g)
                    for k in range(4):
                        mm = pe.matmul(gbank(g)[0:m, k * P:(k + 1) * P], UM[:, 4 * half + k, q0:q0 + m],
                                       ident[:], start=(k == 0), stop=True, skip_group_check=True)
                    mm.then_inc(unit_done, 1)
            MM, CC, CB, TA, N5 = (small[x] for x in ("MM", "CC", "CB", "TA", "N5"))
            g = UNIT0["rank"]
            bank_free(g)
            pe.wait_ge(rt_m, 1)
            for t in range(3):
                mm = pe.matmul(gbank(g)[0:NE, 0:1], MM[0:QRY_TILES[t][1], t, :], ones[0:QRY_TILES[t][1], 0:1], start=(t == 0), stop=(t == 2))
            mm.then_inc(unit_done, 1)
            g += 1
            bank_free(g)
            pe.wait_ge(rt_m, 2)
            for t in range(3):
                c = slice(NE * t, NE * t + NE)
                m = QRY_TILES[t][1]
                for tt in range(t):
                    pe.matmul(gbank(g)[:, c], ones[:], MM[:, tt, :], start=(tt == 0), stop=False,
                              skip_group_check=True)
                pe.matmul(gbank(g)[:, c], utri[0:m, :], MM[0:m, t, :], start=(t == 0), stop=False,
                          skip_group_check=True)
                pe.matmul(gbank(g)[:, c], CB[0:NE, :], utri[0:NE, 0:NE], start=False, stop=True,
                          skip_group_check=True)
            pe.matmul(gbank(g)[0:NE, 96:97], utri[0:NE, 0:NE], CC[0:NE, 0:1], start=False, stop=True,
                      skip_group_check=True)
            pe.matmul(gbank(g)[0:NE, 97:98], utri[0:NE, 0:NE], CC[0:NE, 1:2], start=False, stop=False,
                      skip_group_check=True)
            pe.matmul(gbank(g)[0:NE, 97:98], ident[0:NE, 0:NE], CC[0:NE, 1:2], start=False, stop=True,
                      skip_group_check=True).then_inc(unit_done, 1)
            g += 1
            bank_free(g)
            pe.wait_ge(rt_m, 3)
            pe.matmul(gbank(g)[0:1, 0:81], ones[0:NE, 0:1], TA[0:NE, 0:81], start=True, stop=True)\
                .then_inc(unit_done, 1)
            pe.wait_ge(perm_done, 1)
            pe.wait_ge(ut_hi, 6)
            pe.wait_ge(ut_lo, 6)
            for k in range(KB):
                for half in range(2):
                    g = UNIT0["disp"] + 2 * k + half
                    bank_free(g)
                    c0 = half * (XCOLS // 2)
                    for t in range(3):
                        for j, part in enumerate((UTH, UTL)):
                            mm = pe.matmul(gbank(g)[:, 0:XCOLS // 2], part[:, t, k * P:(k + 1) * P],
                                           PERM[:, t, c0:c0 + XCOLS // 2], start=(t == 0 and j == 0),
                                           stop=(t == 2 and j == 1))
                    mm.then_inc(unit_done, 1)
            pe.wait_ge(freed["act"], FREED[UNIT0["disp"] + 15][1])
            pe.wait_ge(tbl_done, 1)

            def hidden(base, s):
                pe.wait_ge(xw_done, base + (s + 1))
                pe.wait_ge(xhid_done, base + (s + 1))
                for b in range(2):
                    pe.wait_ge(xp_full[3 * s + b], base * 8 + 16)
                    hb = PS[:, 2 * b + s, :]
                    for m in range(4):
                        for k in range(KB):
                            mm = pe.matmul(hb[:, WIN * m:WIN * m + WIN],
                                           XPT[3 * s + b][:, (m * KB + k) * P:(m * KB + k + 1) * P],
                                           XW[s][:, k, :], start=(k == 0), stop=(k == KB - 1))
                mm.then_inc(xh_done, 1)

            def outputs(base, s):
                pe.wait_ge(xp_full[3 * s + 2], base * 8 + 16)
                pe.wait_ge(xye_done, base + (s + 1))
                pe.wait_ge(xhid_done, base + (s + 3))
                for m in range(8):
                    for k in range(4):
                        mm = pe.matmul(PS[:, 4 + 2 * s + m // 4, WIN * (m % 4):WIN * (m % 4) + WIN],
                                       XPT[3 * s + 2][:, (m * 4 + k) * P:(m * 4 + k + 1) * P],
                                       HID[s][:, k, :], start=(k == 0), stop=(k == 3))
                mm.then_inc(xy_done, 1)

            hidden(0, 0)
            last = pe.value_load(TBL[0:1, 81:82], min_val=2, max_val=ITEMS - 2)
            with pe.Fori(0, last, 2) as i:
                hidden(i, 1)
                outputs(i, 0)
                hidden(i + 2, 0)
                outputs(i, 1)
            hidden(last, 1)
            outputs(last, 0)
            outputs(last, 1)
            pe.wait_ge(xye_done, last + 4)
            pe.nop().then_inc(moe_pe, 1)
            pe.wait_ge(moe_act, 1)
            for st in range(5):
                m = min(P, SLOTS - P * st)
                for half in range(2):
                    g = UNIT0["yslot"] + 2 * st + half
                    bank_free(g)
                    for k in range(4):
                        mm = pe.matmul(gbank(g)[0:m, k * P:(k + 1) * P],
                                       YS[:, 4 * half + k, P * st:P * st + m], ident[:],
                                       start=(k == 0), stop=True, skip_group_check=True)
                    mm.then_inc(unit_done, 1)
            pe.wait_ge(g_done, 3)
            for st in range(5):
                m = min(P, SLOTS - P * st)
                g = UNIT0["gt"] + st
                bank_free(g)
                for t, (q0, mq) in enumerate(QRY_TILES):
                    mm = pe.matmul(gbank(g)[0:m, q0:q0 + mq], G[0:mq, t, P * st:P * st + m],
                                   ident[0:mq, 0:mq], start=(t == 0), stop=True, skip_group_check=True)
                mm.then_inc(unit_done, 1)
            pe.wait_ge(freed["act"], FREED[UNIT0["yslot"] + 9][1])
            pe.wait_ge(freed["dve"], FREED[UNIT0["gt"] + 4][1])
            for k in range(KB):
                g = UNIT0["comb"] + k
                bank_free(g)
                for st in range(5):
                    m = min(P, SLOTS - P * st)
                    mm = pe.matmul(gbank(g)[:, 0:T], YSLOT[0:m, st, k * P:(k + 1) * P], GT[0:m, st, :],
                                   start=(st == 0), stop=(st == 4))
                mm.then_inc(unit_done, 1)
                if k:
                    norm_step(UMT, k - 1, KB)
            norm_step(UMT, KB - 1, KB)
            pe.wait_ge(var_done, 3)
            norm_sum(SQ3, KB)
            n = FIRST_SLAB["ret_qk"]
            for h in range(RH):
                slab_ready(n + h)
                if h == 0:
                    products_as_normed(UNIT0["rqk"], 4, n, KB, *U, 8)
                    continue
                for u in range(4):
                    product(UNIT0["rqk"] + 4 * h + u, n + h, 8 * u, KB, *U)
            n = FIRST_SLAB["ret_v"]
            for h in range(RH):
                slab_ready(n + h)
                for j, t0 in enumerate(TOK3):
                    token_major(UNIT0["rv"] + 3 * h + j, n + h, KB, 512, 0, *UT, t0)
            n = FIRST_SLAB["ret_gate"]
            def ret_scores(h):
                for j, (c, mk) in enumerate(KEY_COLS):
                    i = 3 * h + j
                    if i >= 3:
                        pe.wait_ge(st_done, i - 2)
                    for b in range(2):
                        mm = pe.matmul(sbank(i % 3)[0:mk, 0:T], RK[:, 2 * h + b, c:c + mk], RQ[:, 2 * h + b, :],
                                       start=(b == 0), stop=(b == 1))
                    mm.then_inc(st_mm, 1)

            for h in range(4):
                slab_ready(n + h)
                if h == 3:
                    pe.wait_ge(rqk_done, 8)
                    ret_scores(0)
                for u in range(4):
                    product(UNIT0["gate"] + 4 * h + u, n + h, 8 * u, KB, *U)
            pe.wait_ge(freed["act"], FREED[UNIT0["rv"] + 11][1])

            def ret_out(k0, k1):
                g, n = UNIT0["rwo"], FIRST_SLAB["ret_o"]
                if k0 == 0:
                    slab_ready(n)
                    for u in range(2):
                        bank_free(g + u)
                for k in range(k0, k1):
                    if k % 4 == 0:
                        pe.wait_ge(rhi_done, k // 4 + 1)
                        pe.wait_ge(rlo_done, k // 4 + 1)
                    for u in range(2):
                        c = (16 * u + k) * P
                        for j, (w, x) in enumerate(((WH, RHI[:, k, :]), (WH, RLO[k // 4][:, k % 4, :]),
                                                    (WL, RHI[:, k, :]))):
                            mm = pe.matmul(gbank(g + u)[:, 0:T], w[n % 2][:, c:c + P], x,
                                           start=(k == 0 and j == 0), stop=(k == 15 and j == 2))
                        if k == 15:
                            mm.then_inc(unit_done, 1)

            def ret_values(h):
                pe.wait_ge(st_done, 3 * (h + 1))
                for v in range(4):
                    g = UNIT0["ro"] + 4 * h + v
                    bank_free(g)
                    for j, (k0, mk) in enumerate(KEY_TILES):
                        mm = pe.matmul(gbank(g)[:, 0:T], RVV[h][0:mk, j, v * P:(v + 1) * P],
                                       ST[h % 2][0:mk, j, :], start=(j == 0), stop=(j == 2))
                    mm.then_inc(unit_done, 1)

            ret_values(0)
            ret_scores(1)
            for h in range(RH):
                pe.wait_ge(freed["act"], FREED[UNIT0["ro"] + 4 * h + 3][1])
                if h:
                    pe.wait_ge(gvar, h)
                for v in range(4):
                    mm = pe.matmul(sbank(3)[:, 0:T], ones[:], RO[h % 2][:, v, :], start=(v == 0), stop=(v == 3))
                mm.then_inc(ro_sum, 1)
                if h + 1 < RH:
                    ret_values(h + 1)
                else:
                    ret_out(0, RH)
                pe.wait_ge(rsq_done, h + 1)
                pe.wait_ge(gmu_done, h + 1)
                for v in range(4):
                    mm = pe.matmul(sbank(3)[:, 0:T], ones[:], RSQ[h % 2][:, v, :], start=(v == 0), stop=(v == 3))
                mm.then_inc(gv_mm, 1)
                if h + 2 < RH:
                    ret_scores(h + 2)
                elif h == RH - 1:
                    ret_out(RH, 2 * RH)
            ret_out(2 * RH, 4 * RH)
            n = FIRST_SLAB["ret_o"]
            for s in range(4):
                slab_ready(n + s)
                if s == 0:
                    continue
                for u in range(2):
                    product(UNIT0["rwo"] + 2 * s + u, n + s, 16 * u, 16,
                            lambda k: RHI[:, k, :], lambda k: RLO[k // 4][:, k % 4, :])
                    norm_step(SQR, 2 * s + u - 2, KB)
            norm_step(SQR, KB - 2, KB)

            def ffn(layer, parts, sq, sq_next):
                norm_step(sq, KB - 1, KB)
                n = FIRST_SLAB[f"up{layer}"]
                for s in range(11):
                    slab_ready(n + s)
                    if s == 0:
                        products_as_normed(UNIT0[f"up{layer}"], 4, n, KB, *U, parts)
                        continue
                    for u in range(4):
                        product(UNIT0[f"up{layer}"] + 4 * s + u, n + s, 8 * u, KB, *U)
                n = FIRST_SLAB[f"down{layer}"]
                pe.wait_ge(f_hi, FB * (layer + 1) - 2)
                pe.wait_ge(f_lo, FB * (layer + 1) - 2)
                for s in range(8):
                    slab_ready(n + s)
                    product(UNIT0[f"down{layer}"] + s, n + s, 0, FB,
                            lambda k: TH[:, k, :], lambda k: TL[:, k, :],
                            {k: ((f_hi, FB * layer + k + 1), (f_lo, FB * layer + k + 1))
                             for k in (FB - 2, FB - 1)} if s == 0 else {})
                    if s:
                        norm_step(sq_next, s - 1, KB)

            ffn(0, 16, SQR, SQM)
            norm_step(SQM, KB - 1, KB)
            n = FIRST_SLAB["kv_c"]
            slab_ready(n)
            products_as_normed(UNIT0["kvc"], 4, n, KB, *U, 24)
            slab_ready(n + 1)
            product(UNIT0["krq"], n + 1, 0, KB, *U)
            pe.wait_ge(nlo_done, 8 * 5)
            pe.wait_ge(nhi_done, 8 * 5)
            for u in range(1, 4):
                product(UNIT0["krq"] + u, n + 1, 8 * u, KB, *U2)
            norm_sum(SQQ, 4)
            slab_ready(n + 2)
            for u in range(3):
                product(UNIT0["qar"] + u, n + 2, 8 * u, KB, *U2)
            CK = (lambda k: CKH[:, k, :]), (lambda k: CKL[:, k, :])
            CKT = (lambda k, t: CKH[:, k, t:t + P]), (lambda k, t: CKL[:, k, t:t + P])
            slab_ready(n + 3)
            products_as_normed(UNIT0["kn"], 4, n + 3, 4, *CK, 40)
            norm_sum(SQQ, 6)
            for u in range(4, 8):
                product(UNIT0["kn"] + u, n + 3, 4 * u, 4, *CK)
            slab_ready(n + 4)
            for j, t0 in enumerate(TOK3):
                for half in range(2):
                    token_major(UNIT0["vm"] + 2 * j + half, n + 4, 4, D, 512 * half, *CKT, t0)
            pe.wait_ge(nlo_done, 8 * 5 + 10)
            pe.wait_ge(nhi_done, 8 * 5 + 10)
            n = FIRST_SLAB["q_b"]

            def rotate_mla(j):
                t, src = (QR[:, j - 1, :], UNIT0["qr"] + j - 1) if j else (KR2[:, :], UNIT0["krq"])
                pe.wait_ge(freed["act"], FREED[src][1])
                if j >= 4:
                    pe.wait_ge(rot_free, 10 + j - 3)
                pe.matmul(sbank(j % 4)[:, 0:T], rot[:], t, start=True, stop=True).then_inc(rot_mm, 1)

            rotate_mla(0)
            for s in range(3):
                slab_ready(n + s)
                for u in range(4):
                    product(UNIT0["qn"] + 4 * s + u, n + s, 6 * u, 6,
                            lambda k: CQH[:, k, :], lambda k: CQL[:, k, :])
                    if s == 2 and u:
                        rotate_mla(u)
            rotate_mla(4)
            pe.wait_ge(rot_done, 15)

            def mla_query(h):
                r = slice(HD * (h % 2), HD * (h % 2) + HD)
                return (QN[:, h, :], KN[:, h, :]), (QR[r, h // 2, :], KR2[r, :])

            attention(mla_query, lambda h, j, mk: VM[0:mk, j, h * P:(h + 1) * P], PR2, PT2, "om",
                      lambda h: None)
            pe.wait_ge(freed["dve"], FREED[UNIT0["om7"]][1])
            n = FIRST_SLAB["mla_o"]
            for s in range(2):
                slab_ready(n + s)
                for u in range(4):
                    product(UNIT0["mo"] + 4 * s + u, n + s, 8 * u, KB,
                            lambda k: OMH[:, k, :], lambda k: OML[:, k, :])
                    if 4 * s + u:
                        norm_step(SQ2, 4 * s + u - 1, KB)
            ffn(1, 50, SQ2, SQ2)
            norm_step(SQ2, KB - 1, KB)

        @block.scalar
        def _(act):
            steps = [0]

            def link(ins):
                steps[0] += 1
                ins.then_inc(act_step, 1)
                act.wait_ge(act_step, steps[0])

            def hi(n):
                act.wait_ge(raw_full[n % 3], 16 * (n // 3 + 1))
                if n >= 2:
                    act.wait_ge(unit_done, SLAB_UNITS[n - 2])
                w = SLABS[n][1] * P
                act.activation(WH[n % 2][:, 0:w], RAW[n % 3][:, 0:w], ACT.Copy).then_inc(hi_done, 1)

            def read_out(g, dst, func=ACT.Copy, rows=slice(0, P), cols=slice(0, T), **kw):
                act.wait_ge(unit_done, g + 1)
                act.activation(dst, gbank(g)[rows, cols], func, **kw).then_inc(freed["act"], 1)

            norms, split = [0], [0]

            def squares(dst, src, nb=1):
                act.activation(dst, src, ACT.Square).then_inc(sq_done, nb)

            def square_of_sum(dst, name, m):
                act.wait_ge(freed["dve"], FREED[UNIT0[name] + m][1])
                squares(dst[:, m, :], H[:, m, :])

            def std():
                norms[0] += 1
                act.wait_ge(var_done, norms[0])
                act.activation(rs[:], rs[:], ACT.Sqrt).then_inc(std_done, 1)

            def high(dst, src, nrm):
                act.wait_ge(nrm_done, nrm)
                act.activation(dst, src, ACT.Copy).then_inc(nhi_done, 1)

            act.wait_ge(h_in, 16)
            for k in range(KB):
                if k == 4:
                    act.wait_ge(h_in2, 16)
                squares(SQ[:, k, :], H[:, k, :])
            std()
            hi(0)
            for k in range(KB):
                high(UH[:, k, :], SQ[:, k, :], k + 1)
            hi(1)
            act.wait_ge(ka_zero, 3)
            for u in range(4):
                g = UNIT0["qa"] + u
                act.wait_ge(unit_done, g + 1)
                act.activation(QA[0][0:HD, u, :], gbank(g)[0:HD, 0:T], ACT.Copy, scale=HD ** -0.5)
                read_out(g, QA[1][HD:, u, :], rows=slice(HD, P), scale=HD ** -0.5)
            hi(2)
            for u in range(4):
                read_out(UNIT0["ka"] + u, KA[:, u, 0:T])
            hi(3)
            for j in range(3):
                if j < 2:
                    read_out(UNIT0["va"] + j, VA[:, j, :], cols=slice(0, 512))
                else:
                    read_out(UNIT0["va"] + j, VA[0:32, j, :], rows=slice(96, P), cols=slice(0, 512))
            hi(4)
            for u in range(4):
                read_out(UNIT0["qb"] + u, QB[:, u, :])
            hi(5)
            for u, dst in enumerate((CKV, KR, KI, WIT)):
                read_out(UNIT0["misc"] + u, dst[:])
            hi(6)
            for u in range(4):
                read_out(UNIT0["qi"] + u, QI[:, u, :])
            hi(7)
            def gates(n):
                for u in range(4):
                    k = 4 * (n - 6) + u
                    read_out(UNIT0["ga"] + k, (GA if k < KB else GB)[:, k % KB, :], ACT.Sigmoid)

            for n in range(6, 9):
                gates(n)
                hi(n + 2)
            act.wait_ge(tt_mm, 1)
            for j, (k0, mk) in enumerate(KEY_TILES):
                act.activation(CKVT[0:mk, j, :], sbank(2)[0:mk, j * P:(j + 1) * P], ACT.Copy)\
                    .then_inc(tt_done, 1)
            for rows, c in ((P, slice(0, 2)), (16, slice(2, 3))):
                act.activation(WI[0:rows, c, :], sbank(2)[0:rows, 384 + 8 * c.start:384 + 8 * c.stop]
                               .rearrange("p (t h) -> p t h", h=8), ACT.Copy).then_inc(tt_done, 1)

            def sb_log(h):
                L = SB_L[h % 2]
                act.wait_ge(sb_z, h + 1)
                link(act.activation(L[:], sbank(h % 2)[:, 0:SBW], ACT.Abs))
                link(act.activation(L[:], L[:], ACT.Exp, scale=-1.0))
                act.activation(L[:], L[:], ACT.Ln, bias=1.0).then_inc(sb_l, 1)

            def index_relu(i):
                m = QRY_TILES[i // 2][1]
                for j in range(4 * i, 4 * i + 4):
                    act.wait_ge(ix_mm, j + 1)
                    if j >= 4:
                        act.wait_ge(ix_used, j - 3)
                    act.activation(RL[j % 4][0:m, :], PS[0:m, 2 + j % 2, 0:T], ACT.Relu).then_inc(ix_relu, 1)

            def sb_high(h):
                act.wait_ge(sb_y, h + 1)
                r = slice(HD * (h % 2), HD * (h % 2) + HD)
                act.activation(YAH[r, h // 2, :], PS[r, h % 2, 0:T], ACT.Copy).then_inc(sb_yh, 1)

            act.wait_ge(lo_done, 9)
            sb_log(0)
            sb_log(1)
            gates(9)
            for h in range(HEADS):
                if 1 < h + 1 < HEADS:
                    sb_log(h + 1)
                act.wait_ge(sb_x, h + 1)
                if h >= 2:
                    act.wait_ge(sb_y, h - 1)
                act.activation(SB_A[h % 2][:], sbank(2 + h % 2)[:, 0:SBW], ACT.Exp).then_inc(sb_e, 1)
                if h:
                    sb_high(h - 1)
                if h < 6:
                    index_relu(h)
            sb_high(HEADS - 1)

            for h in range(HEADS):
                read_out(UNIT0["qlat"] + h, QLAT[:, h, :])

            attn = [0]

            def attention(pr, pt, scale, name, tail):
                base = attn[0]
                steps_ = [(h, t) for h in range(HEADS) for t in range(3)]

                def exps(i):
                    m = QRY_TILES[steps_[i][1]][1]
                    act.wait_ge(at_b, base + i + 1)
                    act.activation(pr[i % 2][0:m, :], pr[i % 2][0:m, :], ACT.Exp, scale=scale,
                                   bias=SMALL[0:m, 2 + i % 2:3 + i % 2],
                                   accum_out=SMALL[0:m, 4 + i % 2:5 + i % 2]).then_inc(at_e, 1)

                exps(0)
                for i, (h, t) in enumerate(steps_):
                    if i + 1 < len(steps_):
                        exps(i + 1)
                    if t == 0 and h:
                        tail(h - 1)
                    q0, m = QRY_TILES[t]
                    act.wait_ge(at_t, base + i + 1)
                    if t == 0 and h >= 2:
                        act.wait_ge(unit_done, UNIT0[f"{name}{h - 2}"] + 1)
                    b = sbank(2 + i % 2)
                    act.activation(pt[h % 2][:, 0:2, q0:q0 + m],
                                   b[:, 0:2 * P].rearrange("p (j q) -> p j q", j=2)[:, :, 0:m], ACT.Copy)
                    act.activation(pt[h % 2][0:32, 2, q0:q0 + m], b[0:32, 2 * P:2 * P + m], ACT.Copy)\
                        .then_inc(at_ca, 1)
                tail(HEADS - 1)
                attn[0] += len(steps_)

            def dsa_tail(h):
                if h:
                    act.wait_ge(unit_done, UNIT0[f"yb{h - 1}"] + 1)
                read_out(UNIT0[f"olat{h}"], OL[:])

            attention(PR, PT, HD ** -0.5, "olat", dsa_tail)
            act.wait_ge(unit_done, UNIT0["yb7"] + 1)
            hi(11)
            hi(12)
            for m in range(8):
                act.wait_ge(z_done, m + 1)
                act.activation(ZH[:, m, :], ZT[:, m % 2, :], ACT.Copy).then_inc(z_hi, 1)
            hi(13)

            for m in range(KB):
                square_of_sum(UMT, "wo", m)
            std()
            act.wait_ge(ut_zero, 2)
            for t, (q0, m) in enumerate(QRY_TILES):
                for half in range(2):
                    g = UNIT0["utok"] + 2 * t + half
                    c = slice(512 * half, 512 * half + 512)
                    read_out(g, UTOK[0:m, t, c], rows=slice(0, m), cols=slice(0, 512))
                    act.wait_ge(freed["act"], FREED[g][1])
                    act.activation(UTH[0:m, t, c], UTOK[0:m, t, c], ACT.Copy).then_inc(ut_hi, 1)
            for j, tile in enumerate(("GE", "M2")):
                act.wait_ge(rt_exp, j + 1)
                act.activation(small[tile][:], small[tile][:], ACT.Exp).then_inc(rt_gd, 1)
            for k in range(KB):
                for half in range(2):
                    c0 = half * (XCOLS // 2)
                    read_out(UNIT0["disp"] + 2 * k + half, XS[:, k, c0:c0 + XCOLS // 2],
                             cols=slice(0, XCOLS // 2))
            act.wait_ge(tbl_done, 1)
            items = act.value_load(TBL[0:1, 80:81], min_val=1, max_val=ITEMS // 2) * 2
            act.nop().then_inc(xye_done, 2)
            with act.Fori(0, items, 2) as i:
                for s in range(2):
                    at_ = act.value_load(TBL[0:1, bass.ds(i + s, 1)], min_val=0, max_val=SLOTS)
                    act.wait_ge(xh_done, i + (s + 3))
                    act.wait_ge(xhid_done, i + (s + 1))
                    act.activation(SG[s][:], PS[:, s, 0:4 * WIN].rearrange("p (m w) -> p m w", m=4),
                                   ACT.Sigmoid).then_inc(xs_done, 1)
                    act.wait_ge(xy_done, i + (s + 3))
                    act.wait_ge(xye_done, i + (s + 2))
                    act.activation(YS[:, :, bass.ds(at_, WIN)].rearrange("p (b m) w -> p b m w", b=2),
                                   PS[:, 4 + 2 * s:6 + 2 * s, 0:4 * WIN].rearrange("p b (m w) -> p b m w", m=4),
                                   ACT.Copy).then_inc(xye_done, 1)
            act.wait_ge(xye_done, items + 2)
            act.nop().then_inc(moe_act, 1)
            for st in range(5):
                m = min(P, SLOTS - P * st)
                for half in range(2):
                    read_out(UNIT0["yslot"] + 2 * st + half, YSLOT[0:m, st, 512 * half:512 * half + 512],
                             rows=slice(0, m), cols=slice(0, 512))
            act.wait_ge(moe_pe, 1)
            hi(N_FIRST)
            for m in range(KB):
                square_of_sum(UMT, "comb", m)
            std()
            act.wait_ge(meta2_in, 16)
            for k in range(KB):
                act.wait_ge(nrm_done, 16 + k + 1)
                squares(SQ3[:, k, :], H[:, k, :])
            std()
            for k in range(KB):
                high(UH[:, k, :], SQ3[:, k, :], 24 + k + 1)
            hi(N_FIRST + 1)
            n = FIRST_SLAB["ret_qk"]
            for h in range(RH):
                hi(n + h + 2)
            for h in range(RH):
                for j in range(3):
                    if j < 2:
                        read_out(UNIT0["rv"] + 3 * h + j, RVV[h][:, j, :], cols=slice(0, 512))
                    else:
                        read_out(UNIT0["rv"] + 3 * h + j, RVV[h][0:32, j, :], rows=slice(96, P),
                                 cols=slice(0, 512))
                hi(n + RH + h + 2)
            for s in range(4):
                for u in range(4):
                    j = 4 * s + u
                    g = UNIT0["gate"] + j
                    act.wait_ge(unit_done, g + 1)
                    if j == 0:
                        act.wait_ge(rqk_done, 8)
                    if j >= 2:
                        act.wait_ge(freed["dve"], FREED[g - 2][1])
                    act.activation(GSIG[j % 2][:], gbank(g)[:, 0:T], ACT.Sigmoid).then_inc(gsig_done, 1)
                hi(n + 2 * RH + s + 2)
            def ret_read(h):
                if h >= 2:
                    act.wait_ge(rn_done, h - 1)
                for v in range(4):
                    read_out(UNIT0["ro"] + 4 * h + v, RO[h % 2][:, v, :])

            def ret_square(h):
                act.wait_ge(oc_done, h + 1)
                if h >= 2:
                    act.wait_ge(rlo_done, h - 1)
                act.activation(RSQ[h % 2][:], RO[h % 2][:], ACT.Square).then_inc(rsq_done, 1)

            ret_read(0)
            ret_square(0)
            for h in range(RH):
                if h + 1 < RH:
                    ret_read(h + 1)
                act.wait_ge(gvar, h + 1)
                act.activation(GRS[:], GRS[:], ACT.Sqrt).then_inc(gstd, 1)
                act.wait_ge(rn_done, h + 1)
                act.activation(RHI[:, 4 * h:4 * h + 4, :], RSQ[h % 2][:], ACT.Copy).then_inc(rhi_done, 1)
                if h + 1 < RH:
                    ret_square(h + 1)
            n = FIRST_SLAB["ret_o"]
            for s in range(4):
                square_of_sum(SQR, "rwo", 2 * s)
                if s < 3:
                    hi(n + s + 2)
                square_of_sum(SQR, "rwo", 2 * s + 1)

            def ffn(layer, nrm, sq_next):
                std()
                for k in range(KB):
                    high(UH[:, k, :], SQ2[:, k, :], nrm + k + 1)
                n = FIRST_SLAB[f"up{layer}"]
                hi(n + 1)
                f0 = FB * layer

                def high_hidden(p):
                    act.wait_ge(freed["dve"], FREED[UNIT0[f"up{layer}"] + 2 * p + 1][1])
                    act.activation(TH[:, p, :], FU[p % 2][:], ACT.Copy).then_inc(f_hi, 1)

                for p in range(FB):
                    g = UNIT0[f"up{layer}"] + 2 * p
                    act.wait_ge(unit_done, g + 1)
                    if p >= 2:
                        act.wait_ge(freed["dve"], FREED[g - 4][1])
                    act.activation(FS[p % 2][:], gbank(g)[:, 0:T], ACT.Sigmoid).then_inc(f_sig, 1)
                    if p:
                        high_hidden(p - 1)
                    if p % 2:
                        if n + p // 2 + 2 < len(SLABS):
                            hi(n + p // 2 + 2)
                high_hidden(FB - 1)
                n = FIRST_SLAB[f"down{layer}"]
                for s in range(8):
                    if s < 7 and n + s + 2 < len(SLABS):
                        hi(n + s + 2)
                    square_of_sum(sq_next, f"down{layer}", s)

            ffn(0, 32, SQM)
            std()
            for k in range(KB):
                high(UH[:, k, :], SQM[:, k, :], 40 + k + 1)
            hi(FIRST_SLAB["kv_c"] + 1)
            for k in range(KB):
                high(U2H[:, k, :], SQQ[:, k, :], 48 + k + 1)
            for u in range(4):
                read_out(UNIT0["kvc"] + u, CKRAW[:, u, :])
            act.wait_ge(freed["act"], FREED[UNIT0["kvc"] + 3][1])
            act.wait_ge(nlo_done, 40)
            squares(SQQ[:, 0:4, :], CKRAW[:], 4)
            hi(FIRST_SLAB["kv_c"] + 2)
            read_out(UNIT0["krq"], KR2[:])
            for u in range(3):
                read_out(UNIT0["krq"] + 1 + u, CRAW[:, u, :])
            hi(FIRST_SLAB["kv_c"] + 3)
            std()
            for k in range(4):
                high(CKH[:, k, :], SQQ[:, k, :], 56 + k + 1)
            for u in range(3):
                read_out(UNIT0["qar"] + u, CRAW[:, 3 + u, :])
            act.wait_ge(freed["act"], FREED[UNIT0["qar"] + 2][1])
            act.wait_ge(nlo_done, 44)
            squares(SQQ[:, 0:6, :], CRAW[:], 6)
            hi(FIRST_SLAB["kv_c"] + 4)
            for u in range(4):
                read_out(UNIT0["kn"] + u, KN[:, u, :])
            std()
            for u in range(4, 8):
                read_out(UNIT0["kn"] + u, KN[:, u, :])
            for k in range(6):
                high(CQH[:, k, :], SQQ[:, k, :], 60 + k + 1)
            hi(FIRST_SLAB["kv_c"] + 5)
            act.wait_ge(nlo_done, 50)
            for j in range(3):
                for half in range(2):
                    g = UNIT0["vm"] + 2 * j + half
                    c = slice(512 * half, 512 * half + 512)
                    if j < 2:
                        read_out(g, VM[:, j, c], cols=slice(0, 512))
                    else:
                        read_out(g, VM[0:32, j, c], rows=slice(96, P), cols=slice(0, 512))
            hi(FIRST_SLAB["kv_c"] + 6)
            for s in range(3):
                for u in range(4):
                    j = 4 * s + u
                    read_out(UNIT0["qn"] + j, QN[:, j, :] if j < 8 else QR[:, j - 8, :])
                hi(FIRST_SLAB["q_b"] + s + 2)
            attention(PR2, PT2, (P + HD) ** -0.5, "om", lambda h: None)
            for s in range(2):
                for u in range(4):
                    if u == 3 and s == 0:
                        hi(FIRST_SLAB["mla_o"] + 2)
                    square_of_sum(SQ2, "mo", 4 * s + u)
            ffn(1, 66, SQ2)
            std()

        @block.vector
        def _(dve):
            steps = [0]

            def link(ins):
                steps[0] += 1
                ins.then_inc(dve_step, 1)
                dve.wait_ge(dve_step, steps[0])

            def lo(n):
                dve.wait_ge(hi_done, n + 1)
                w = SLABS[n][1] * P
                dve.tensor_tensor(WL[n % 2][:, 0:w], RAW[n % 3][:, 0:w], WH[n % 2][:, 0:w].bitcast(F32),
                                  ALU.subtract).then_inc(lo_done, 1)

            def freeing(ins, n=1):
                ins.then_inc(freed["dve"], n)

            norms, nrm = [0], [0]

            def scale_of(n, between=lambda: None):
                norms[0] += 1
                dve.wait_ge(ssq_done, norms[0])
                dve.tensor_scalar(rs[:], sbank(0)[:, 0:T], 1.0 / n, EPS, ALU.mult, ALU.add).then_inc(var_done, 1)
                between()
                dve.wait_ge(std_done, norms[0])
                link(dve.reciprocal(rs[:], rs[:]))

            def normed(dst, src, gain, nb, c0=0):
                for k in range(nb):
                    gcol = GAINS[gain] + k
                    dve.scalar_tensor_tensor(out=dst[:, k, c0:], in0=src[:, k, c0:], scalar=gains[:, gcol:gcol + 1],
                                             in1=rs[:, c0:], op0=ALU.mult, op1=ALU.mult).then_inc(nrm_done, 1)

            def add_to_h(g, m):
                dve.wait_ge(unit_done, g + 1)
                freeing(dve.tensor_tensor(H[:, m, :], gbank(g)[:, 0:T], H[:, m, :], ALU.add))

            def bc(ap, shape):
                return ap.broadcast_to(shape)

            dve.memset(QA[0][HD:, :, :], 0.0).then_inc(ka_zero, 1)
            dve.memset(QA[1][0:HD, :, :], 0.0).then_inc(ka_zero, 1)
            dve.wait_ge(norm_in, 16 * 2)
            scale_of(D)
            normed(SQ, H, "mix", KB)
            dve.wait_ge(hi_done, 1)
            for u in range(4):
                c = slice(1024 * u, 1024 * u + 1024)
                dve.tensor_tensor(WL[0][:, c], RAW[0][:, c], WH[0][:, c].bitcast(F32),
                                  ALU.subtract).then_inc(lo_first if u < 3 else lo_done, 1)
            for n in range(1, 8):
                lo(n)

            dve.wait_ge(const_in, 16 * 4)

            def rotated(j, t, scratch):
                dve.wait_ge(rot_mm, j + 1)
                dve.tensor_tensor(scratch[:, j % 2, :], sbank((j if j < 10 else j - 10) % 4)[:, 0:T], sinw[:],
                                  ALU.mult).then_inc(rot_free, 1)
                link(dve.tensor_tensor(t, t, cosw[:], ALU.mult))
                dve.wait_ge(rot_free, j + 1)
                dve.tensor_tensor(t, t, scratch[:, j % 2, :], ALU.add).then_inc(rot_done, 1)

            ROT = [QB[:, j, :] for j in range(4)] + [KR[:], KI[:]] + [QI[:, j, :] for j in range(4)]
            for n in range(6, 9):
                for j in range(4 * (n - 6), min(4 * (n - 6) + 4, 10)):
                    rotated(j, ROT[j], ROT_T)
                lo(n + 2)

            def sb_softplus(h):
                dve.wait_ge(sb_l, h + 1)
                link(dve.scalar_tensor_tensor(out=SB_SP[h % 2][:], in0=sbank(h % 2)[:, 0:SBW], scalar=0.0,
                                              in1=SB_L[h % 2][:], op0=ALU.max, op1=ALU.add))
                dve.tensor_tensor(SB_SPM[h % 2][:], SB_SP[h % 2][:], SBM[:], ALU.mult).then_inc(sb_spm, 1)

            def index_scores(i):
                t = i // 2
                m = QRY_TILES[t][1]
                sc = SCORE[0:m, t, :]
                for j in range(4 * i, 4 * i + 4):
                    h = j % HEADS
                    dve.wait_ge(ix_relu, j + 1)
                    if h:
                        dve.wait_ge(ix_used, j)
                        dve.scalar_tensor_tensor(out=sc, in0=RL[j % 4][0:m, :], scalar=WI[0:m, t, h:h + 1], in1=sc,
                                                 op0=ALU.mult, op1=ALU.add).then_inc(ix_used, 1)
                    else:
                        dve.tensor_scalar(sc, RL[j % 4][0:m, :], WI[0:m, t, h:h + 1], None, ALU.mult)\
                            .then_inc(ix_used, 1)
                if i % 2:
                    dve.wait_ge(ix_used, HEADS * (t + 1))
                    link(dve.tensor_tensor(sc, sc, BND[0:m, t, :], ALU.min))

            def take_best(t):
                m = QRY_TILES[t][1]
                sc = SCORE[0:m, t, :]
                link(dve.max(MAX8[0:m, :], sc))
                link(dve.match_replace(sc, MAX8[0:m, :], sc, -3.4e38))

            def key_mask(t):
                m = QRY_TILES[t][1]
                sc = SCORE[0:m, t, :]
                link(dve.scalar_tensor_tensor(out=sc, in0=sc, scalar=-3.3e38, in1=ADM[0:m, t, :],
                                              op0=ALU.is_le, op1=ALU.mult))
                dve.tensor_scalar(NEG[0:m, t, :], sc, -1.0, BIG, ALU.add, ALU.mult).then_inc(ix_neg, 1)

            rounds = [0]

            def index_part(h):
                if h < 6:
                    index_scores(h)
                for _ in range(ROUNDS[h]):
                    take_best(rounds[0] // (TOPK // 8))
                    rounds[0] += 1
                    if rounds[0] % (TOPK // 8) == 0:
                        key_mask(rounds[0] // (TOPK // 8) - 1)

            def sb_out(h):
                dve.wait_ge(sb_y, h + 1)
                r = slice(HD * (h % 2), HD * (h % 2) + HD)
                dve.wait_ge(sb_yh, h + 1)
                dve.tensor_tensor(YAL[r, h // 2, :], PS[r, h % 2, 0:T], YAH[r, h // 2, :].bitcast(F32),
                                  ALU.subtract).then_inc(sb_yd, 1)

            dve.wait_ge(sb_in, 48)
            sb_softplus(0)
            sb_softplus(1)
            dve.wait_ge(dsa_in, 64)
            for h in range(HEADS):
                if 1 < h + 1 < HEADS:
                    sb_softplus(h + 1)
                dve.wait_ge(sb_e, h + 1)
                dve.scalar_tensor_tensor(out=SB_A[h % 2][:], in0=SB_A[h % 2][:], scalar=3e38, in1=SBM[:],
                                         op0=ALU.min, op1=ALU.mult).then_inc(sb_am, 1)
                if h:
                    sb_out(h - 1)
                if h == HEADS - 1:
                    sb_out(h)
                index_part(h)
            dve.wait_ge(ix_neg, 3)

            attn = [0]

            def attention(neg, pr, scale, tail):
                base = attn[0]
                steps_ = [(h, t) for h in range(HEADS) for t in range(3)]

                def maxima(i):
                    t = steps_[i][1]
                    m = QRY_TILES[t][1]
                    dve.wait_ge(at_l, base + i + 1)
                    if i >= 2:
                        dve.wait_ge(at_t, base + i - 1)
                    mx = SMALL[0:m, i % 2:i % 2 + 1]
                    dve.tensor_tensor_reduce(pr[i % 2][0:m, :], sbank(i % 2)[0:m, 0:T], neg[0:m, t, :], 1.0,
                                             -3.4e38, ALU.add, ALU.max, mx).then_inc(at_m, 1)
                    dve.wait_ge(at_m, base + i + 1)
                    dve.tensor_scalar(SMALL[0:m, 2 + i % 2:3 + i % 2], mx, -scale, None, ALU.mult)\
                        .then_inc(at_b, 1)

                maxima(0)
                for i, (h, t) in enumerate(steps_):
                    m = QRY_TILES[t][1]
                    dve.wait_ge(at_e, base + i + 1)
                    rc = SMALL[0:m, 6 + i % 2:7 + i % 2]
                    link(dve.reciprocal(rc, SMALL[0:m, 4 + i % 2:5 + i % 2]))
                    dve.tensor_scalar(pr[i % 2][0:m, :], pr[i % 2][0:m, :], rc, None, ALU.mult).then_inc(at_p, 1)
                    if i + 1 < len(steps_):
                        maxima(i + 1)
                    if t == 1 and h:
                        tail(h - 1)
                tail(HEADS - 1)
                attn[0] += len(steps_)

            def split_out(g, rows, dh, dl):
                dve.wait_ge(unit_done, g + 1)
                link(dve.tensor_copy(dh, gbank(g)[rows, 0:T]))
                freeing(dve.tensor_tensor(dl, gbank(g)[rows, 0:T], dh.bitcast(F32), ALU.subtract))

            def dsa_tail(h):
                r = slice(HD * (h % 2), HD * (h % 2) + HD)
                split_out(UNIT0[f"yb{h}"], r, YBH[r, h // 2, :], YBL[r, h // 2, :])

            attention(NEG, PR, HD ** -0.5, dsa_tail)
            lo(11)

            for m in range(8):
                g = UNIT0["za"] + m
                dve.wait_ge(unit_done, g + 1)
                freeing(dve.tensor_tensor(GA[:, m, :], gbank(g)[:, 0:T], GA[:, m, :], ALU.mult))
            lo(12)
            for m in range(8):
                g = UNIT0["zb"] + m
                dve.wait_ge(unit_done, g + 1)
                if m >= 2:
                    dve.wait_ge(z_lo, m - 1)
                freeing(dve.tensor_tensor(ZT[:, m % 2, :], gbank(g)[:, 0:T], GB[:, m, :], ALU.mult))
                dve.wait_ge(freed["dve"], FREED[g][1])
                dve.tensor_tensor(ZT[:, m % 2, :], ZT[:, m % 2, :], GA[:, m, :], ALU.add).then_inc(z_done, 1)
            lo(13)
            for m in range(8):
                add_to_h(UNIT0["wo"] + m, m)

            scale_of(D)
            normed(UM, H, "ffn", KB)
            q = small
            n3 = [P, 3]
            LG = q["LG"]
            link(dve.memset(LG[:], 0.0))
            dve.wait_ge(moe_in, 16 * 6)
            g = UNIT0["router"]
            dve.wait_ge(unit_done, g + 1)
            dve.tensor_tensor(LG[:, 0:2, :], gbank(g)[:, 0:72].rearrange("p (t e) -> p t e", t=2),
                              bc(q["RB"][:].unsqueeze(1), [P, 2, 36]), ALU.add)
            freeing(dve.tensor_tensor(LG[0:16, 2, :], gbank(g)[0:16, 72:108], q["RB"][0:16, :], ALU.add))
            dve.wait_ge(freed["dve"], FREED[g][1])
            lg, le = LG[:, :, 0:NG], LG[:, :, NG:NG + NE]

            def first_max(dst, src, n, desc, top_):
                tmp = q["GTMP"] if n == NG else q["ET"]
                link(dve.tensor_reduce(top_[:], src, AX.X, ALU.max))
                link(dve.tensor_tensor(tmp[:], src, bc(top_[:].unsqueeze(2), [P, 3, n]), ALU.is_ge))
                link(dve.tensor_tensor(tmp[:], tmp[:], bc(desc.unsqueeze(1), [P, 3, n]), ALU.mult))
                link(dve.tensor_reduce(q["TM"][:], tmp[:], AX.X, ALU.max))
                link(dve.tensor_tensor(dst[:], bc(desc.unsqueeze(1), [P, 3, n]),
                                       bc(q["TM"][:].unsqueeze(2), [P, 3, n]), ALU.is_equal))

            first_max(q["OG"], lg, NG, q["DESC"][:, 0:NG], q["GM"])
            dve.tensor_tensor(q["GE"][:], lg, bc(q["GM"][:].unsqueeze(2), [P, 3, NG]), ALU.subtract)\
                .then_inc(rt_exp, 1)
            link(dve.tensor_scalar(q["OG"][:], q["OG"][:], -1.0, BIG, ALU.add, ALU.mult))
            for t in range(3):
                ins = dve.tensor_tensor(q["EM"][:, t, :].rearrange("p (g e) -> p g e", g=NG),
                                        le[:, t, :].rearrange("p (g e) -> p g e", g=NG),
                                        bc(q["OG"][:, t, :].unsqueeze(2), [P, NG, EPG]), ALU.add)
            link(ins)
            first_max(q["O1"], q["EM"][:], NE, q["DESC"][:, NG:NG + NE], q["M1"])
            link(dve.scalar_tensor_tensor(out=q["EM"][:], in0=q["O1"][:], scalar=-2 * BIG, in1=q["EM"][:],
                                          op0=ALU.mult, op1=ALU.add))
            first_max(q["O2"], q["EM"][:], NE, q["DESC"][:, NG:NG + NE], q["M2"])
            dve.tensor_tensor(q["MM"][:], q["O1"][:], q["O2"][:], ALU.add).then_inc(rt_m, 1)
            dve.tensor_tensor(q["M2"][:], q["M2"][:], q["M1"][:], ALU.subtract).then_inc(rt_exp, 1)
            CC, TA, TF, IO = q["CC"], q["TA"], q["TF"], q["IOTA"]
            g = UNIT0["rank"]
            e = slice(0, NE)
            dve.wait_ge(unit_done, g + 1)
            freeing(dve.tensor_copy(CC[e, 0:1], gbank(g)[e, 0:1]))
            dve.wait_ge(freed["dve"], FREED[g][1])
            link(dve.tensor_scalar(q["N5"][e, :], q["THR"][e, :], CC[e, 0:1], None, ALU.is_lt))
            link(dve.tensor_reduce(CC[e, 1:2], q["N5"][e, :], AX.X, ALU.add))
            dve.tensor_scalar(q["CB"][e, :], ones[e, :], CC[e, 0:1], None, ALU.mult).then_inc(rt_m, 1)
            g += 1
            dve.wait_ge(unit_done, g + 1)
            link(dve.tensor_copy(CC[e, 2:4], gbank(g)[e, 96:98]))
            link(dve.tensor_tensor(CC[e, 4:5], CC[e, 3:4], CC[e, 1:2], ALU.subtract))
            link(dve.scalar_tensor_tensor(out=CC[e, 5:6], in0=CC[e, 4:5], scalar=-float(WIN), in1=CC[e, 2:3],
                                          op0=ALU.mult, op1=ALU.add))
            link(dve.tensor_scalar(CC[e, 5:6], CC[e, 5:6], -float(SLOTS), None, ALU.add))
            link(dve.tensor_scalar(TA[e, ITEMS:2 * ITEMS], IO[e, 0:ITEMS], CC[e, 3:4], None, ALU.is_ge))
            link(dve.scalar_tensor_tensor(out=TF[e, 0:ITEMS], in0=IO[e, 0:ITEMS], scalar=CC[e, 4:5],
                                          in1=TA[e, ITEMS:2 * ITEMS], op0=ALU.is_ge, op1=ALU.subtract))
            link(dve.tensor_scalar(TF[e, ITEMS:2 * ITEMS], IO[e, 0:ITEMS], float(WIN), CC[e, 5:6],
                                   ALU.mult, ALU.add))
            link(dve.tensor_tensor(TA[e, 0:ITEMS], TF[e, ITEMS:2 * ITEMS], TF[e, 0:ITEMS], ALU.mult))
            dve.tensor_copy(TA[e, 80:81], CC[e, 1:2]).then_inc(rt_m, 1)
            dst = gbank(g)[:, 0:3 * NE].rearrange("p (t e) -> p t e", t=3)
            for o, d in (("O1", "DST1"), ("O2", "DST2")):
                link(dve.tensor_tensor(q["ET"][:], dst, q[o][:], ALU.mult))
                link(dve.tensor_reduce(q[d][:], q["ET"][:], AX.X, ALU.add))
            freeing(dve.tensor_copy(q["GTMP"][:, 0, 0:1], gbank(g)[:, 0:1]))
            g += 1
            dve.wait_ge(unit_done, g + 1)
            dve.tensor_scalar(TF[0:1, 0:ITEMS], gbank(g)[0:1, 0:ITEMS], float(SLOTS), None, ALU.add)
            dve.tensor_scalar(TF[0:1, ITEMS:2 * ITEMS], gbank(g)[0:1, ITEMS:2 * ITEMS], float(NE - 1), None,
                              ALU.min)
            link(dve.tensor_copy(CC[0:1, 6:7], gbank(g)[0:1, 80:81]))
            pairs = TA[0:1, 0:ITEMS // 2]
            freeing(dve.tensor_scalar(pairs, IO[0:1, 0:ITEMS:2], CC[0:1, 6:7], None, ALU.is_lt))
            dve.wait_ge(freed["dve"], FREED[g][1])
            link(dve.tensor_reduce(TF[0:1, 80:81], pairs, AX.X, ALU.add))
            link(dve.tensor_scalar(TF[0:1, 81:82], TF[0:1, 80:81], 2.0, -2.0, ALU.mult, ALU.add))
            dve.tensor_copy(TBL[0:1, 0:82], TF[0:1, 0:82]).then_inc(tbl_done, 1)
            for t in range(3):
                link(dve.tensor_scalar(PERM[:, t, :], IO[:], q["DST1"][:, t:t + 1], None, ALU.is_equal))
                ins = dve.scalar_tensor_tensor(out=PERM[:, t, :], in0=IO[:], scalar=q["DST2"][:, t:t + 1],
                                               in1=PERM[:, t, :].bitcast(F32), op0=ALU.is_equal, op1=ALU.add)
            ins.then_inc(perm_done, 1)
            dve.wait_ge(rt_gd, 2)
            link(dve.tensor_reduce(q["PG"][:], q["GE"][:], AX.X, ALU.add))
            link(dve.scalar_tensor_tensor(out=q["G1"][:], in0=q["M2"][:], scalar=1.0, in1=q["PG"][:],
                                          op0=ALU.add, op1=ALU.mult))
            link(dve.reciprocal(q["G1"][:], q["G1"][:]))
            link(dve.tensor_tensor(q["G2"][:], q["G1"][:], q["M2"][:], ALU.mult))
            for t in range(3):
                dve.tensor_scalar(G[:, t, :], IO[:, 0:SLOTS], q["DST1"][:, t:t + 1], q["G1"][:, t:t + 1],
                                  ALU.is_equal, ALU.mult)
            dve.wait_ge(unit_done, UNIT0["disp"] + 16)
            for t in range(3):
                link(dve.tensor_scalar(PERMF[:, t, 0:SLOTS], IO[:, 0:SLOTS], q["DST2"][:, t:t + 1],
                                       q["G2"][:, t:t + 1], ALU.is_equal, ALU.mult))
                dve.tensor_tensor(G[:, t, :], G[:, t, :], PERMF[:, t, 0:SLOTS], ALU.add).then_inc(g_done, 1)
            items = dve.value_load(TBL[0:1, 80:81], min_val=1, max_val=ITEMS // 2) * 2
            dve.nop().then_inc(xhid_done, 2)
            with dve.Fori(0, items, 2) as i:
                for s in range(2):
                    dve.wait_ge(xs_done, i + (s + 1))
                    dve.wait_ge(xy_done, i + (s + 1))
                    dve.tensor_tensor(SG[s][:], PS[:, s, 0:4 * WIN].rearrange("p (m w) -> p m w", m=4),
                                      SG[s][:], ALU.mult).then_inc(xt_done, 1)
                    dve.wait_ge(xt_done, i + (s + 1))
                    dve.tensor_tensor(HID[s][:], PS[:, 2 + s, 0:4 * WIN].rearrange("p (m w) -> p m w", m=4),
                                      SG[s][:], ALU.mult).then_inc(xhid_done, 1)
            for st in range(5):
                m = min(P, SLOTS - P * st)
                g = UNIT0["gt"] + st
                dve.wait_ge(unit_done, g + 1)
                freeing(dve.tensor_copy(GT[0:m, st, :], gbank(g)[0:m, 0:T]))
            lo(N_FIRST)
            for m in range(8):
                add_to_h(UNIT0["comb"] + m, m)
            scale_of(D)
            normed(H, H, "final", KB, META)
            scale_of(D)
            dve.wait_ge(meta2_in, 16)
            normed(SQ3, H, "mix0", KB)
            lo(N_FIRST + 1)
            n = FIRST_SLAB["ret_qk"]
            for h in range(RH):
                for p in range(2):
                    g = UNIT0["rqk"] + 4 * h + 2 * p
                    b = g % 4
                    dve.wait_ge(unit_done, g + 2)
                    pair = PS[:, b:b + 2, 0:T]
                    dst_ = (RQ, RK)[p]
                    link(dve.tensor_tensor(R1[:], pair, bc(cosw[:].unsqueeze(1), [P, 2, T]), ALU.mult))
                    freeing(dve.tensor_tensor(R2[:], pair, bc(sinw[:].unsqueeze(1), [P, 2, T]), ALU.mult), 2)
                    dve.wait_ge(freed["dve"], FREED[g + 1][1])
                    dve.tensor_tensor(dst_[:, 2 * h, :], R1[:, 0, :], R2[:, 1, :], ALU.subtract)
                    dve.tensor_tensor(dst_[:, 2 * h + 1, :], R2[:, 0, :], R1[:, 1, :], ALU.add)\
                        .then_inc(rqk_done, 1)
                    dve.wait_ge(rqk_done, 2 * h + p + 1)
                lo(n + h + 2)
            for h in range(RH):
                lo(n + RH + h + 2)
            for s in range(4):
                for u in range(4):
                    j = 4 * s + u
                    g = UNIT0["gate"] + j
                    dve.wait_ge(gsig_done, j + 1)
                    freeing(dve.tensor_tensor(GATE[:, j, :], gbank(g)[:, 0:T], GSIG[j % 2][:], ALU.mult))
                if s < 3:
                    lo(n + 2 * RH + s + 2)

            def weigh(h):
                dve.wait_ge(dec_in[h % 2], 16 * (h // 2 + 1))
                if h >= 2:
                    dve.wait_ge(unit_done, UNIT0["ro"] + 4 * (h - 1))
                for j, (k0, mk) in enumerate(KEY_COLS):
                    i = 3 * h + j
                    dve.wait_ge(st_mm, i + 1)
                    dve.tensor_tensor(ST[h % 2][0:mk, j, :], sbank(i % 3)[0:mk, 0:T], DEC[h % 2][0:mk, j, :],
                                      ALU.mult).then_inc(st_done, 1)

            dve.wait_ge(unit_done, UNIT0["gate"] + 16)
            weigh(0)
            lo(n + 2 * RH + 5)
            weigh(1)
            for h in range(RH):
                ro = RO[h % 2]
                dve.wait_ge(ro_sum, h + 1)
                dve.tensor_scalar(GMU[:], sbank(3)[:, 0:T], 1.0 / RV, None, ALU.mult).then_inc(gmu_done, 1)
                dve.wait_ge(gmu_done, h + 1)
                dve.tensor_tensor(ro[:], ro[:], bc(GMU[:].unsqueeze(1), [P, 4, T]), ALU.subtract)\
                    .then_inc(oc_done, 1)
                dve.wait_ge(gv_mm, h + 1)
                dve.tensor_scalar(GRS[:], sbank(3)[:, 0:T], 1.0 / RV, GN_EPS, ALU.mult, ALU.add).then_inc(gvar, 1)
                dve.wait_ge(gstd, h + 1)
                dve.wait_ge(oc_done, h + 1)
                link(dve.reciprocal(GRS[:], GRS[:]))
                if h + 2 < RH:
                    weigh(h + 2)
                link(dve.tensor_tensor(ro[:], ro[:], bc(GRS[:].unsqueeze(1), [P, 4, T]), ALU.mult))
                for v in range(4):
                    c = GAINS["gn"] + 4 * h + v
                    ins = dve.scalar_tensor_tensor(out=RSQ[h % 2][:, v, :], in0=ro[:, v, :],
                                                   scalar=gains[:, c:c + 1], in1=GATE[:, 4 * h + v, :],
                                                   op0=ALU.mult, op1=ALU.mult)
                ins.then_inc(rn_done, 1)
            n = FIRST_SLAB["ret_o"]
            for s in range(4):
                for u in range(2):
                    add_to_h(UNIT0["rwo"] + 2 * s + u, 2 * s + u)
                if s < 3:
                    lo(n + s + 2)

            def ffn(layer, gain):
                scale_of(D)
                normed(SQ2, H, gain, KB)
                n = FIRST_SLAB[f"up{layer}"]
                lo(n + 1)
                f0 = FB * layer
                for p in range(FB):
                    g = UNIT0[f"up{layer}"] + 2 * p
                    dve.wait_ge(f_sig, f0 + p + 1)
                    freeing(dve.tensor_tensor(FT[p % 2][:], gbank(g)[:, 0:T], FS[p % 2][:], ALU.mult))
                    dve.wait_ge(freed["dve"], FREED[g][1])
                    dve.wait_ge(unit_done, g + 2)
                    if p >= 2:
                        dve.wait_ge(f_lo, f0 + p - 1)
                    freeing(dve.tensor_tensor(FU[p % 2][:], gbank(g + 1)[:, 0:T], FT[p % 2][:], ALU.mult))
                    if p % 2 and n + p // 2 + 2 < len(SLABS):
                        lo(n + p // 2 + 2)
                n = FIRST_SLAB[f"down{layer}"]
                for s in range(8):
                    add_to_h(UNIT0[f"down{layer}"] + s, s)
                    if s < 7 and n + s + 2 < len(SLABS):
                        lo(n + s + 2)

            ffn(0, "ffn0")
            scale_of(D)
            normed(SQM, H, "kv", KB)
            n = FIRST_SLAB["kv_c"]
            lo(n + 1)
            normed(SQQ, H, "mix1", KB)
            lo(n + 2)
            scale_of(4 * P, lambda: lo(n + 3))
            normed(SQQ, CKRAW, "kva", 4)
            lo(n + 4)
            scale_of(6 * P)
            normed(SQQ, CRAW, "qa", 6)
            lo(n + 5)
            lo(n + 6)
            dve.wait_ge(mla_in, 32)
            rotated(10, KR2[:], ROT_M)
            lo(n + 7)
            lo(n + 8)
            for j in range(4):
                rotated(11 + j, QR[:, j, :], ROT_M)
            lo(n + 9)
            dve.wait_ge(mla_in, 48)
            attention(NEG2, PR2, (P + HD) ** -0.5,
                      lambda h: split_out(UNIT0[f"om{h}"], slice(0, P), OMH[:, h, :], OML[:, h, :]))
            n = FIRST_SLAB["mla_o"]
            for s in range(2):
                for u in range(4):
                    add_to_h(UNIT0["mo"] + 4 * s + u, 4 * s + u)
                if s == 0:
                    lo(n + 2)
            ffn(1, "ffn1")
            scale_of(D)
            normed(OUT, H, "final2", KB)

        @block.gpsimd
        def _(pool):
            low_count = [0]

            def lows(dst, hi_, src, nb):
                for k in range(nb):
                    low_count[0] += 1
                    pool.wait_ge(nhi_done, low_count[0])
                    pool.tensor_tensor(dst[:, k, :], src[:, k, :], hi_[:, k, :].bitcast(F32), ALU.subtract)\
                        .then_inc(nlo_done, 1)

            pool.memset(KA[:, :, T:], 0.0).then_inc(ka_zero, 1)
            lows(UL, UH, SQ, KB)
            for m in range(8):
                pool.wait_ge(z_hi, m + 1)
                pool.tensor_tensor(ZL[:, m, :], ZT[:, m % 2, :], ZH[:, m, :].bitcast(F32), ALU.subtract)\
                    .then_inc(z_lo, 1)
            pool.wait_ge(freed["dve"], FREED[UNIT0["wo"] + 7][1])
            pool.memset(UTH[:, 2, :].bitcast(F32), 0.0).then_inc(ut_zero, 1)
            pool.wait_ge(ut_zero, 1)
            pool.wait_ge(ssq_done, 2)
            pool.memset(UTL[:, 2, :].bitcast(F32), 0.0).then_inc(ut_zero, 1)
            pool.wait_ge(ut_zero, 2)
            for t, (q0, m) in enumerate(QRY_TILES):
                for half in range(2):
                    c = slice(512 * half, 512 * half + 512)
                    pool.wait_ge(ut_hi, 2 * t + half + 1)
                    if t or half:
                        pool.wait_ge(ut_lo, 2 * t + half)
                    pool.tensor_tensor(UTL[0:m, t, c], UTOK[0:m, t, c], UTH[0:m, t, c].bitcast(F32),
                                       ALU.subtract).then_inc(ut_lo, 1)
            pool.wait_ge(freed["act"], FREED[UNIT0["disp"] + 15][1])
            pool.wait_ge(tbl_done, 1)
            items = pool.value_load(TBL[0:1, 80:81], min_val=1, max_val=ITEMS // 2) * 2
            with pool.Fori(0, items, 2) as i:
                for s in range(2):
                    at_ = pool.value_load(TBL[0:1, bass.ds(i + s, 1)], min_val=0, max_val=SLOTS)
                    pool.wait_ge(xh_done, i + (s + 1))
                    pool.tensor_copy(XW[s][:], XS[:, :, bass.ds(at_, WIN)]).then_inc(xw_done, 1)
            lows(UL, UH, SQ3, KB)
            for h in range(RH):
                pool.wait_ge(rhi_done, h + 1)
                pool.tensor_tensor(RLO[h][:], RSQ[h % 2][:], RHI[:, 4 * h:4 * h + 4, :].bitcast(F32), ALU.subtract)\
                    .then_inc(rlo_done, 1)

            def ffn(layer):
                lows(UL, UH, SQ2, KB)
                for p in range(FB):
                    pool.wait_ge(f_hi, FB * layer + p + 1)
                    pool.tensor_tensor(TL[:, p, :], FU[p % 2][:], TH[:, p, :].bitcast(F32), ALU.subtract)\
                        .then_inc(f_lo, 1)

            ffn(0)
            lows(UL, UH, SQM, KB)
            lows(U2L, U2H, SQQ, KB)
            lows(CKL, CKH, SQQ, 4)
            lows(CQL, CQH, SQQ, 6)
            ffn(1)


def constants():
    f4 = np.float32
    pos = np.arange(T)
    chunk = np.where(pos < META, 0, 1 + (pos - META) // CHUNK)
    c = {}
    c["c_ident"] = np.eye(P, dtype=f4)
    c["c_ones"] = np.ones((P, P), f4)
    i, j = np.indices((P, P))
    c["c_negu"] = np.where(i >= j, -1.0, 0.0).astype(f4)
    c["c_negones"] = -np.ones((P, P), f4)
    c["m_utri"] = (i < j).astype(f4)

    def swap(period, half):
        r = np.zeros((P, P), f4)
        for m in range(P):
            w = m % period
            if w < half:
                r[m + half, m] = -1.0
            elif w < 2 * half:
                r[m - half, m] = 1.0
        return r

    def angles(inv, rows):
        ang = pos.astype(f4)[None, :] * inv.astype(f4)[np.maximum(rows, 0)][:, None]
        cos = np.where(rows[:, None] >= 0, np.cos(ang.astype(np.float64)), 1.0).astype(f4)
        sin = np.where(rows[:, None] >= 0, np.sin(ang.astype(np.float64)), 0.0).astype(f4)
        return cos, sin

    r = np.arange(P)
    c["rot_dsa"], c["rot_mla"] = swap(HD, 8), swap(HD, 32)
    inv = f4(500000.0) ** (-np.arange(8, dtype=f4) / f4(8))
    c["cos_dsa"], c["sin_dsa"] = angles(inv, np.where(r % HD < 16, r % 8, -1))
    inv = f4(1.0) / (f4(10000.0) ** (np.arange(0, 256, 2, dtype=f4) / f4(256)))
    c["cos_ret"], c["sin_ret"] = angles(inv, r)
    inv = f4(1.0) / (f4(10000.0) ** (np.arange(0, 64, 2, dtype=f4) / f4(64)))
    c["cos_mla"], c["sin_mla"] = angles(inv, r % 32)
    m = np.zeros((P, SBW), f4)
    for (col, q, w), (k0, mk) in zip(SB_COLS, KEY_TILES):
        m[0:mk, col:col + w] = (k0 + np.arange(mk))[:, None] < (q + np.arange(w))[None, :]
    c["sb_mask"] = m
    adm = np.zeros((P, 3, T), f4)
    for t, (q0, mq) in enumerate(QRY_TILES):
        adm[0:mq, t, :] = chunk[None, :] <= chunk[q0:q0 + mq, None]
    c["adm"] = adm
    c["bound"] = np.where(adm > 0, 3e38, -3e38).astype(f4)
    c["neg"] = np.where(adm > 0, 0.0, -BIG).astype(f4)
    dec = np.zeros((RH, P, 3, T), f4)
    for h in range(RH):
        lg = np.log1p(-(2.0 ** (-5.0 - h)))
        for t, (k0, mk) in enumerate(KEY_TILES):
            k = (k0 + np.arange(mk))[:, None]
            dec[h, 0:mk, t, :] = np.where(chunk[k] <= chunk[None, :], np.exp(lg * np.abs(k - pos[None, :])), 0) / 16.0
    c["decay"] = dec
    c["m_IOTA"] = np.broadcast_to(np.arange(XCOLS, dtype=f4), (P, XCOLS)).copy()
    c["m_THR"] = np.broadcast_to(WIN * np.arange(5, dtype=f4), (P, 5)).copy()
    c["m_DESC"] = np.broadcast_to(np.concatenate([np.arange(NG, 0, -1), np.arange(NE, 0, -1)]).astype(f4),
                                  (P, NG + NE)).copy()
    return c


def units(w):
    k, m = w.shape
    return w.reshape(k // P, P, m // P, P).transpose(1, 2, 0, 3)


def cut(w, n):
    p, u = w.shape[:2]
    return w.reshape(p, n, u // n, -1).transpose(1, 0, 2, 3).reshape(n, p, -1)


def layout(x):
    np_ = {k: np.asarray(v) for k, v in x.items()}
    d = {}
    fm = lambda t: np.ascontiguousarray(t.T.reshape(KB, P, -1).transpose(1, 0, 2))
    d["h_first"] = fm(np.concatenate([np_["meta_tokens"], np_["x"][0]], axis=0))
    d["meta2"] = fm(np_["meta_2"])
    col = lambda g: g.reshape(-1, P).T
    d["gains"] = np.concatenate([col(g) for g in (
        np_["norm_mix_g"][0], np_["norm_ffn_g"][0], np_["norm_final_g"], np_["norm_mix_g_2"][0],
        np_["norm_ffn_g_2"][0], np_["mla_norm_kv_g_2"], np_["norm_mix_g_2"][1], np_["mla_kv_a_norm_g_2"],
        np_["mla_q_a_norm_g_2"][0], np_["norm_ffn_g_2"][1], np_["final_g_2"], np_["ret_gn_g_2"][0])], axis=1)
    w = np_["w_in"][0]
    parts = np.split(w, np.cumsum([512, 512, 512, 512, LAT, 16, 512, HD, HEADS, D, D])[:-1], axis=1)
    qa, ka, va, qb, ckv, kr, qi, ki, wi, ga, gb = parts
    zeros = lambda n: np.zeros((D, n), w.dtype)
    slab_kmajor = lambda v: v.reshape(-1, P, v.shape[1]).transpose(1, 0, 2).reshape(1, P, -1)
    d["w_in_qa"], d["w_in_ka"] = cut(units(qa), 1), cut(units(ka), 1)
    d["w_in_va"] = slab_kmajor(va)
    d["w_in_qb"], d["w_in_qi"] = cut(units(qb), 1), cut(units(qi), 1)
    misc = np.concatenate([ckv, kr, zeros(48), kr, zeros(48), ki, ki, wi, zeros(P - HEADS)], axis=1)
    d["w_in_misc"] = cut(units(misc), 1)
    d["w_in_ga"], d["w_in_gb"] = cut(units(ga), 2), cut(units(gb), 2)
    d["w_up_a"], d["w_up_b"] = cut(units(np_["w_up_a"][0]), 1), cut(units(np_["w_up_b"][0]), 1)
    d["w_o"] = cut(units(np_["w_o"][0]), 2)
    uk = np_["w_uk"][0].transpose(0, 2, 1)
    uk = np.concatenate([np.zeros((HEADS, 16, LAT), uk.dtype), uk], axis=1)
    d["w_uk"] = uk.reshape(4, P, LAT).transpose(1, 0, 2)
    d["w_uv"] = np_["w_uv"][0].transpose(1, 0, 2)
    d["m_RB"] = np.broadcast_to(np.concatenate([np_["b_group"][0], np_["b_router"][0]]), (P, NG + NE))
    d["m_WRT"] = np.concatenate([np_["w_group"][0], np_["w_router"][0]], axis=1)\
        .reshape(KB, P, NG + NE).transpose(1, 0, 2)
    expert = lambda v: v.reshape(NE, v.shape[1] // P, P, v.shape[2] // P, P).transpose(0, 2, 3, 1, 4)\
        .reshape(NE, P, -1)
    d["w1"], d["w3"], d["w2"] = (expert(np_[k][0]) for k in ("w1", "w3", "w2"))
    w = np_["ret_w_in_2"][0]
    q, k = w[:, 0:D].reshape(D, RH, 256), w[:, D:2 * D].reshape(D, RH, 256)
    d["ret_qk"] = cut(units(np.concatenate([q, k], axis=2).reshape(D, 2 * D)), 4)
    d["ret_v"] = np.concatenate([slab_kmajor(w[:, 2 * D + RV * h:2 * D + RV * (h + 1)]) for h in range(RH)])
    d["ret_gate"] = cut(units(w[:, 4 * D:6 * D]), 4)
    d["ret_o"] = cut(units(np_["ret_w_o_2"][0]), 4)
    for layer in range(2):
        w1, w3 = units(np_["ffn_w1_2"][layer]), units(np_["ffn_w3_2"][layer])
        d[f"up{layer}"] = cut(np.stack([w1, w3], axis=2).reshape(P, 2 * FB, KB, P), 11)
        d[f"down{layer}"] = cut(units(np_["ffn_w2_2"][layer]), 8)
    w = np_["mla_w_kv_a_2"]
    d["kv_c"] = cut(units(w[:, 0:512]), 1)
    qa = np_["mla_w_q_a_2"][0]
    d["kr_qa"] = cut(units(np.concatenate([w[:, 512:], w[:, 512:], qa[:, 0:3 * P]], axis=1)), 1)
    d["qa_rest"] = cut(units(qa[:, 3 * P:]), 1)
    w = np_["mla_w_kv_b_2"].reshape(512, HEADS, 2 * P)
    d["kv_k"] = cut(units(w[:, :, 0:P].reshape(512, D)), 1)
    d["kv_v"] = slab_kmajor(w[:, :, P:].reshape(512, D))
    w = np_["mla_w_q_b_2"][0].reshape(768, HEADS, P + HD)
    d["q_b"] = cut(units(np.concatenate([w[:, :, 0:P].reshape(768, D), w[:, :, P:].reshape(768, 512)], axis=1)), 3)
    d["mla_o"] = cut(units(np_["mla_w_o_2"][0]), 2)
    d.update(constants())
    return {k: np.ascontiguousarray(v) for k, v in d.items()}


def kernel(**inputs):
    import concourse.bacc as bacc
    from concourse.bass_utils import run_bass_kernel_spmd

    arrays = layout(inputs)
    nc = bacc.Bacc("TRN2", target_bir_lowering=False, num_devices=1)
    a = {k: nc.dram_tensor("in_" + k, v.shape, mybir.dt.from_np(v.dtype), kind="ExternalInput").ap()
         for k, v in arrays.items()}
    out = nc.dram_tensor("out_0", (P, KB, SEQ), F32, kind="ExternalOutput").ap()
    program(nc, a, out)
    r = run_bass_kernel_spmd(nc, [{"in_" + k: v for k, v in arrays.items()}], core_ids=[0])
    y = r.results[0]["out_0"]
    return y.transpose(2, 1, 0).reshape(1, SEQ, D)
```
